# Optimizing a Trainium2 kernel written in Bass

```python
import math
import jax, jax.numpy as jnp
from jax import lax
import numpy as np

D_MODEL = 1024
BATCH = 1
SEQ = 256
DEPTH = 1

D_PLE = 256
D_MIX = D_MODEL
S5_WIDTH = D_MIX // 2
S5_GROUP = 16
S5_GROUPS = S5_WIDTH // S5_GROUP
S5_STATE = 64
RWKV_WIDTH = D_MIX - S5_WIDTH
RWKV_HEAD = 64
RWKV_HEADS = RWKV_WIDTH // RWKV_HEAD
D_IN = S5_WIDTH + 3 * RWKV_WIDTH
DECAY_LORA = 64
ICLR_LORA = 64
GATE_LORA = 128
RWKV_GN_EPS = 64e-5
N_EXPERTS = 32
TOP_K = 4
D_FF = D_MODEL
SWIGLU_LIMIT = 7.0
SWIGLU_ALPHA = 1.702
MOE_BLOCK = 256
RMS_EPS = 1e-6
LAMBDA_RE_MAX = -1e-4

kernel_name = 'hybrid_s5_rwkv7_moe_ple_layer'

def rms_norm(x, g):
    xf = x.astype(jnp.float32)
    y = xf * lax.rsqrt(jnp.mean(xf * xf, axis=-1, keepdims=True) + RMS_EPS)
    return (y * g.astype(jnp.float32)).astype(x.dtype)

def token_shift(t):
    return jnp.pad(t, ((0, 0), (1, 0), (0, 0)))[:, :-1]

def s5_mixer(u, lam_re, lam_im, log_dt, b_re, b_im, c_re, c_im, d_skip, w_glu):
    f32 = jnp.float32
    bsz, seq, _ = u.shape
    uf = u.astype(f32)
    ug = uf.reshape(bsz, seq, S5_GROUPS, S5_GROUP)
    lre = jnp.minimum(lam_re.astype(f32), LAMBDA_RE_MAX)
    lim = lam_im.astype(f32)
    dt = jnp.exp(log_dt.astype(f32))[:, None]
    mag = jnp.exp(lre * dt)
    lb_re = mag * jnp.cos(lim * dt)
    lb_im = mag * jnp.sin(lim * dt)
    den = lre * lre + lim * lim
    z_re = lb_re - 1.0
    coef_re = ((z_re * lre + lb_im * lim) / den)[..., None]
    coef_im = ((lb_im * lre - z_re * lim) / den)[..., None]
    b_re = b_re.astype(f32)
    b_im = b_im.astype(f32)
    bb_re = coef_re * b_re - coef_im * b_im
    bb_im = coef_re * b_im + coef_im * b_re
    bu_re = jnp.einsum('bsgc,gpc->bsgp', ug, bb_re)
    bu_im = jnp.einsum('bsgc,gpc->bsgp', ug, bb_im)
    a_re = jnp.broadcast_to(lb_re, bu_re.shape)
    a_im = jnp.broadcast_to(lb_im, bu_im.shape)

    def combine(e1, e2):
        a1r, a1i, b1r, b1i = e1
        a2r, a2i, b2r, b2i = e2
        return (a2r * a1r - a2i * a1i,
                a2r * a1i + a2i * a1r,
                a2r * b1r - a2i * b1i + b2r,
                a2r * b1i + a2i * b1r + b2i)

    _, _, xs_re, xs_im = lax.associative_scan(combine, (a_re, a_im, bu_re, bu_im), axis=1)
    y = (jnp.einsum('bsgp,gcp->bsgc', xs_re, c_re.astype(f32))
         - jnp.einsum('bsgp,gcp->bsgc', xs_im, c_im.astype(f32)))
    y = y.reshape(bsz, seq, S5_WIDTH) + d_skip.astype(f32) * uf
    y = jax.nn.gelu(y)
    y = y * jax.nn.sigmoid(y @ w_glu.astype(f32))
    return y.astype(u.dtype)

def rwkv7_step(state, inp):
    r_t, w_t, k_t, v_t, neg_kk_t, kka_t = inp
    sa = jnp.einsum('bhvk,bhk->bhv', state, neg_kk_t)
    state = (state * w_t[:, :, None, :]
             + sa[..., None] * kka_t[:, :, None, :]
             + v_t[..., None] * k_t[:, :, None, :])
    return state, jnp.einsum('bhvk,bhk->bhv', state, r_t)

def rwkv7_mixer(h, r, k, v, mu_rkv, mu_wag, w0, w1, w2, a0, a1, a2, g1, g2,
                k_k, k_a, r_k, ln_w, ln_b):
    f32 = jnp.float32
    bsz, seq, _ = h.shape
    hf = h.astype(f32)
    dh = token_shift(hf) - hf
    xw = hf + dh * mu_wag[0]
    xa = hf + dh * mu_wag[1]
    xg = hf + dh * mu_wag[2]
    r = r.astype(f32)
    k = k.astype(f32)
    v = v.astype(f32)
    r = r + (token_shift(r) - r) * mu_rkv[0]
    k = k + (token_shift(k) - k) * mu_rkv[1]
    v = v + (token_shift(v) - v) * mu_rkv[2]
    w_log = -jax.nn.softplus(-(w0 + jnp.tanh(xw @ w1) @ w2)) - 0.5
    decay = jnp.exp(-jnp.exp(w_log))
    a = jax.nn.sigmoid(a0 + (xa @ a1) @ a2)
    g = jax.nn.sigmoid(xg @ g1) @ g2

    def heads(t):
        return t.reshape(bsz, seq, RWKV_HEADS, RWKV_HEAD)

    kk = heads(k * k_k)
    kk = kk / jnp.maximum(jnp.sqrt(jnp.sum(kk * kk, axis=-1, keepdims=True)), 1e-12)
    k = k * (1.0 + (a - 1.0) * k_a)
    rh, kh, vh, wh, ah = heads(r), heads(k), heads(v), heads(decay), heads(a)

    def seq_first(t):
        return jnp.moveaxis(t, 1, 0)

    state0 = jnp.zeros((bsz, RWKV_HEADS, RWKV_HEAD, RWKV_HEAD), f32)
    _, ys = lax.scan(rwkv7_step, state0,
                     (seq_first(rh), seq_first(wh), seq_first(kh), seq_first(vh),
                      seq_first(-kk), seq_first(kk * ah)))
    y = jnp.moveaxis(ys, 0, 1)
    mean = jnp.mean(y, axis=-1, keepdims=True)
    var = jnp.mean(jnp.square(y - mean), axis=-1, keepdims=True)
    yn = ((y - mean) * lax.rsqrt(var + RWKV_GN_EPS)).reshape(bsz, seq, RWKV_WIDTH)
    yn = yn * ln_w + ln_b
    bonus = jnp.sum(rh * kh * r_k, axis=-1, keepdims=True) * vh
    out = (yn + bonus.reshape(bsz, seq, RWKV_WIDTH)) * g
    return out.astype(h.dtype)

def moe_ffn(h, router_w, router_b, w_gate, b_gate, w_up, b_up, w_down, b_down):
    f32 = jnp.float32
    bsz, seq, dm = h.shape
    n_tok = bsz * seq
    hf = h.reshape(n_tok, dm)
    logits = (hf @ router_w).astype(f32) + router_b.astype(f32)
    top_v, top_i = lax.top_k(logits, TOP_K)
    gates = jax.nn.softmax(top_v, axis=-1)
    m = n_tok * TOP_K
    e_flat = top_i.reshape(m)
    tok_flat = jnp.repeat(jnp.arange(n_tok, dtype=jnp.int32), TOP_K)
    g_flat = gates.reshape(m)
    order = jnp.argsort(e_flat)
    e_s = e_flat[order]
    tok_s = tok_flat[order]
    g_s = g_flat[order]
    counts = jnp.bincount(e_flat, length=N_EXPERTS)
    starts = jnp.cumsum(counts) - counts
    padded = ((counts + MOE_BLOCK - 1) // MOE_BLOCK) * MOE_BLOCK
    pends = jnp.cumsum(padded)
    pstarts = pends - padded
    dest = pstarts[e_s] + (jnp.arange(m) - starts[e_s])
    n_blocks = (m + MOE_BLOCK - 1) // MOE_BLOCK + N_EXPERTS
    m_pad = n_blocks * MOE_BLOCK
    tok_pad = jnp.zeros((m_pad,), jnp.int32).at[dest].set(tok_s)
    g_pad = jnp.zeros((m_pad,), f32).at[dest].set(g_s)
    block_e = jnp.minimum(
        jnp.searchsorted(pends, jnp.arange(n_blocks) * MOE_BLOCK, side='right'),
        N_EXPERTS - 1)

    def run_block(args):
        e, toks, gw = args
        xb = hf[toks]
        gt = jnp.minimum(xb @ w_gate[e] + b_gate[e], SWIGLU_LIMIT)
        up = jnp.clip(xb @ w_up[e] + b_up[e], -SWIGLU_LIMIT, SWIGLU_LIMIT)
        act = (up + 1.0) * gt * jax.nn.sigmoid(SWIGLU_ALPHA * gt)
        yb = act @ w_down[e] + b_down[e]
        return yb.astype(f32) * gw[:, None]

    ys = lax.map(run_block, (block_e, tok_pad.reshape(n_blocks, MOE_BLOCK),
                             g_pad.reshape(n_blocks, MOE_BLOCK)))
    out = jnp.zeros((n_tok, dm), f32).at[tok_pad].add(ys.reshape(m_pad, dm))
    return out.reshape(bsz, seq, dm).astype(h.dtype)

def setup_inputs(seed: int = 0) -> dict:
    key = jax.random.key(seed)
    ks = iter(jax.random.split(key, 64))
    f32 = jnp.float32
    L, D = DEPTH, D_MODEL

    def nrm(shape, scale):
        return jax.random.normal(next(ks), shape, f32) * scale

    def unif(shape, lo, hi):
        return jax.random.uniform(next(ks), shape, f32, lo, hi)

    lam_im = jnp.broadcast_to(jnp.pi * jnp.arange(S5_STATE, dtype=f32), (L, S5_GROUPS, S5_STATE))
    return {
        'x': nrm((BATCH, SEQ, D), 1.0),
        'p': nrm((DEPTH, BATCH, SEQ, D_PLE), 1.0),
        'norm_mix_g': 1.0 + nrm((L, D), 0.02),
        'w_in': nrm((L, D, D_IN), D ** -0.5),
        's5_lam_re': -0.5 + nrm((L, S5_GROUPS, S5_STATE), 0.01),
        's5_lam_im': lam_im,
        's5_log_dt': unif((L, S5_GROUPS), math.log(1e-3), math.log(1e-1)),
        's5_b_re': nrm((L, S5_GROUPS, S5_STATE, S5_GROUP), (2 * S5_GROUP) ** -0.5),
        's5_b_im': nrm((L, S5_GROUPS, S5_STATE, S5_GROUP), (2 * S5_GROUP) ** -0.5),
        's5_c_re': nrm((L, S5_GROUPS, S5_GROUP, S5_STATE), (2 * S5_STATE) ** -0.5),
        's5_c_im': nrm((L, S5_GROUPS, S5_GROUP, S5_STATE), (2 * S5_STATE) ** -0.5),
        's5_d': nrm((L, S5_WIDTH), 1.0),
        's5_w_glu': nrm((L, S5_WIDTH, S5_WIDTH), S5_WIDTH ** -0.5),
        'rwkv_mu_rkv': unif((L, 3, RWKV_WIDTH), 0.2, 0.8),
        'rwkv_mu_wag': unif((L, 3, D), 0.2, 0.8),
        'rwkv_w0': unif((L, RWKV_WIDTH), -6.0, -1.0),
        'rwkv_w1': nrm((L, D, DECAY_LORA), D ** -0.5),
        'rwkv_w2': nrm((L, DECAY_LORA, RWKV_WIDTH), 0.5 * DECAY_LORA ** -0.5),
        'rwkv_a0': nrm((L, RWKV_WIDTH), 0.1),
        'rwkv_a1': nrm((L, D, ICLR_LORA), D ** -0.5),
        'rwkv_a2': nrm((L, ICLR_LORA, RWKV_WIDTH), 0.5 * ICLR_LORA ** -0.5),
        'rwkv_g1': nrm((L, D, GATE_LORA), D ** -0.5),
        'rwkv_g2': nrm((L, GATE_LORA, RWKV_WIDTH), GATE_LORA ** -0.5),
        'rwkv_k_k': 0.85 + nrm((L, RWKV_WIDTH), 0.02),
        'rwkv_k_a': 1.0 + nrm((L, RWKV_WIDTH), 0.02),
        'rwkv_r_k': nrm((L, RWKV_HEADS, RWKV_HEAD), 0.1),
        'rwkv_ln_w': 1.0 + nrm((L, RWKV_WIDTH), 0.02),
        'rwkv_ln_b': nrm((L, RWKV_WIDTH), 0.02),
        'w_out': nrm((L, D_MIX, D), D_MIX ** -0.5),
        'norm_moe_g': 1.0 + nrm((L, D), 0.02),
        'router_w': nrm((L, D, N_EXPERTS), D ** -0.5),
        'router_b': nrm((L, N_EXPERTS), 0.01),
        'exp_w_gate': nrm((L, N_EXPERTS, D, D_FF), D ** -0.5),
        'exp_b_gate': nrm((L, N_EXPERTS, D_FF), 0.01),
        'exp_w_up': nrm((L, N_EXPERTS, D, D_FF), D ** -0.5),
        'exp_b_up': nrm((L, N_EXPERTS, D_FF), 0.01),
        'exp_w_down': nrm((L, N_EXPERTS, D_FF, D), D_FF ** -0.5),
        'exp_b_down': nrm((L, N_EXPERTS, D), 0.01),
        'norm_ple_g': 1.0 + nrm((L, D), 0.02),
        'ple_w_proj': nrm((L, D_PLE, D), D_PLE ** -0.5),
        'ple_w_gate': nrm((L, D, D), D ** -0.5),
        'final_norm_g': 1.0 + nrm((D,), 0.02),
    }

def reference(x, p, norm_mix_g, w_in, s5_lam_re, s5_lam_im, s5_log_dt, s5_b_re, s5_b_im,
              s5_c_re, s5_c_im, s5_d, s5_w_glu, rwkv_mu_rkv, rwkv_mu_wag, rwkv_w0, rwkv_w1,
              rwkv_w2, rwkv_a0, rwkv_a1, rwkv_a2, rwkv_g1, rwkv_g2, rwkv_k_k, rwkv_k_a,
              rwkv_r_k, rwkv_ln_w, rwkv_ln_b, w_out, norm_moe_g, router_w, router_b,
              exp_w_gate, exp_b_gate, exp_w_up, exp_b_up, exp_w_down, exp_b_down,
              norm_ple_g, ple_w_proj, ple_w_gate, final_norm_g):
    r0 = S5_WIDTH
    k0 = r0 + RWKV_WIDTH
    v0 = k0 + RWKV_WIDTH
    for i in range(DEPTH):
        h = rms_norm(x, norm_mix_g[i])
        proj = h @ w_in[i]
        y_s5 = s5_mixer(proj[..., :r0], s5_lam_re[i], s5_lam_im[i], s5_log_dt[i],
                        s5_b_re[i], s5_b_im[i], s5_c_re[i], s5_c_im[i], s5_d[i], s5_w_glu[i])
        y_rwkv = rwkv7_mixer(h, proj[..., r0:k0], proj[..., k0:v0], proj[..., v0:],
                             rwkv_mu_rkv[i], rwkv_mu_wag[i], rwkv_w0[i], rwkv_w1[i], rwkv_w2[i],
                             rwkv_a0[i], rwkv_a1[i], rwkv_a2[i], rwkv_g1[i], rwkv_g2[i],
                             rwkv_k_k[i], rwkv_k_a[i], rwkv_r_k[i], rwkv_ln_w[i], rwkv_ln_b[i])
        x = x + jnp.concatenate([y_s5, y_rwkv], axis=-1) @ w_out[i]
        x = x + moe_ffn(rms_norm(x, norm_moe_g[i]), router_w[i], router_b[i],
                        exp_w_gate[i], exp_b_gate[i], exp_w_up[i], exp_b_up[i],
                        exp_w_down[i], exp_b_down[i])
        gate = jax.nn.sigmoid(rms_norm(x, norm_ple_g[i]) @ ple_w_gate[i])
        x = x + (p[i] @ ple_w_proj[i]) * gate
    return rms_norm(x, final_norm_g)


_drawn_inputs = setup_inputs


def setup_inputs(seed=0):
    import zlib

    import numpy as np

    out = dict(_drawn_inputs(seed))
    spreads = {}
    factors = {'s5_lam_re': 200.0,
     'rwkv_k_k': 3.204,
     'rwkv_ln_b': 3.074,
     'exp_b_gate': 8.0,
     'exp_b_up': 8.0,
     'exp_b_down': 8.0,
     'norm_ple_g': 41.422,
     's5_log_dt': 18.589,
     's5_b_re': 17.523,
     's5_b_im': 10.142,
     's5_c_im': 17.267,
     's5_lam_im': 8.0,
     's5_c_re': 8.0}
    for name, (base, spread) in spreads.items():
        noise = np.random.default_rng([zlib.crc32(name.encode()), seed]).standard_normal(out[name].shape)
        drawn = base * np.exp(spread * noise) if base else spread * noise
        out[name] = __import__('jax').numpy.asarray(drawn.astype(out[name].dtype))
    for name, factor in factors.items():
        out[name] = (out[name] * factor).astype(out[name].dtype)
    return out
```

```python
from contextlib import ExitStack

import numpy as np
import concourse.bass as bass
from concourse import mybir

P = 128
T = 256
D = 1024
KD = D // P
W = 512
FT = W // P
TT = T // P
CH = 64
NCH = T // CH
UNITS = NCH * FT
NJ = 16
E = 32
SLOTS = 64
MAX_PASS = T // SLOTS
NC = 12
UNIT = 1024
ARENA = 46

F32 = mybir.dt.float32
BF16 = mybir.dt.bfloat16
I32 = mybir.dt.int32
U32 = mybir.dt.uint32
ALU = mybir.AluOpType
ACT = mybir.ActivationFunctionType
AX = mybir.AxisListType

INV_2PI = float(1.0 / (2.0 * np.pi))
ROUND = float(1.5 * 2 ** 23)
PI_A, PI_B = 6.28125, float(2 * np.pi - 6.28125)
PI = 3.1415925
DECAY = float(np.exp(-0.5))

C_ID, C_ONES, C_TRI, C_HEAD, C_IOTA = 0, 128, 256, 384, 512
C_ID2, C_SU, C_UI, C_SL1, C_SU1 = 640, 704, 768, 832, 896
C_LEV = 960
LEVELS = 5
C_TIME = C_LEV + 64 * LEVELS
C_E32 = C_TIME + T
NCONST = C_E32 + E
PARAMS = {}
for _n, _c in (("g_mix", KD), ("mu_w", KD), ("mu_a", KD), ("mu_g", KD), ("mu_r", FT), ("mu_k", FT),
               ("mu_v", FT), ("w0", FT), ("a0", FT), ("k_k", FT), ("k_a", FT), ("r_k", FT),
               ("ln_w", FT), ("ln_b", FT), ("s5_d", FT), ("g_moe", KD), ("g_ple", KD),
               ("lam_re", NJ), ("lam_im", NJ), ("log_dt", NJ)):
    PARAMS[_n] = (sum(c for _, c in PARAMS.values()), _c)
NPARAM = sum(c for _, c in PARAMS.values())


def constants():
    p = np.arange(P)
    c = np.zeros((P, NCONST), np.float32)
    c[:, C_ID:C_ID + P] = np.eye(P)
    c[:, C_ONES:C_ONES + P] = 1.0
    c[:, C_TRI:C_TRI + P] = p[:, None] < p[None, :]
    c[:, C_HEAD:C_HEAD + P] = p[:, None] // CH == p[None, :] // CH
    c[:, C_IOTA:C_IOTA + P] = np.arange(P) % SLOTS
    s, t = p[:, None] % CH, np.arange(CH)[None, :]
    c[:, C_ID2:C_ID2 + CH] = s == t
    c[:, C_SU:C_SU + CH] = s < t
    c[:, C_UI:C_UI + CH] = s <= t
    c[:, C_SU1:C_SU1 + CH] = (s < t) & (s // 2 == t // 2)
    c[:, C_SL1:C_SL1 + CH] = (s > t) & (s // 2 == t // 2)
    for n in range(LEVELS):
        b = 2 << n
        c[:, C_LEV + n * CH:C_LEV + (n + 1) * CH] = (s // (2 * b) == t // (2 * b)) & (s // b > t // b)
    c[:, C_TIME:C_TIME + T] = np.arange(T)
    c[:, C_E32:C_E32 + E] = np.arange(E)
    return c


def layer(nc, io):
    with ExitStack() as ctx:
        def sb(name, shape, dt=F32):
            return ctx.enter_context(nc.sbuf_tensor(name, shape, dt))

        def sem(name):
            return ctx.enter_context(nc.semaphore(name))

        arena = sb("arena", [P, ARENA * UNIT])
        con = sb("con", [P, NCONST])
        par = sb("par", [P, NPARAM + 2])
        lora_hidden = sb("lora_hidden", [P, 2 * T])
        bb = sb("bb", [P, 2, NJ * 32])
        cc = sb("cc", [P, 2, NJ * 32])
        s5p = sb("s5p", [P, 20, NJ])
        small = sb("small", [P, 64])
        chunk_decay = sb("chunk_decay", [P, FT, NCH])
        u0 = sb("u0", [P, FT * CH])
        uu = sb("uu", [P, FT * CH])
        state = sb("state", [P, FT * CH])
        banks = [ctx.enter_context(nc.psum_tensor(f"bank{i}", [P, 512], F32)) for i in range(8)]

        def un(i, n=1):
            return arena[:, i * UNIT:(i + n) * UNIT]

        def feat(i, n=1):
            return un(i, n).rearrange("p (f t) -> p f t", t=T)

        def units(i):
            return un(i).rearrange("p (u t) -> p u t", t=CH)

        def prm(name):
            a, n = PARAMS[name]
            return par[:, a:a + n]

        ident = con[:, C_ID:C_ID + P]
        ones = con[:, C_ONES:C_ONES + P]
        head_ones = con[:, C_HEAD:C_HEAD + P]

        xT, sq, hT, dh = feat(31, 2), feat(33, 2), feat(35, 2), feat(33, 2)
        xw, xa, xg = feat(37, 2), feat(39, 2), feat(41, 2)
        lora1 = un(26, 2).rearrange("p (k f) -> p k f", k=KD)
        lora2 = un(28)
        wglu = un(29, 2).rearrange("p (k f) -> p k f", k=FT)
        uT = feat(24)
        raw = {"k": feat(43), "r": feat(44), "v": feat(45)}
        S5C, S5S = [feat(16), feat(18)], [feat(17), feat(19)]
        sA, sB, sT1, sT2 = feat(20), feat(21), feat(22), feat(23)
        lw, la, lg = feat(31), feat(32), feat(33)
        tmp = feat(34)
        rr, kx, vv = feat(37), feat(38), feat(39)
        kkn, k2, kb, bonus = feat(40), feat(41), feat(42), feat(43)
        Lc, EL = feat(44), feat(45)
        at, bh, kh, rt = feat(31), feat(42), feat(41), feat(37)
        rk = feat(34)
        Vs, Bs, Ks = units(32), units(34), units(35)
        X, Y, Wk, Mx, MO = units(36), units(38), units(40), units(44), units(45)
        KA, RB, RK = units(26), units(27), units(28)
        yT = feat(45)
        yc, ysq, yrs = feat(36), feat(38), feat(40)
        ys5 = feat(25)
        mix_s5, mix_rw = feat(24), feat(35)
        x_tok = un(31, 2).rearrange("p (t d) -> p t d", d=D)
        x2 = x_tok
        wout = [un(8 + 2 * c, 2).rearrange("p (k n) -> p k n", n=D) for c in range(4)]
        ring = [un(2 * c, 2).rearrange("p (k n) -> p k n", n=D) for c in range(NC)]
        win = [un(2 * c, 2).rearrange("p (k n) -> p k n", n=T) for c in range(8)]

        s = {n: sem(n) for n in (
            "consts_in", "s5_in", "xT_in", "lora_in", "lora2_in", "glu_in", "x_in",
            "eps_ready", "sq_ready", "rms_summed", "rms_root", "kk_root", "var_root", "h_ready", "mixed", "proj_done", "proj_copied",
            "lora1_done", "lora_hidden_ready", "lora2_done", "lora2_copied",
            "s5_dt", "s5_arg", "s5_mag", "s5_theta", "s5_sin", "bb_ready", "bb_turned", "bb_copied",
            "table_arg", "table_sin", "table_ready", "bu_done", "bu_copied", "phase_off",
            "scanned", "phase_on", "s5_out_done", "s5_y", "s5_gelu", "glu_done", "glu_sig", "mix_s5_ready",
            "kk_ready", "kk_squared", "kk_summed", "decay_ready", "exp_ready", "scaled", "rk_ready",
            "rk_summed", "bonus_ready", "scores_done", "scores_copied", "turned", "turned_copied",
            "w_done", "w_copied", "xy_done", "xy_ready", "mo_ready", "state_zero",
            "u0_done", "u0_ready", "u_done", "u_ready", "state_done", "state_ready", "y_done", "y_copied",
            "mean_done", "centred", "y_squared", "var_done", "mix_rw_ready",
            "out_done", "x2_ready", "dve_chain", "act_chain", "pool_chain")}
        win_in = [sem(f"win_in{q}") for q in range(8)]
        wout_in = sem("wout_in")
        chunk_in = [sem(f"chunk_in{c}") for c in range(NC)]

        def chain(eng, name):
            n = [0]

            def link(ins):
                n[0] += 1
                ins.then_inc(s[name], 1)
                eng.wait_ge(s[name], n[0])
            return link

        def mm(out, lhsT, rhs, start, stop):
            return nc.tensor.matmul(out, lhsT, rhs, start=start, stop=stop, skip_group_check=True)

        def pair(out, lhsT, rhs, start=True, stop=True):
            for h in range(2):
                a = slice(h * CH, (h + 1) * CH)
                last = mm(out[a], lhsT[a], rhs[a], start, stop)
            return last

        order = [0, 1, 4, 5, 2, 3, 6, 7]
        expert_weights = [io["exp_w_gate"], io["exp_w_up"], io["exp_w_down"]]

        def chunk_src(c, e):
            w = expert_weights[c // 4]
            k = 2 * (c % 4)
            return w[bass.ds(e, 1), k * P:(k + 2) * P, :].rearrange("o (k p) n -> p (o k) n", p=P)

        with nc.Block() as block:
            @block.sync
            def _(sp):
                sp.dma_start(xT[:, :, :], io["xT"].rearrange("(k p) t -> p k t", p=P)).then_inc(s["xT_in"], 16)
                sp.dma_start(con[:, :], io["consts"]).then_inc(s["consts_in"], 16)
                sp.dma_start(par[:, 0:NPARAM], io["params"]).then_inc(s["consts_in"], 16)
                w = io["w_in"].rearrange("(k p) n -> p k n", p=P)
                for n, q in enumerate(order):
                    sp.dma_start(win[q][:, :, :], w[:, :, q * T:(q + 1) * T]).then_inc(win_in[q], 16)
                    if n == 1:
                        sp.dma_start(lora1[:, :, :], io["lora1"].rearrange("(k p) n -> p k n", p=P)).then_inc(s["lora_in"], 16)
                        sp.dma_start(lora2[:, :], io["lora2"]).then_inc(s["lora2_in"], 16)
                sp.dma_start(wglu[:, :, :], io["w_glu"].rearrange("(k p) n -> p k n", p=P)).then_inc(s["glu_in"], 16)
                sp.wait_ge(s["proj_done"], 8)
                wo = io["w_out"].rearrange("(c k p) n -> c p k n", p=P, k=2)
                for c in range(4):
                    sp.dma_start(wout[c][:, :, :], wo[c]).then_inc(wout_in, 16)
                for c in range(4):
                    sp.dma_start(ring[c][:, :, :], chunk_src(c, 0)).then_inc(chunk_in[c], 16)
                sp.wait_ge(s["u0_done"], NCH)
                sp.wait_ge(s["y_done"], NCH)
                sp.wait_ge(s["state_done"], NCH - 1)
                sp.dma_start(x_tok[:, :, :], io["x"].rearrange("(t p) d -> p t d", p=P)).then_inc(s["x_in"], 16)

            @block.gpsimd
            def _(pool):
                link = chain(pool, "pool_chain")
                pool.dma_start(bb[:, 0, :], io["s5_b_re"]).then_inc(s["s5_in"], 16)
                pool.dma_start(bb[:, 1, :], io["s5_b_im"]).then_inc(s["s5_in"], 16)
                pool.dma_start(cc[:, 0, :], io["s5_c_re"]).then_inc(s["s5_in"], 16)
                pool.dma_start(cc[:, 1, :], io["s5_c_im"]).then_inc(s["s5_in"], 16)
                tt = nc.gpsimd.tensor_tensor
                for g in range(4):
                    c, sn = S5C[g % 2], S5S[g % 2]
                    pool.wait_ge(s["bu_copied"], 4 * (g + 1))
                    pool.wait_ge(s["table_ready"], g + 1)
                    tt(sT1, sA, c, ALU.mult)
                    link(tt(sT2, sB, sn, ALU.mult))
                    link(tt(sT1, sT1, sT2, ALU.add))
                    link(tt(sT2, sA, sn, ALU.mult))
                    link(tt(sA, sB, c, ALU.mult))
                    tt(sT2, sA, sT2, ALU.subtract).then_inc(s["phase_off"], 1)
                    pool.wait_ge(s["scanned"], g + 1)
                    tt(sT1, sA, c, ALU.mult)
                    link(tt(sT2, sB, sn, ALU.mult))
                    link(tt(sT1, sT1, sT2, ALU.subtract))
                    link(tt(sT2, sA, sn, ALU.mult))
                    link(tt(sA, sB, c, ALU.mult))
                    tt(sT2, sA, sT2, ALU.add).then_inc(s["phase_on"], 1)
                    if g < 3:
                        pool.wait_ge(s["s5_out_done"], g + 1)

            @block.scalar
            def _(act):
                link = chain(act, "act_chain")
                A = nc.scalar.activation
                act.wait_ge(s["xT_in"], 16)
                A(sq[:, :, :], xT[:, :, :], ACT.Square).then_inc(s["sq_ready"], 1)
                act.wait_ge(s["consts_in"], 32)
                A(s5p[:, 0, :], prm("log_dt"), ACT.Exp).then_inc(s["s5_dt"], 1)
                act.wait_ge(s["rms_summed"], 1)
                act.wait_ge(s["eps_ready"], 1)
                A(un(43)[:, 0:T], banks[7][:, 0:T], ACT.Sqrt, bias=par[:, NPARAM:NPARAM + 1], scale=1.0 / D).then_inc(s["rms_root"], 1)
                act.wait_ge(s["s5_arg"], 1)
                A(s5p[:, 4, :], s5p[:, 2, :], ACT.Exp).then_inc(s["s5_mag"], 1)
                act.wait_ge(s["s5_theta"], 1)
                A(s5p[:, 7, :], s5p[:, 5, :], ACT.Sin)
                A(s5p[:, 8, :], s5p[:, 5, :], ACT.Sin, scale=0.5).then_inc(s["s5_sin"], 1)
                act.wait_ge(s["s5_in"], 64)
                A(cc[:, 1, :], cc[:, 1, :], ACT.Copy, scale=-1.0).then_inc(s["bb_copied"], 1)
                act.wait_ge(s["bb_turned"], 1)
                A(bb[:, 0, :], banks[5][:, :], ACT.Copy)
                A(bb[:, 1, :], banks[6][:, :], ACT.Copy).then_inc(s["bb_copied"], 1)

                def copy_proj(n):
                    q = order[n]
                    act.wait_ge(s["proj_done"], n + 1)
                    if q < 2:
                        dst = uT[:, 2 * q:2 * q + 2, :]
                    else:
                        dst = raw["rkv"[(q - 2) // 2]][:, 2 * (q % 2):2 * (q % 2) + 2, :]
                    A(dst, banks[n % 2][:, :].rearrange("p (f t) -> p f t", t=T), ACT.Copy).then_inc(s["proj_copied"], 1)

                def table_sin(g):
                    act.wait_ge(s["table_arg"], g + 1)
                    A(S5C[g % 2][:, :, :], S5S[g % 2][:, :, :], ACT.Sin, scale=0.5)
                    A(S5S[g % 2][:, :, :], S5S[g % 2][:, :, :], ACT.Sin).then_inc(s["table_sin"], 1)

                def bu_copy(g):
                    for j in range(4):
                        act.wait_ge(s["bu_done"], 4 * g + j + 1)
                        if g and j == 0:
                            act.wait_ge(s["phase_on"], g)
                        A(sA[:, j, :], banks[2 + j % 2][:, 0:T], ACT.Copy)
                        A(sB[:, j, :], banks[2 + j % 2][:, T:2 * T], ACT.Copy).then_inc(s["bu_copied"], 1)

                for n in range(2):
                    copy_proj(n)
                act.wait_ge(s["lora1_done"], 2)
                A(lora_hidden[0:CH, 0:T], banks[4][0:CH, 0:T], ACT.Tanh)
                A(lora_hidden[CH:P, 0:T], banks[4][CH:P, 0:T], ACT.Copy).then_inc(s["lora_hidden_ready"], 1)
                act.wait_ge(s["lora1_done"], 3)
                A(lora_hidden[:, T:2 * T], banks[3][:, 0:T], ACT.Sigmoid).then_inc(s["lora_hidden_ready"], 1)
                bu_copy(0)
                for m, (dst, bias) in enumerate(((lw, "w0"), (la, "a0"), (lg, None))):
                    if m == 0:
                        act.wait_ge(s["h_ready"], 1)
                    if m == 2:
                        act.wait_ge(s["mixed"], 3)
                    for i in range(FT):
                        if i % 2 == 0:
                            act.wait_ge(s["lora2_done"], 2 * m + i // 2 + 1)
                        src = banks[5 + i // 2][:, (i % 2) * T:(i % 2 + 1) * T]
                        if bias:
                            last = A(dst[:, i, :], src, ACT.Sigmoid, bias=prm(bias)[:, i:i + 1])
                        else:
                            last = A(dst[:, i, :], src, ACT.Copy)
                        if i % 2:
                            last.then_inc(s["lora2_copied"], 1)
                for n in range(2, 8):
                    if n == 2:
                        act.wait_ge(s["lora1_done"], 3)
                    copy_proj(n)
                    if n == 3:
                        table_sin(0)
                table_sin(1)
                act.wait_ge(s["kk_ready"], 1)
                A(tmp[:, :, :], kkn[:, :, :], ACT.Square).then_inc(s["kk_squared"], 1)
                act.wait_ge(s["kk_summed"], 1)
                for b in range(2):
                    m = A(kb[:, 2 * b:2 * b + 2, :], banks[4 + b].rearrange("p (f t) -> p f t", t=T), ACT.Sqrt)
                m.then_inc(s["kk_root"], 1)
                act.wait_ge(s["decay_ready"], 1)
                A(EL[:, :, :], Lc[:, :, :], ACT.Exp)
                link(A(chunk_decay[:, :, :], Lc[:, :, CH - 1::CH], ACT.Exp))
                A(Lc[:, :, :], Lc[:, :, :], ACT.Exp, scale=-1.0)
                A(lw[:, :, :], lw[:, :, :], ACT.Exp).then_inc(s["exp_ready"], 1)
                bu_copy(1)
                for m, dst in enumerate((Vs, Bs, Ks)):
                    if m == 0:
                        act.wait_ge(s["scaled"], 1)
                    if m == 1:
                        act.wait_ge(s["bonus_ready"], 1)
                    for b in range(2):
                        act.wait_ge(s["turned"], 2 * m + b + 1)
                        A(dst[:, 8 * b:8 * b + 8, :], banks[b].rearrange("p (u t) -> p u t", t=CH), ACT.Copy).then_inc(s["turned_copied"], 1)
                for lev in range(LEVELS):
                    for b in range(2):
                        act.wait_ge(s["w_done"], 2 * lev + b + 1)
                        A(Wk[:, 8 * b:8 * b + 8, :], banks[4 + b].rearrange("p (u t) -> p u t", t=CH), ACT.Copy).then_inc(s["w_copied"], 1)
                    if lev == 1:
                        table_sin(2)
                    if lev == 3:
                        table_sin(3)
                    if lev == 4:
                        bu_copy(2)
                for c in range(NCH):
                    act.wait_ge(s["u0_done"], c + 1)
                    A(u0[:, :], banks[0][:, 0:FT * CH], ACT.Copy).then_inc(s["u0_ready"], 1)
                    act.wait_ge(s["u_done"], c + 1)
                    A(uu[:, :], banks[1][:, 0:FT * CH], ACT.Copy).then_inc(s["u_ready"], 1)
                    act.wait_ge(s["y_done"], c + 1)
                    if c == 0:
                        act.wait_ge(s["w_done"], 2 * LEVELS)
                    A(yT[:, :, c * CH:(c + 1) * CH], banks[5][:, 0:FT * CH].rearrange("p (f t) -> p f t", t=CH), ACT.Copy).then_inc(s["y_copied"], 1)
                act.wait_ge(s["centred"], 1)
                A(ysq[:, :, :], yc[:, :, :], ACT.Square).then_inc(s["y_squared"], 1)
                act.wait_ge(s["var_done"], 1)
                for b in range(2):
                    m = A(yrs[:, 2 * b:2 * b + 2, :], banks[4 + b].rearrange("p (f t) -> p f t", t=T), ACT.Sqrt,
                          bias=par[:, NPARAM + 1:NPARAM + 2], scale=1.0 / CH)
                m.then_inc(s["var_root"], 1)
                bu_copy(3)
                act.wait_ge(s["s5_y"], 4)
                A(ys5[:, :, :], ys5[:, :, :], ACT.Gelu_apprx_tanh).then_inc(s["s5_gelu"], 1)
                for b in range(2):
                    act.wait_ge(s["glu_done"], b + 1)
                    act.wait_ge(s["s5_y"], 4)
                    A(mix_s5[:, 2 * b:2 * b + 2, :], banks[b].rearrange("p (f t) -> p f t", t=T), ACT.Sigmoid).then_inc(s["glu_sig"], 1)

            @block.vector
            def _(dve):
                link = chain(dve, "dve_chain")
                V = nc.vector
                tt, ts, stt = V.tensor_tensor, V.tensor_scalar, V.scalar_tensor_tensor

                def reduce_angle(dst, turns, arg):
                    link(ts(turns, arg, INV_2PI, ROUND, ALU.mult, ALU.add))
                    link(ts(turns, turns, -ROUND, None, ALU.add))
                    link(stt(dst, turns, -PI_A, arg, ALU.mult, ALU.add))
                    link(stt(dst, turns, -PI_B, dst, ALU.mult, ALU.add))

                V.memset(par[:, NPARAM:NPARAM + 1], 1e-6)
                V.memset(par[:, NPARAM + 1:NPARAM + 2], 64e-5).then_inc(s["eps_ready"], 1)
                lre, lim = s5p[:, 1, :], prm("lam_im")
                dve.wait_ge(s["consts_in"], 32)
                link(ts(lre, prm("lam_re"), -1e-4, None, ALU.min))
                dve.wait_ge(s["s5_dt"], 1)
                tt(s5p[:, 2, :], lre, s5p[:, 0, :], ALU.mult).then_inc(s["s5_arg"], 1)
                link(tt(s5p[:, 3, :], lim, s5p[:, 0, :], ALU.mult))
                reduce_angle(s5p[:, 5, :], s5p[:, 6, :], s5p[:, 3, :])
                ts(s5p[:, 5, :], s5p[:, 5, :], PI, -PI, ALU.min, ALU.max).then_inc(s["s5_theta"], 1)
                dve.wait_ge(s["rms_root"], 1)
                link(V.reciprocal(un(43)[:, 0:T], un(43)[:, 0:T]))
                for k in range(KD):
                    h = stt(hT[:, k, :], xT[:, k, :], prm("g_mix")[:, k:k + 1], un(43)[:, 0:T], ALU.mult, ALU.mult)
                h.then_inc(s["h_ready"], 1)
                dve.wait_ge(s["h_ready"], 1)
                dve.wait_ge(s["s5_sin"], 1)
                dve.wait_ge(s["s5_mag"], 1)
                sh2, cs, lbr, lbi, zre = (s5p[:, i, :] for i in range(9, 14))
                den, ca, cb, cr, ci = (s5p[:, i, :] for i in range(14, 19))
                link(tt(sh2, s5p[:, 8, :], s5p[:, 8, :], ALU.mult))
                link(ts(cs, sh2, -2.0, 1.0, ALU.mult, ALU.add))
                link(tt(lbr, s5p[:, 4, :], cs, ALU.mult))
                link(tt(lbi, s5p[:, 4, :], s5p[:, 7, :], ALU.mult))
                link(ts(zre, lbr, -1.0, None, ALU.add))
                link(tt(ca, lre, lre, ALU.mult))
                link(tt(cb, lim, lim, ALU.mult))
                link(tt(den, ca, cb, ALU.add))
                link(V.reciprocal(den, den))
                link(tt(ca, zre, lre, ALU.mult))
                link(tt(cb, lbi, lim, ALU.mult))
                link(tt(ca, ca, cb, ALU.add))
                link(tt(cr, ca, den, ALU.mult))
                link(tt(ca, lbi, lre, ALU.mult))
                link(tt(cb, zre, lim, ALU.mult))
                link(tt(ca, ca, cb, ALU.subtract))
                link(tt(ci, ca, den, ALU.mult))
                dve.wait_ge(s["s5_in"], 64)
                bre = bb[:, 0, :].rearrange("p (j c) -> p j c", j=NJ)
                bim = bb[:, 1, :].rearrange("p (j c) -> p j c", j=NJ)
                crb = cr[:, :, None].to_broadcast([P, NJ, 32])
                cib = ci[:, :, None].to_broadcast([P, NJ, 32])
                q1, q2, q3 = (un(44)[:, i * 512:(i + 1) * 512].rearrange("p (j c) -> p j c", j=NJ) for i in (0, 1, 2 - 2))
                q3 = un(45)[:, 0:512].rearrange("p (j c) -> p j c", j=NJ)
                link(tt(q1, bre, crb, ALU.mult))
                link(tt(q2, bim, cib, ALU.mult))
                link(tt(q1, q1, q2, ALU.subtract))
                link(tt(q2, bim, crb, ALU.mult))
                link(tt(q3, bre, cib, ALU.mult))
                link(V.tensor_copy(bre, q1))
                tt(bim, q2, q3, ALU.add).then_inc(s["bb_ready"], 1)
                tt(dh[:, :, 1:T], hT[:, :, 0:T - 1], hT[:, :, 1:T], ALU.subtract)
                link(ts(dh[:, :, 0:1], hT[:, :, 0:1], -1.0, None, ALU.mult))
                for dst, mu in ((xw, "mu_w"), (xa, "mu_a"), (xg, "mu_g")):
                    for k in range(KD):
                        m = stt(dst[:, k, :], dh[:, k, :], prm(mu)[:, k:k + 1], hT[:, k, :], ALU.mult, ALU.add)
                    m.then_inc(s["mixed"], 1)

                def table_arg(g):
                    c, sn = S5C[g % 2], S5S[g % 2]
                    if g >= 2:
                        dve.wait_ge(s["phase_on"], g - 1)
                    th = s5p[:, 5, 4 * g:4 * g + 4]
                    link(tt(sn, th[:, :, None].to_broadcast([P, 4, T]),
                            con[:, C_TIME:C_TIME + T][:, None, :].to_broadcast([P, 4, T]), ALU.mult))
                    reduce_angle(sn, c, sn)
                    ts(sn, sn, PI, -PI, ALU.min, ALU.max).then_inc(s["table_arg"], 1)

                def table_cos(g):
                    c = S5C[g % 2]
                    dve.wait_ge(s["table_sin"], g + 1)
                    link(tt(c, c, c, ALU.mult))
                    ts(c, c, -2.0, 1.0, ALU.mult, ALU.add).then_inc(s["table_ready"], 1)

                def scan(g):
                    dve.wait_ge(s["phase_off"], g + 1)
                    for j in range(4):
                        mag = s5p[:, 4, 4 * g + j:4 * g + j + 1].to_broadcast([P, T])
                        V.tensor_tensor_scan(sA[:, j, :], mag, sT1[:, j, :], 0.0, ALU.mult, ALU.add)
                        z = V.tensor_tensor_scan(sB[:, j, :], mag, sT2[:, j, :], 0.0, ALU.mult, ALU.add)
                    z.then_inc(s["scanned"], 1)

                def s5_y(g):
                    dve.wait_ge(s["s5_out_done"], g + 1)
                    stt(ys5[:, g, :], uT[:, g, :], prm("s5_d")[:, g:g + 1], banks[2][:, 0:T], ALU.mult, ALU.add).then_inc(s["s5_y"], 1)

                table_arg(0)
                table_arg(1)
                table_cos(0)
                for n, (name, dst) in enumerate((("k", kx), ("r", rr), ("v", vv))):
                    src = raw[name]
                    dve.wait_ge(s["proj_copied"], 4 + 2 * n)
                    if n == 0:
                        dve.wait_ge(s["lora1_done"], 3)
                    tt(tmp[:, :, 1:T], src[:, :, 0:T - 1], src[:, :, 1:T], ALU.subtract)
                    link(ts(tmp[:, :, 0:1], src[:, :, 0:1], -1.0, None, ALU.mult))
                    for i in range(FT):
                        m = stt(dst[:, i, :], tmp[:, i, :], prm("mu_" + name)[:, i:i + 1], src[:, i, :], ALU.mult, ALU.add)
                    link(m)
                    if n == 0:
                        scan(0)
                        for i in range(FT):
                            m = ts(kkn[:, i, :], kx[:, i, :], prm("k_k")[:, i:i + 1], None, ALU.mult)
                        link(m)
                table_cos(1)
                V.tensor_copy(s5p[:, 19, :], s5p[:, 4, :]).then_inc(s["kk_ready"], 1)
                s5_y(0)
                dve.wait_ge(s["lora2_copied"], 6)
                link(ts(lw, lw, -DECAY, None, ALU.mult))
                link(V.memset(EL, 1.0))
                link(V.memset(EL[:, :, 0::CH], 0.0))
                link(V.tensor_tensor_scan(un(44), un(45), un(31), 0.0, ALU.mult, ALU.add))
                tt(lw, Lc, lw, ALU.subtract).then_inc(s["decay_ready"], 1)
                link(ts(k2, la, -1.0, None, ALU.add))
                for i in range(FT):
                    m = ts(k2[:, i, :], k2[:, i, :], prm("k_a")[:, i:i + 1], 1.0, ALU.mult, ALU.add)
                link(m)
                link(tt(k2, k2, kx, ALU.mult))
                dve.wait_ge(s["kk_root"], 1)
                link(ts(kb, kb, 1e-12, None, ALU.max))
                link(V.reciprocal(kb, kb))
                link(tt(kkn, kkn, kb, ALU.mult))
                link(tt(kb, kkn, la, ALU.mult))
                link(tt(rk, rr, k2, ALU.mult))
                for i in range(FT):
                    m = ts(rk[:, i, :], rk[:, i, :], prm("r_k")[:, i:i + 1], None, ALU.mult)
                m.then_inc(s["rk_ready"], 1)
                dve.wait_ge(s["rk_ready"], 1)
                dve.wait_ge(s["exp_ready"], 1)
                stt(un(31), un(31), -1.0, un(40), ALU.mult, ALU.mult)
                tt(bh, kb, Lc, ALU.mult)
                tt(kh, k2, Lc, ALU.mult)
                tt(rt, rr, EL, ALU.mult).then_inc(s["scaled"], 1)
                dve.wait_ge(s["scaled"], 1)
                dve.wait_ge(s["rk_summed"], 1)
                for b in range(2):
                    m = tt(bonus[:, 2 * b:2 * b + 2, :], banks[6 + b].rearrange("p (f t) -> p f t", t=T), vv[:, 2 * b:2 * b + 2, :], ALU.mult)
                m.then_inc(s["bonus_ready"], 1)
                V.memset(state[:, :], 0.0).then_inc(s["state_zero"], 1)
                dve.wait_ge(s["scaled"], 1)

                def col(c):
                    return con[:, c:c + CH][:, None, :].to_broadcast([P, 8, CH])
                eye = col(C_ID2)
                for m, (dst, mask) in enumerate(((X, C_SU1), (Mx, None), (KA, C_SU), (RB, C_UI), (RK, C_UI))):
                    for b in range(2):
                        dve.wait_ge(s["scores_done"], 2 * m + b + 1)
                        src = banks[(4 if m % 2 == 0 else 6) + b].rearrange("p (u t) -> p u t", t=CH)
                        d = dst[:, 8 * b:8 * b + 8, :]
                        if m == 1:
                            link(V.tensor_copy(d, src))
                            link(tt(Y[:, 8 * b:8 * b + 8, :], d, col(C_SL1), ALU.mult))
                            tt(Y[:, 8 * b:8 * b + 8, :], Y[:, 8 * b:8 * b + 8, :], eye, ALU.add).then_inc(s["scores_copied"], 1)
                        elif m == 0:
                            link(tt(d, src, col(mask), ALU.mult))
                            tt(d, d, eye, ALU.add).then_inc(s["scores_copied"], 1)
                        else:
                            tt(d, src, col(mask), ALU.mult).then_inc(s["scores_copied"], 1)
                scan(1)
                for lev in range(LEVELS):
                    if lev:
                        dve.wait_ge(s["w_done"], 2 * lev)
                    for b in range(2):
                        lm = con[:, C_LEV + lev * CH:C_LEV + (lev + 1) * CH][:, None, :].to_broadcast([P, 8, CH])
                        if lev == 0:
                            dve.wait_ge(s["scores_copied"], 4)
                        tt(MO[:, 8 * b:8 * b + 8, :], Mx[:, 8 * b:8 * b + 8, :], lm, ALU.mult).then_inc(s["mo_ready"], 1)
                    for m, dst in enumerate((X, Y)):
                        if lev == LEVELS - 1 and m:
                            continue
                        if m == 0:
                            dve.wait_ge(s["xy_done"], 4 * (lev + 1) if lev < LEVELS - 1 else 4 * lev + 2)
                        for b in range(2):
                            d = dst[:, 8 * b:8 * b + 8, :]
                            tt(d, d, banks[(6 if m == 0 else 0) + b].rearrange("p (u t) -> p u t", t=CH), ALU.add).then_inc(s["xy_ready"], 1)
                    if lev == 0:
                        table_arg(2)
                    if lev == 1:
                        table_cos(2)
                    if lev == 2:
                        table_arg(3)
                    if lev == 3:
                        s5_y(1)
                        table_cos(3)
                for c in range(NCH - 1):
                    dve.wait_ge(s["state_done"], c + 1)
                    dve.wait_ge(s["y_done"], c + 1)
                    link(tt(state[:, :], banks[4][:, 0:FT * CH], state[:, :], ALU.add))
                    tt(state[:, :].rearrange("p (f v) -> p f v", v=CH), state[:, :].rearrange("p (f v) -> p f v", v=CH),
                       chunk_decay[:, :, c:c + 1].to_broadcast([P, FT, CH]), ALU.mult).then_inc(s["state_ready"], 1)
                    if c == 1:
                        scan(2)
                dve.wait_ge(s["mean_done"], 1)
                for b in range(2):
                    m = stt(yc[:, 2 * b:2 * b + 2, :], banks[6 + b].rearrange("p (f t) -> p f t", t=T), -1.0 / CH, yT[:, 2 * b:2 * b + 2, :], ALU.mult, ALU.add)
                m.then_inc(s["centred"], 1)
                dve.wait_ge(s["centred"], 1)
                dve.wait_ge(s["var_root"], 1)
                link(V.reciprocal(yrs, yrs))
                link(tt(yc, yc, yrs, ALU.mult))
                for i in range(FT):
                    m = ts(yc[:, i, :], yc[:, i, :], prm("ln_w")[:, i:i + 1], prm("ln_b")[:, i:i + 1], ALU.mult, ALU.add)
                link(m)
                link(tt(yc, yc, bonus, ALU.add))
                tt(mix_rw, yc, lg, ALU.mult).then_inc(s["mix_rw_ready"], 1)
                s5_y(2)
                scan(3)
                s5_y(3)
                for b in range(2):
                    dve.wait_ge(s["glu_sig"], b + 1)
                    tt(mix_s5[:, 2 * b:2 * b + 2, :], mix_s5[:, 2 * b:2 * b + 2, :], ys5[:, 2 * b:2 * b + 2, :], ALU.mult).then_inc(s["mix_s5_ready"], 1)
                dve.wait_ge(s["x_in"], 16)
                for t in range(TT):
                    for hf in range(2):
                        n = 2 * t + hf
                        dve.wait_ge(s["out_done"], n + 1)
                        tt(x2[:, t, hf * 512:(hf + 1) * 512], x_tok[:, t, hf * 512:(hf + 1) * 512], banks[n][:, :], ALU.add).then_inc(s["x2_ready"], 1)

            @block.tensor
            def _(pe):
                pe.wait_ge(s["consts_in"], 32)
                pe.wait_ge(s["sq_ready"], 1)
                for k in range(KD):
                    last = mm(banks[7][:, 0:T], ones, sq[:, k, :], k == 0, k == KD - 1)
                last.then_inc(s["rms_summed"], 1)
                pe.wait_ge(s["bb_ready"], 1)
                for m in range(2):
                    for J in range(4):
                        last = nc.tensor.transpose(banks[5 + m][:, J * P:(J + 1) * P], bb[:, m, J * P:(J + 1) * P], ident)
                last.then_inc(s["bb_turned"], 1)

                def project(n):
                    q = order[n]
                    pe.wait_ge(win_in[q], 16)
                    if n >= 2:
                        pe.wait_ge(s["proj_copied"], n - 1)
                    for f in range(2):
                        for k in range(KD):
                            last = mm(banks[n % 2][:, f * T:(f + 1) * T], win[q][:, k, f * P:(f + 1) * P], hT[:, k, :], k == 0, k == KD - 1)
                    last.then_inc(s["proj_done"], 1)

                def bu(g):
                    pe.wait_ge(s["bb_copied"], 2)
                    pe.wait_ge(s["proj_copied"], 2)
                    pe.wait_ge(s["lora_hidden_ready"], 2)
                    if g:
                        pe.wait_ge(s["s5_y"], g)
                    for j in range(4):
                        if 4 * g + j >= 2:
                            pe.wait_ge(s["bu_copied"], 4 * g + j - 1)
                        a = slice(32 * j, 32 * j + 32)
                        for m in range(2):
                            last = mm(banks[2 + j % 2][:, m * T:(m + 1) * T], bb[a, m, g * P:(g + 1) * P], uT[a, g, :], True, True)
                        last.then_inc(s["bu_done"], 1)

                def s5_out(g):
                    pe.wait_ge(s["phase_on"], g + 1)
                    for j in range(4):
                        a = slice(32 * j, 32 * j + 32)
                        for m, src in enumerate((sT1, sT2)):
                            last = mm(banks[2][a, 0:T], cc[:, m, (4 * g + j) * 32:(4 * g + j + 1) * 32], src[:, j, :], m == 0, m == 1)
                    last.then_inc(s["s5_out_done"], 1)

                pe.wait_ge(s["h_ready"], 1)
                project(0)
                project(1)
                pe.wait_ge(s["lora_in"], 16)
                for m, (src, a, b, out) in enumerate(((xw, 0, 64, banks[4][0:CH, 0:T]), (xa, 64, 128, banks[4][CH:P, 0:T]),
                                                      (xg, 128, 256, banks[3][:, 0:T]))):
                    pe.wait_ge(s["mixed"], m + 1)
                    for k in range(KD):
                        last = mm(out, lora1[:, k, a:b], src[:, k, :], k == 0, k == KD - 1)
                    last.then_inc(s["lora1_done"], 1)
                bu(0)
                pe.wait_ge(s["lora2_in"], 16)
                for m in range(3):
                    pe.wait_ge(s["lora_hidden_ready"], 1 if m < 2 else 2)
                    for i in range(FT):
                        if m and i % 2 == 0:
                            pe.wait_ge(s["lora2_copied"], 2 * m - 2 + i // 2 + 1)
                        out = banks[5 + i // 2][:, (i % 2) * T:(i % 2 + 1) * T]
                        if m == 0:
                            last = mm(out, lora2[0:CH, i * P:(i + 1) * P], lora_hidden[0:CH, 0:T], True, True)
                        elif m == 1:
                            last = mm(out, lora2[CH:P, i * P:(i + 1) * P], lora_hidden[CH:P, 0:T], True, True)
                        else:
                            last = mm(out, lora2[:, W + i * P:W + (i + 1) * P], lora_hidden[:, T:2 * T], True, True)
                        if i % 2:
                            last.then_inc(s["lora2_done"], 1)
                for n in range(2, 8):
                    project(n)
                pe.wait_ge(s["kk_squared"], 1)
                for b in range(2):
                    last = mm(banks[4 + b][:, :], head_ones, tmp[:, 2 * b:2 * b + 2, :], True, True)
                last.then_inc(s["kk_summed"], 1)
                s5_out(0)
                bu(1)
                pe.wait_ge(s["rk_ready"], 1)
                pe.wait_ge(s["lora2_copied"], 6)
                for b in range(2):
                    last = mm(banks[6 + b][:, :], head_ones, rk[:, 2 * b:2 * b + 2, :], True, True)
                last.then_inc(s["rk_summed"], 1)

                def fm(arr, u):
                    return arr[:, u % FT, (u // FT) * CH:(u // FT + 1) * CH]

                pe.wait_ge(s["scaled"], 1)
                pe.wait_ge(s["proj_copied"], 8)
                for m, (l, r) in enumerate(((bh, at), (at, bh), (kh, at), (bh, rt), (kh, rt))):
                    if m == 1:
                        pe.wait_ge(s["bonus_ready"], 1)
                    for b in range(2):
                        if m >= 2:
                            pe.wait_ge(s["scores_copied"], 2 * m - 4 + b + 1)
                        bank = banks[(4 if m % 2 == 0 else 6) + b]
                        for u in range(8 * b, 8 * b + 8):
                            last = pair(bank[:, (u % 8) * CH:(u % 8 + 1) * CH], fm(l, u), fm(r, u))
                        last.then_inc(s["scores_done"], 1)
                    if m in (1, 2, 3):
                        src = (vv, bh, kh)[m - 1]
                        for b in range(2):
                            if m > 1:
                                pe.wait_ge(s["turned_copied"], 2 * (m - 1) - 2 + b + 1)
                            for u in range(8 * b, 8 * b + 8):
                                last = pair(banks[b][:, (u % 8) * CH:(u % 8 + 1) * CH], fm(src, u), con[:, C_ID2:C_ID2 + CH])
                            last.then_inc(s["turned"], 1)
                for lev in range(LEVELS):
                    if lev == 0:
                        pe.wait_ge(s["scores_copied"], 10)
                        pe.wait_ge(s["turned_copied"], 6)
                    else:
                        pe.wait_ge(s["xy_ready"], 4 * lev)
                    for b in range(2):
                        pe.wait_ge(s["mo_ready"], 2 * lev + b + 1)
                        for u in range(8 * b, 8 * b + 8):
                            last = pair(banks[4 + b][:, (u % 8) * CH:(u % 8 + 1) * CH], MO[:, u, :], X[:, u, :])
                        last.then_inc(s["w_done"], 1)
                    if lev == 3:
                        s5_out(1)
                    if lev == 4:
                        bu(2)
                    for m in range(2 if lev < LEVELS - 1 else 1):
                        for b in range(2):
                            pe.wait_ge(s["w_copied"], 2 * lev + b + 1)
                            for u in range(8 * b, 8 * b + 8):
                                out = banks[(6 if m == 0 else 0) + b][:, (u % 8) * CH:(u % 8 + 1) * CH]
                                last = pair(out, Y[:, u, :], Wk[:, u, :]) if m == 0 else pair(out, Wk[:, u, :], Y[:, u, :])
                            last.then_inc(s["xy_done"], 1)
                pe.wait_ge(s["xy_ready"], 4 * LEVELS - 2)
                pe.wait_ge(s["state_zero"], 1)
                for c in range(NCH):
                    if c:
                        pe.wait_ge(s["state_ready"], c)
                        pe.wait_ge(s["y_copied"], c)
                    for i in range(FT):
                        u = c * FT + i
                        o = slice(i * CH, (i + 1) * CH)
                        pair(banks[0][:, o], fm(at, u), state[:, o], True, False)
                        last = pair(banks[0][:, o], KA[:, u, :], Vs[:, u, :], False, True)
                    last.then_inc(s["u0_done"], 1)
                    for i in range(FT):
                        u = c * FT + i
                        o = slice(i * CH, (i + 1) * CH)
                        pair(banks[5][:, o], state[:, o], fm(rt, u), i == 0, False)
                        pair(banks[5][:, o], Vs[:, u, :], RK[:, u, :], False, False)
                    pe.wait_ge(s["u0_ready"], c + 1)
                    for i in range(FT):
                        u = c * FT + i
                        o = slice(i * CH, (i + 1) * CH)
                        last = pair(banks[1][:, o], X[:, u, :], u0[:, o])
                    last.then_inc(s["u_done"], 1)
                    pe.wait_ge(s["u_ready"], c + 1)
                    if c < NCH - 1:
                        for i in range(FT):
                            u = c * FT + i
                            o = slice(i * CH, (i + 1) * CH)
                            pair(banks[4][:, o], Ks[:, u, :], Vs[:, u, :], True, False)
                            last = pair(banks[4][:, o], Bs[:, u, :], uu[:, o], False, True)
                        last.then_inc(s["state_done"], 1)
                    for i in range(FT):
                        u = c * FT + i
                        o = slice(i * CH, (i + 1) * CH)
                        last = pair(banks[5][:, o], uu[:, o], RB[:, u, :], False, True)
                    last.then_inc(s["y_done"], 1)
                pe.wait_ge(s["y_copied"], NCH)
                for b in range(2):
                    last = mm(banks[6 + b][:, :], head_ones, yT[:, 2 * b:2 * b + 2, :], True, True)
                last.then_inc(s["mean_done"], 1)
                pe.wait_ge(s["y_squared"], 1)
                for b in range(2):
                    last = mm(banks[4 + b][:, :], head_ones, ysq[:, 2 * b:2 * b + 2, :], True, True)
                last.then_inc(s["var_done"], 1)
                s5_out(2)
                bu(3)
                s5_out(3)
                pe.wait_ge(s["s5_gelu"], 1)
                pe.wait_ge(s["glu_in"], 16)
                for f in range(FT):
                    for k in range(FT):
                        last = mm(banks[f // 2][:, (f % 2) * T:(f % 2 + 1) * T], wglu[:, k, f * P:(f + 1) * P], ys5[:, k, :], k == 0, k == FT - 1)
                    if f % 2:
                        last.then_inc(s["glu_done"], 1)
                pe.wait_ge(wout_in, 64)
                pe.wait_ge(s["glu_sig"], 2)
                pe.wait_ge(s["mix_rw_ready"], 1)
                for t in range(TT):
                    for hf in range(2):
                        for n, k in enumerate((4, 5, 6, 7, 0, 1, 2, 3)):
                            if k < 4:
                                pe.wait_ge(s["mix_s5_ready"], 1 + k // 2)
                            src = mix_s5[:, k, t * P:(t + 1) * P] if k < FT else mix_rw[:, k - FT, t * P:(t + 1) * P]
                            last = mm(banks[2 * t + hf][:, :], src, wout[k // 2][:, k % 2, hf * 512:(hf + 1) * 512], n == 0, n == KD - 1)
                        last.then_inc(s["out_done"], 1)

        experts(nc, io, ctx, arena, con, par, banks, ring, chunk_in, chunk_src, x2)


def experts(nc, io, ctx, arena, con, par, banks, ring, chunk_in, chunk_src, x2):
    def sb(name, shape, dt=F32):
        return ctx.enter_context(nc.sbuf_tensor(name, shape, dt))

    def un(i, n=1):
        return arena[:, i * UNIT:(i + n) * UNIT]

    def prm(name):
        a, n = PARAMS[name]
        return par[:, a:a + n]

    ident = con[:, C_ID:C_ID + P]
    ones = con[:, C_ONES:C_ONES + P]
    tri = con[:, C_TRI:C_TRI + P]
    HF = D // 2

    xn = un(33, 2).rearrange("p (t d) -> p t d", d=D)
    xres = un(35, 2).rearrange("p (t d) -> p t d", d=D)
    parts = un(24, 3).bitcast(BF16).rearrange("p (t q d) -> p t q d", t=TT, q=3)
    hT = un(27, 2).rearrange("p (k t) -> p k t", k=KD)
    bias = un(37, 3).rearrange("p (m d) -> p m d", m=3)
    y = un(40)[:, 0:HF]
    xg = un(40)[:, HF:2 * HF].rearrange("p (k s) -> p k s", k=KD)
    gt = un(41)[:, 0:HF]
    up = un(41)[:, HF:2 * HF]
    sg = un(42)[:, 0:HF]
    actT = un(42)[:, HF:2 * HF].rearrange("p (h k s) -> p k h s", h=2, k=4)
    gT = un(43)[:, 0:TT * P].rearrange("p (t m) -> p t m", t=TT)
    pg = un(43)[:, 256:512].rearrange("p (t m) -> p t m", t=TT)
    onehot = un(43)[:, 512:576].bitcast(BF16).rearrange("p (t m) -> p t m", t=TT)
    pick = un(43)[:, 576:640]
    router = un(43)[:, 640:640 + KD * E].rearrange("p (k e) -> p k e", k=KD)
    rbias = un(43)[:, 896:896 + E]
    lg = un(44)[:, 0:64].rearrange("p (t e) -> p t e", t=TT)
    gates = un(44)[:, 64:128].rearrange("p (t e) -> p t e", t=TT)
    mask = un(44)[:, 128:192].rearrange("p (t e) -> p t e", t=TT)
    rank = un(44)[:, 192:256].rearrange("p (t e) -> p t e", t=TT)
    top = un(44)[:, 256:272].rearrange("p (t e) -> p t e", t=TT)
    topi = un(44)[:, 272:288].bitcast(U32).rearrange("p (t e) -> p t e", t=TT)
    topf = un(44)[:, 288:304].rearrange("p (t e) -> p t e", t=TT)
    ex = un(44)[:, 304:320].rearrange("p (t e) -> p t e", t=TT)
    st = un(44)[:, 320:352]
    hot = un(44)[:, 352:384]
    cnt = un(44)[:, 384:416]
    cflag = un(44)[:, 416:424]
    nexp = un(44)[:, 424:425].bitcast(I32)
    ssq = un(44)[:, 426:430]

    def sem(name):
        return ctx.enter_context(nc.semaphore(name))

    s = {n: sem("m_" + n) for n in (
        "router_in", "bias_in", "ssq", "root", "xn_ready", "turned", "h_ready", "logits_done", "top_ready", "exp_ready",
        "mask_ready", "rank_done", "count_ready", "dve", "swish_ready", "poolc", "up_read",
        "ranks_moved", "hot_ready", "gathered", "xg_ready", "gate_done", "up_done", "down_done", "chunks_used",
        "gt_ready", "sig_ready", "act_ready", "pg_ready", "gT_done", "gT_ready", "actT_done", "actT_ready",
        "y_ready", "scattered", "picked")}

    def mm(out, lhsT, rhs, start, stop):
        return nc.tensor.matmul(out, lhsT, rhs, start=start, stop=stop, skip_group_check=True)

    def chain(eng, name):
        n = [0]

        def link(ins):
            n[0] += 1
            ins.then_inc(s[name], 1)
            eng.wait_ge(s[name], n[0])
        return link

    with nc.Block() as block:
        @block.sync
        def _(sp):
            sp.dma_start(router[:, :, :], io["router_w"].rearrange("(k p) e -> p k e", p=P)).then_inc(s["router_in"], 16)
            sp.dma_start(rbias[0:1, :], io["router_b"]).then_inc(s["router_in"], 16)
            for m, b in enumerate(("exp_b_gate", "exp_b_up", "exp_b_down")):
                sp.dma_start(bias[0:E, m, :], io[b]).then_inc(s["bias_in"], 16)
            for c in range(4, NC):
                sp.dma_start(ring[c][:, :, :], chunk_src(c, 0)).then_inc(chunk_in[c], 16)

        @block.scalar
        def _(act):
            for t in range(TT):
                last = nc.scalar.activation(xn[:, t, :], x2[:, t, :], ACT.Square, accum_out=ssq[:, t:t + 1])
            last.then_inc(s["ssq"], 1)
            act.wait_ge(s["ssq"], 1)
            nc.scalar.activation(st[:, 0:2], ssq[:, 0:2], ACT.Sqrt, bias=par[:, NPARAM:NPARAM + 1], scale=1.0 / D).then_inc(s["root"], 1)
            for k in range(KD):
                act.wait_ge(s["turned"], k + 1)
                nc.scalar.activation(hT[:, k, :], banks[4 + k % 4][:, 0:T], ACT.Copy, scale=prm("g_moe")[:, k:k + 1]).then_inc(s["h_ready"], 1)
            act.wait_ge(s["top_ready"], 1)
            for t in range(TT):
                last = nc.scalar.activation(ex[:, t, 0:4], top[:, t, 0:4], ACT.Exp, bias=st[:, 2 + t:3 + t], accum_out=st[:, 4 + t:5 + t])
            last.then_inc(s["exp_ready"], 1)

        @block.vector
        def _(dve):
            link = chain(dve, "dve")
            V = nc.vector
            tt, ts, stt = V.tensor_tensor, V.tensor_scalar, V.scalar_tensor_tensor
            dve.wait_ge(s["root"], 1)
            link(V.reciprocal(st[:, 0:2], st[:, 0:2]))
            for t in range(TT):
                ts(xn[:, t, :], x2[:, t, :], st[:, t:t + 1], None, ALU.mult).then_inc(s["xn_ready"], 1)
            dve.wait_ge(s["xn_ready"], 2)
            for t in range(TT):
                V.memset(gT[:, t, :], 0.0)
                link(V.tensor_copy(parts[:, t, 0, :], xn[:, t, :]))
                link(tt(xres[:, t, :], xn[:, t, :], parts[:, t, 0, :], ALU.subtract))
                link(V.tensor_copy(parts[:, t, 1, :], xres[:, t, :]))
                link(tt(xres[:, t, :], xres[:, t, :], parts[:, t, 1, :], ALU.subtract))
                link(V.tensor_copy(parts[:, t, 2, :], xres[:, t, :]))
            V.memset(y, 0.0).then_inc(s["y_ready"], 1)
            for i, name in enumerate(("gT_ready", "actT_ready", "gT_done")):
                V.memset(st[:, 8 + i:9 + i], 0.0).then_inc(s[name], 1)
            for t in range(TT):
                dve.wait_ge(s["logits_done"], t + 1)
                link(V.tensor_copy(lg[:, t, :], banks[4 + t][:, 0:E]))
                link(V.max(top[:, t, :], lg[:, t, :]))
                link(V.max_index(topi[:, t, :], top[:, t, :], lg[:, t, :]))
                link(V.tensor_copy(topf[:, t, :], topi[:, t, :]))
                link(ts(st[:, 2 + t:3 + t], top[:, t, 0:1], -1.0, None, ALU.mult))
            V.memset(cflag[:, 4:8], 0.0).then_inc(s["top_ready"], 1)
            dve.wait_ge(s["exp_ready"], 1)
            link(V.reciprocal(st[:, 6:8], st[:, 4:6]))
            for t in range(TT):
                link(ts(ex[:, t, 0:4], ex[:, t, 0:4], st[:, 6 + t:7 + t], None, ALU.mult))
                link(V.memset(gates[:, t, :], 0.0))
                link(V.memset(mask[:, t, :], 0.0))
                for j in range(4):
                    link(ts(hot, con[:, C_E32:C_E32 + E], topf[:, t, j:j + 1], None, ALU.is_equal))
                    link(tt(mask[:, t, :], mask[:, t, :], hot, ALU.add))
                    link(stt(gates[:, t, :], hot, ex[:, t, j:j + 1], gates[:, t, :], ALU.mult, ALU.add))
            V.memset(cflag[:, 0:4], 0.0).then_inc(s["mask_ready"], 1)
            dve.wait_ge(s["rank_done"], 1)
            for t in range(TT):
                link(stt(rank[:, t, :], mask[:, t, :], -1000.0, banks[6][:, 32 * t:32 * t + 32], ALU.mult, ALU.add))
                link(ts(rank[:, t, :], rank[:, t, :], 1000.0, None, ALU.add))
            link(V.tensor_reduce(cnt[:, 0:1], banks[6][:, 64:96], AX.X, ALU.max))
            for n in range(1, MAX_PASS):
                link(ts(cflag[:, n:n + 1], cnt[:, 0:1], float(n * SLOTS), float(E), ALU.is_gt, ALU.mult))
            link(V.tensor_reduce(cnt[:, 1:2], cflag[:, 0:MAX_PASS], AX.X, ALU.add))
            ts(nexp[:, 0:1], cnt[:, 1:2], float(E), None, ALU.add).then_inc(s["count_ready"], 1)

        @block.tensor
        def _(pe):
            for t in range(TT):
                for hf in range(2):
                    mm(banks[2 * t + hf][:, :], ident, x2[:, t, hf * HF:(hf + 1) * HF], True, False)
            pe.wait_ge(s["xn_ready"], 2)
            for k in range(KD):
                if k >= 4:
                    pe.wait_ge(s["h_ready"], k - 3)
                for t in range(TT):
                    last = nc.tensor.transpose(banks[4 + k % 4][:, t * P:(t + 1) * P], xn[:, t, k * P:(k + 1) * P], ident)
                last.then_inc(s["turned"], 1)
            pe.wait_ge(s["router_in"], 32)
            pe.wait_ge(s["h_ready"], KD)
            for t in range(TT):
                for k in range(KD):
                    mm(banks[4 + t][:, 0:E], hT[:, k, t * P:(t + 1) * P], router[:, k, :], k == 0, False)
                mm(banks[4 + t][:, 0:E], ones[0:1, :], rbias[0:1, :], False, True).then_inc(s["logits_done"], 1)
            pe.wait_ge(s["mask_ready"], 1)
            mm(banks[6][:, 0:32], tri, mask[:, 0, :], True, True)
            mm(banks[6][:, 32:64], ones, mask[:, 0, :], True, False)
            mm(banks[6][:, 32:64], tri, mask[:, 1, :], False, True)
            mm(banks[6][:, 64:96], ones, mask[:, 0, :], True, False)
            mm(banks[6][:, 64:96], ones, mask[:, 1, :], False, True).then_inc(s["rank_done"], 1)

    GATE, UP, GAT, YB = banks[4], banks[5], banks[6], banks[7]
    wdone = sem("m_tail_in")

    def count(eng):
        return eng.value_load(nexp[0:1, 0:1], min_val=E, max_val=MAX_PASS * E)

    fin = un(33, 2).rearrange("p (t d) -> p t d", d=D)
    t2 = {n: sem("t_" + n) for n in (
        "w_in", "p_in", "fg_in", "sum", "sum2", "x3_ready", "ssq", "xn_ready", "turned", "h_ready", "proj_done", "gate_done",
        "sig_ready", "x4_ready", "ssq2", "out_ready", "out")}
    pT = un(29)[:, 0:TT * T].rearrange("p (k t) -> p k t", k=2)
    fg = un(45)

    with nc.Block() as block:
        @block.sync
        def _(sp):
            n_all = count(sp)
            sp.dma_start(pT[:, :, :], io["pT"].rearrange("(k p) t -> p k t", p=P)).then_inc(t2["p_in"], 16)
            sp.dma_start(fg[:, :], io["final_g"].to_broadcast([P, D])).then_inc(t2["fg_in"], 16)
            with sp.Fori(1, n_all) as n:
                e = sp.snap(n % E)
                for c in range(NC):
                    sp.wait_ge(s["chunks_used"], (n - 1) * NC + c + 1)
                    sp.dma_start(ring[c][:, :, :], chunk_src(c, e)).then_inc(chunk_in[c], 16)
            wg = io["ple_w_gate"].rearrange("(c k p) n -> c p k n", p=P, k=2)
            for c in range(5):
                sp.wait_ge(s["gate_done" if c < 4 else "up_done"], n_all)
                src = io["ple_w_proj"].rearrange("(k p) n -> p k n", p=P) if c == 0 else wg[c - 1]
                sp.dma_start(ring[c][:, :, :], src).then_inc(t2["w_in"], 16)

        @block.scalar
        def _(act):
            n_all = count(act)
            with act.Fori(0, n_all) as n:
                act.wait_ge(s["gt_ready"], n + 1)
                nc.scalar.activation(sg, gt, ACT.Sigmoid, scale=1.702).then_inc(s["sig_ready"], 1)
                act.wait_ge(s["gT_done"], n + 2)
                act.wait_ge(s["scattered"], n + 1)
                nc.scalar.activation(gT[:, :, :], YB[:, 0:TT * P].rearrange("p (t m) -> p t m", t=TT), ACT.Copy).then_inc(s["gT_ready"], 1)
                act.wait_ge(s["actT_done"], n + 1)
                nc.scalar.activation(actT[:, :, :, :], GATE[:, :].rearrange("p (k h s) -> p k h s", h=2, k=4), ACT.Copy).then_inc(s["actT_ready"], 1)

        @block.vector
        def _(dve):
            V = nc.vector
            tt, ts, stt = V.tensor_tensor, V.tensor_scalar, V.scalar_tensor_tensor
            n_all = count(dve)
            iota = con[:, C_IOTA:C_IOTA + P]

            def one_hot(e):
                for t in range(TT):
                    ts(onehot[:, t, :], iota[:, 0:SLOTS], rank[:, t, bass.ds(e, 1)], None, ALU.is_equal).then_inc(s["hot_ready"], 1)

            def gathered_times_gain():
                tt(xg[:, :, :], GAT[:, :].rearrange("p (k s) -> p k s", k=KD),
                   prm("g_moe")[:, :, None].to_broadcast([P, KD, SLOTS]), ALU.mult).then_inc(s["xg_ready"], 1)

            one_hot(0)
            dve.wait_ge(s["gathered"], 1)
            gathered_times_gain()
            with dve.Fori(0, n_all) as n:
                e = dve.snap(n % E)
                e_next = dve.snap((n + 1) % E)
                dve.wait_ge(s["gT_done"], n + 1)
                for t in range(TT):
                    ts(pg[:, t, :], iota, rank[:, t, bass.ds(e, 1)], gates[:, t, bass.ds(e, 1)], ALU.is_equal, ALU.mult).then_inc(s["pg_ready"], 1)
                V.tensor_copy(pick[0:E, :], ident[0:E, bass.ds(e, 1)].to_broadcast([E, SLOTS])).then_inc(s["picked"], 1)
                dve.wait_ge(s["pg_ready"], 2 * n + 2)
                for t in range(TT):
                    ts(rank[:, t, bass.ds(e, 1)], rank[:, t, bass.ds(e, 1)], -float(SLOTS), None, ALU.add).then_inc(s["ranks_moved"], 1)
                dve.wait_ge(s["ranks_moved"], 2 * n + 2)
                one_hot(e_next)
                dve.wait_ge(s["gate_done"], n + 1)
                ts(gt, GATE[:, :], 7.0, None, ALU.min).then_inc(s["gt_ready"], 1)
                dve.wait_ge(s["gt_ready"], n + 1)
                dve.wait_ge(s["sig_ready"], n + 1)
                tt(sg, sg, gt, ALU.mult).then_inc(s["swish_ready"], 1)
                dve.wait_ge(s["up_done"], n + 1)
                ts(up, UP[:, :], 7.0, -7.0, ALU.min, ALU.max).then_inc(s["up_read"], 1)
                dve.wait_ge(s["up_read"], n + 1)
                dve.wait_ge(s["swish_ready"], n + 1)
                stt(up, up, 1.0, sg, ALU.add, ALU.mult).then_inc(s["act_ready"], 1)
                dve.wait_ge(s["gathered"], n + 2)
                gathered_times_gain()
                dve.wait_ge(s["down_done"], n + 1)
                dve.wait_ge(s["scattered"], n + 1)
                V.tensor_copy(y, YB[:, :]).then_inc(s["y_ready"], 1)

        @block.tensor
        def _(pe):
            n_all = count(pe)

            def scatter():
                for t in range(TT):
                    for hf in range(2):
                        a = slice(hf * 64, hf * 64 + 64)
                        last = mm(banks[2 * t + hf][:, :], gT[a, t, :], y[a, :], False, True)
                return last

            def gather():
                for k in range(KD):
                    for i in range(3 * TT):
                        last = mm(GAT[:, k * SLOTS:(k + 1) * SLOTS], parts[:, i // 3, i % 3, k * P:(k + 1) * P], onehot[:, i // 3, :], i == 0, i == 3 * TT - 1)
                last.then_inc(s["gathered"], 1)

            pe.wait_ge(s["bias_in"], 48)
            pe.wait_ge(s["hot_ready"], 2)
            gather()
            with pe.Fori(0, n_all) as n:
                pe.wait_ge(s["xg_ready"], n + 1)
                pe.wait_ge(s["actT_ready"], n + 1)
                for m, (bank, done) in enumerate(((GATE, "gate_done"), (UP, "up_done"))):
                    for k in range(KD):
                        c = 4 * m + k // 2
                        if k % 2 == 0:
                            pe.wait_ge(chunk_in[c], 16 * n + 16)
                        for hf in range(2):
                            last = mm(bank[hf * 64:hf * 64 + 64, :], xg[:, k, :], ring[c][:, k % 2, hf * HF:(hf + 1) * HF], k == 0, False)
                        if k % 2:
                            last.then_inc(s["chunks_used"], 1)
                    pe.wait_ge(s["picked"], n + 1)
                    for hf in range(2):
                        last = mm(bank[hf * 64:hf * 64 + 64, :], pick[0:E, :], bias[0:E, m, hf * HF:(hf + 1) * HF], False, True)
                    last.then_inc(s[done], 1)
                pe.wait_ge(s["gT_ready"], n + 1)
                pe.wait_ge(s["y_ready"], n + 1)
                scatter().then_inc(s["scattered"], 1)
                pe.wait_ge(s["pg_ready"], 2 * n + 2)
                for t in range(TT):
                    last = nc.tensor.transpose(YB[:, t * P:(t + 1) * P], pg[:, t, :], ident)
                last.then_inc(s["gT_done"], 1)
                pe.wait_ge(s["act_ready"], n + 1)
                for k in range(4):
                    last = nc.tensor.transpose(GATE[:, k * P:(k + 1) * P], up[:, k * P:(k + 1) * P], ident)
                last.then_inc(s["actT_done"], 1)
                pe.wait_ge(s["hot_ready"], 2 * n + 4)
                gather()
                pe.wait_ge(s["actT_ready"], n + 2)
                pe.wait_ge(s["gT_ready"], n + 2)
                for k in range(KD):
                    c = 8 + k // 2
                    if k % 2 == 0:
                        pe.wait_ge(chunk_in[c], 16 * n + 16)
                    for hf in range(2):
                        last = mm(YB[hf * 64:hf * 64 + 64, :], actT[:, k % 4, k // 4, :], ring[c][:, k % 2, hf * HF:(hf + 1) * HF], k == 0, False)
                    if k % 2:
                        last.then_inc(s["chunks_used"], 1)
                for hf in range(2):
                    last = mm(YB[hf * 64:hf * 64 + 64, :], pick[0:E, :], bias[0:E, 2, hf * HF:(hf + 1) * HF], False, True)
                last.then_inc(s["down_done"], 1)
            pe.wait_ge(s["gT_ready"], n_all + 1)
            pe.wait_ge(s["y_ready"], n_all + 1)
            scatter().then_inc(wdone, 1)

    hT2 = un(24, 2).rearrange("p (k t) -> p k t", k=KD)
    xn2 = un(31, 2).rearrange("p (t d) -> p t d", d=D)
    sig = un(35, 2).rearrange("p (t d) -> p t d", d=D)
    scr = un(41, 2).rearrange("p (t d) -> p t d", d=D)
    st2 = un(44)[:, 0:16]
    with nc.Block() as block:
        @block.vector
        def _(dve):
            link = chain(dve, "poolc")
            V = nc.vector
            tt, ts, stt = V.tensor_tensor, V.tensor_scalar, V.scalar_tensor_tensor
            for t in range(TT):
                for hf in range(2):
                    last = V.tensor_copy(fin[:, t, hf * HF:(hf + 1) * HF], banks[2 * t + hf][:, :])
                last.then_inc(t2["x3_ready"], 1)
            for t in range(TT):
                dve.wait_ge(t2["ssq"], t + 1)
                link(V.reciprocal(st2[:, 2 + t:3 + t], st2[:, t:t + 1]))
                ts(xn2[:, t, :], fin[:, t, :], st2[:, 2 + t:3 + t], None, ALU.mult).then_inc(t2["xn_ready"], 1)
            for n in range(4):
                t, hf = n // 2, n % 2
                o = slice(hf * HF, (hf + 1) * HF)
                dve.wait_ge(t2["sig_ready"], n + 1)
                dve.wait_ge(t2["proj_done"], n + 1)
                link(tt(sig[:, t, o], sig[:, t, o], banks[n][:, :], ALU.mult))
                tt(fin[:, t, o], fin[:, t, o], sig[:, t, o], ALU.add).then_inc(t2["x4_ready"], 1)
            for t in range(TT):
                dve.wait_ge(t2["ssq2"], t + 1)
                link(V.reciprocal(st2[:, 6 + t:7 + t], st2[:, 4 + t:5 + t]))
                dve.wait_ge(t2["fg_in"], 16)
                stt(fin[:, t, :], fin[:, t, :], st2[:, 6 + t:7 + t], fg[:, :], ALU.mult, ALU.mult).then_inc(t2["out_ready"], 1)

        @block.scalar
        def _(act):
            for t in range(TT):
                act.wait_ge(t2["x3_ready"], t + 1)
                nc.scalar.activation(scr[:, t, :], fin[:, t, :], ACT.Square, accum_out=st2[:, 8 + t:9 + t]).then_inc(t2["sum"], 1)
                act.wait_ge(t2["sum"], t + 1)
                nc.scalar.activation(st2[:, t:t + 1], st2[:, 8 + t:9 + t], ACT.Sqrt, bias=par[:, NPARAM:NPARAM + 1], scale=1.0 / D).then_inc(t2["ssq"], 1)
            for k in range(KD):
                act.wait_ge(t2["turned"], k + 1)
                nc.scalar.activation(hT2[:, k, :], banks[4 + k % 4][:, 0:T], ACT.Copy, scale=prm("g_ple")[:, k:k + 1]).then_inc(t2["h_ready"], 1)
            for n in range(4):
                t, hf = n // 2, n % 2
                act.wait_ge(t2["gate_done"], n + 1)
                nc.scalar.activation(sig[:, t, hf * HF:(hf + 1) * HF], banks[4 + n][:, :], ACT.Sigmoid).then_inc(t2["sig_ready"], 1)
            act.wait_ge(t2["ssq"], 2)
            for t in range(TT):
                act.wait_ge(t2["x4_ready"], 2 * t + 2)
                nc.scalar.activation(scr[:, t, :], fin[:, t, :], ACT.Square, accum_out=st2[:, 10 + t:11 + t]).then_inc(t2["sum2"], 1)
                act.wait_ge(t2["sum2"], t + 1)
                nc.scalar.activation(st2[:, 4 + t:5 + t], st2[:, 10 + t:11 + t], ACT.Sqrt, bias=par[:, NPARAM:NPARAM + 1], scale=1.0 / D).then_inc(t2["ssq2"], 1)

        @block.tensor
        def _(pe):
            pe.wait_ge(t2["x3_ready"], 2)
            pe.wait_ge(t2["w_in"], 80)
            pe.wait_ge(t2["p_in"], 16)
            for n in range(4):
                t, hf = n // 2, n % 2
                for k in range(2):
                    last = mm(banks[n][:, :], pT[:, k, t * P:(t + 1) * P], ring[0][:, k, hf * HF:(hf + 1) * HF], k == 0, k == 1)
                last.then_inc(t2["proj_done"], 1)
            pe.wait_ge(t2["xn_ready"], 2)
            for k in range(KD):
                if k >= 4:
                    pe.wait_ge(t2["h_ready"], k - 3)
                for t in range(TT):
                    last = nc.tensor.transpose(banks[4 + k % 4][:, t * P:(t + 1) * P], xn2[:, t, k * P:(k + 1) * P], ident)
                last.then_inc(t2["turned"], 1)
            pe.wait_ge(t2["h_ready"], KD)
            for n in range(4):
                t, hf = n // 2, n % 2
                for k in range(KD):
                    last = mm(banks[4 + n][:, :], hT2[:, k, t * P:(t + 1) * P], ring[1 + k // 2][:, k % 2, hf * HF:(hf + 1) * HF], k == 0, k == KD - 1)
                last.then_inc(t2["gate_done"], 1)

        @block.sync
        def _(sp):
            o = io["out"].rearrange("(t p) d -> p t d", p=P)
            for t in range(TT):
                sp.wait_ge(t2["out_ready"], t + 1)
                sp.dma_start(o[:, t, :], fin[:, t, :]).then_inc(t2["out"], 16)
            sp.wait_ge(t2["out"], 16 * TT)


def columns(v):
    return np.ascontiguousarray(np.asarray(v).reshape(-1, P).T)


def lay_out(a):
    f = {k: np.asarray(v) for k, v in a.items()}
    o = {}
    x = f["x"].reshape(T, D)
    o["x"] = x
    o["xT"] = np.ascontiguousarray(x.T)
    o["pT"] = np.ascontiguousarray(f["p"].reshape(T, -1).T)
    o["consts"] = constants()
    dt = np.repeat(f["s5_log_dt"].reshape(NJ, 2), CH, axis=1)
    mw, mr = f["rwkv_mu_wag"][0], f["rwkv_mu_rkv"][0]
    cols = dict(g_mix=f["norm_mix_g"], mu_w=mw[0], mu_a=mw[1], mu_g=mw[2], mu_r=mr[0], mu_k=mr[1], mu_v=mr[2],
                w0=f["rwkv_w0"], a0=f["rwkv_a0"], k_k=f["rwkv_k_k"], k_a=f["rwkv_k_a"], r_k=f["rwkv_r_k"],
                ln_w=f["rwkv_ln_w"], ln_b=f["rwkv_ln_b"], s5_d=f["s5_d"], g_moe=f["norm_moe_g"],
                g_ple=f["norm_ple_g"], lam_re=f["s5_lam_re"], lam_im=f["s5_lam_im"], log_dt=dt)
    o["params"] = np.concatenate([columns(cols[n]) for n in PARAMS], axis=1)
    for n in ("re", "im"):
        b = f["s5_b_" + n].reshape(NJ, 2, CH, 16)
        bd = np.zeros((2, CH, NJ, 2, 16), np.float32)
        c = f["s5_c_" + n].reshape(NJ, 2, 16, CH)
        cd = np.zeros((2, CH, NJ, 2, 16), np.float32)
        for g in range(2):
            bd[g, :, :, g, :] = b[:, g].transpose(1, 0, 2)
            cd[g, :, :, g, :] = c[:, g].transpose(2, 0, 1)
        o["s5_b_" + n] = bd.reshape(P, NJ * 32)
        o["s5_c_" + n] = cd.reshape(P, NJ * 32)
    o["w_in"] = f["w_in"][0]
    o["lora1"] = np.concatenate([f["rwkv_w1"][0], f["rwkv_a1"][0], f["rwkv_g1"][0]], axis=1)
    o["lora2"] = np.concatenate([np.concatenate([f["rwkv_w2"][0], f["rwkv_a2"][0]], axis=0), f["rwkv_g2"][0]], axis=1)
    o["w_glu"] = f["s5_w_glu"][0]
    o["w_out"] = f["w_out"][0]
    o["router_w"] = f["router_w"][0]
    o["router_b"] = f["router_b"].reshape(1, E)
    for n in ("exp_w_gate", "exp_w_up", "exp_w_down", "exp_b_gate", "exp_b_up", "exp_b_down", "ple_w_proj", "ple_w_gate"):
        o[n] = f[n][0]
    o["final_g"] = f["final_norm_g"].reshape(1, D)
    return o


def kernel(**inputs):
    import concourse.bacc as bacc
    from concourse.bass_utils import run_bass_kernel_spmd

    nc = bacc.Bacc("TRN2", target_bir_lowering=False, num_devices=1)
    arrays, io = {}, {}
    for name, a in lay_out(inputs).items():
        a = np.ascontiguousarray(a)
        arrays["in_" + name] = a
        io[name] = nc.dram_tensor("in_" + name, a.shape, mybir.dt.from_np(a.dtype), kind="ExternalInput").ap()
    io["out"] = nc.dram_tensor("out_0", (T, D), F32, kind="ExternalOutput").ap()
    layer(nc, io)
    got = run_bass_kernel_spmd(nc, [arrays], core_ids=[0])
    return got.results[0]["out_0"].reshape(1, T, D)
```

```python
from contextlib import ExitStack

import numpy as np
import concourse.bass as bass
from concourse import mybir

P = 128
T = 256
D = 1024
KD = D // P
W = 512
FT = W // P
TT = T // P
CH = 64
NCH = T // CH
UNITS = NCH * FT
NJ = 16
E = 32
TOPK = 4
SLOTS = 64
MAX_PASS = T // SLOTS
NC = 12
UNIT = 1024
ARENA = 46

F32 = mybir.dt.float32
BF16 = mybir.dt.bfloat16
I32 = mybir.dt.int32
U32 = mybir.dt.uint32
ALU = mybir.AluOpType
ACT = mybir.ActivationFunctionType
AX = mybir.AxisListType

INV_2PI = float(1.0 / (2.0 * np.pi))
ROUND = float(1.5 * 2 ** 23)
PI_A, PI_B = 6.28125, float(2 * np.pi - 6.28125)
PI = 3.1415925
DECAY = float(np.exp(-0.5))

C_ID, C_ONES, C_TRI, C_HEAD, C_IOTA = 0, 128, 256, 384, 512
C_ID2, C_SU, C_UI, C_SL1, C_SU1 = 640, 704, 768, 832, 896
C_LEV = 960
LEVELS = 5
C_TIME = C_LEV + 64 * LEVELS
C_E32 = C_TIME + T
NCONST = C_E32 + E
PARAMS = {}
for _n, _c in (("g_mix", KD), ("mu_w", KD), ("mu_a", KD), ("mu_g", KD), ("mu_r", FT), ("mu_k", FT),
               ("mu_v", FT), ("w0", FT), ("a0", FT), ("k_k", FT), ("k_a", FT), ("r_k", FT),
               ("ln_w", FT), ("ln_b", FT), ("s5_d", FT), ("g_moe", KD), ("g_ple", KD),
               ("lam_re", NJ), ("lam_im", NJ), ("log_dt", NJ)):
    PARAMS[_n] = (sum(c for _, c in PARAMS.values()), _c)
NPARAM = sum(c for _, c in PARAMS.values())


def constants():
    p = np.arange(P)
    c = np.zeros((P, NCONST), np.float32)
    c[:, C_ID:C_ID + P] = np.eye(P)
    c[:, C_ONES:C_ONES + P] = 1.0
    c[:, C_TRI:C_TRI + P] = p[:, None] < p[None, :]
    c[:, C_HEAD:C_HEAD + P] = p[:, None] // CH == p[None, :] // CH
    c[:, C_IOTA:C_IOTA + P] = np.arange(P) % SLOTS
    s, t = p[:, None] % CH, np.arange(CH)[None, :]
    c[:, C_ID2:C_ID2 + CH] = s == t
    c[:, C_SU:C_SU + CH] = s < t
    c[:, C_UI:C_UI + CH] = s <= t
    c[:, C_SU1:C_SU1 + CH] = (s < t) & (s // 2 == t // 2)
    c[:, C_SL1:C_SL1 + CH] = (s > t) & (s // 2 == t // 2)
    for n in range(LEVELS):
        b = 2 << n
        c[:, C_LEV + n * CH:C_LEV + (n + 1) * CH] = (s // (2 * b) == t // (2 * b)) & (s // b > t // b)
    c[:, C_TIME:C_TIME + T] = np.arange(T)
    c[:, C_E32:C_E32 + E] = np.arange(E)
    return c


def layer(nc, io):
    with ExitStack() as ctx:
        def sb(name, shape, dt=F32):
            return ctx.enter_context(nc.sbuf_tensor(name, shape, dt))

        def sem(name):
            return ctx.enter_context(nc.semaphore(name))

        arena = sb("arena", [P, ARENA * UNIT])
        con = sb("con", [P, NCONST])
        par = sb("par", [P, NPARAM + 2])
        lora_hidden = sb("lora_hidden", [P, 2 * T])
        bb = sb("bb", [P, 2, NJ * 32])
        cc = sb("cc", [P, 2, NJ * 32])
        s5p = sb("s5p", [P, 20, NJ])
        small = sb("small", [P, 64])
        chunk_decay = sb("chunk_decay", [P, FT, NCH])
        u0 = sb("u0", [P, FT * CH])
        uu = sb("uu", [P, FT * CH])
        state = sb("state", [P, FT * CH])
        banks = [ctx.enter_context(nc.psum_tensor(f"bank{i}", [P, 512], F32)) for i in range(8)]

        def un(i, n=1):
            return arena[:, i * UNIT:(i + n) * UNIT]

        def feat(i, n=1):
            return un(i, n).rearrange("p (f t) -> p f t", t=T)

        def units(i):
            return un(i).rearrange("p (u t) -> p u t", t=CH)

        def prm(name):
            a, n = PARAMS[name]
            return par[:, a:a + n]

        ident = con[:, C_ID:C_ID + P]
        ones = con[:, C_ONES:C_ONES + P]
        head_ones = con[:, C_HEAD:C_HEAD + P]

        xT, sq, hT, dh = feat(31, 2), feat(33, 2), feat(35, 2), feat(33, 2)
        xw, xa, xg = feat(37, 2), feat(39, 2), feat(41, 2)
        lora1 = un(26, 2).rearrange("p (k f) -> p k f", k=KD)
        lora2 = un(28)
        wglu = un(29, 2).rearrange("p (k f) -> p k f", k=FT)
        uT = feat(24)
        raw = {"k": feat(43), "r": feat(44), "v": feat(45)}
        S5C, S5S = [feat(16), feat(18)], [feat(17), feat(19)]
        sA, sB, sT1, sT2 = ([feat(a), feat(b)] for a, b in ((20, 8), (21, 9), (22, 10), (23, 11)))
        lw, la, lg = feat(31), feat(32), feat(33)
        tmp = feat(34)
        rr, kx, vv = feat(37), feat(38), feat(39)
        kkn, k2, kb, bonus = feat(40), feat(41), feat(42), feat(43)
        Lc, EL = feat(0), feat(1)
        kksq, rk = feat(2), feat(3)
        at, bh, kh, rt = feat(31), feat(42), feat(5), feat(37)
        Vs, Bs, Ks = units(32), units(4), units(35)
        X, Y, Wk, Mx, MO = units(36), units(38), units(40), units(44), units(45)
        KA, RB, RK = units(26), units(27), units(28)
        yT = feat(45)
        yc, ysq, yrs = feat(44), feat(38), feat(40)
        ys5 = feat(25)
        mix_s5, mix_rw = feat(24), feat(35)
        x_tok = un(31, 2).rearrange("p (t d) -> p t d", d=D)
        x2 = x_tok
        wout = [un(8 + 2 * c, 2).rearrange("p (k n) -> p k n", n=D) for c in range(4)]
        ring = [un(2 * c, 2).rearrange("p (k n) -> p k n", n=D) for c in range(NC)]
        win = [un(2 * c, 2).rearrange("p (k n) -> p k n", n=T) for c in range(8)]

        ssq = small[:, 0:TT]

        s = {n: sem(n) for n in (
            "consts_in", "s5_in", "xT_in", "lora_in", "lora2_in", "glu_in", "x_in",
            "eps_ready", "sq_ready", "rms_summed", "rms_root", "kk_root", "var_root", "h_ready", "mixed", "proj_done", "proj_copied",
            "lora1_done", "lora_hidden_ready", "lora2_done", "lora2_copied",
            "s5_dt", "s5_arg", "s5_mag", "s5_theta", "s5_sin", "bb_ready", "bb_turned", "bb_copied",
            "table_arg", "table_angle", "table_sin", "table_ready", "bu_done", "bu_copied", "phase_off",
            "scanned", "phase_on", "s5_out_done", "s5_y", "s5_gelu", "glu_done", "glu_sig", "mix_s5_ready",
            "kk_ready", "kk_squared", "kk_summed", "decay_ready", "exp_ready", "scaled", "rk_ready",
            "rk_summed", "bonus_ready", "scores_done", "scores_copied", "turned", "y_turned",
            "w_done", "w_copied", "xy_done", "xy_ready", "mo_ready", "state_zero",
            "u0_done", "u0_ready", "u_done", "u_ready", "state_done", "state_ready", "y_done", "y_copied",
            "mean_done", "centred", "y_squared", "var_done", "mix_rw_ready",
            "out_done", "x2_ready", "dve_chain", "act_chain", "pool_chain")}
        win_in = [sem("win_in_u0"), sem("win_in_u1")] + [x for n in "rkv" for x in [sem("win_in_" + n)] * 2]
        wout_in = sem("wout_in")
        p_in = sem("p_in")
        chunk_in = [sem(f"chunk_in{c}") for c in range(NC)]

        def chain(eng, name):
            n = [0]

            def link(ins):
                n[0] += 1
                ins.then_inc(s[name], 1)
                eng.wait_ge(s[name], n[0])
            return link

        def mm(out, lhsT, rhs, start, stop):
            return nc.tensor.matmul(out, lhsT, rhs, start=start, stop=stop, skip_group_check=True)

        def pair(out, lhsT, rhs, start=True, stop=True):
            for h in range(2):
                a = slice(h * CH, (h + 1) * CH)
                last = mm(out[a], lhsT[a], rhs[a], start, stop)
            return last

        SCORE_BANK = (4, 6, 0, 4, 6)
        order = [0, 1, 4, 5, 2, 3, 6, 7]
        expert_weights = [io["exp_w_gate"], io["exp_w_up"], io["exp_w_down"]]

        def chunk_src(c, e):
            w = expert_weights[c // 4]
            k = 2 * (c % 4)
            return w[bass.ds(e, 1), k * P:(k + 2) * P, :].rearrange("o (k p) n -> p (o k) n", p=P)

        with nc.Block() as block:
            @block.sync
            def _(sp):
                sp.dma_start(xT[:, :, :], io["xT"].rearrange("(k p) t -> p k t", p=P)).then_inc(s["xT_in"], 16)
                sp.dma_start(con[:, :], io["consts"]).then_inc(s["consts_in"], 16)
                sp.dma_start(par[:, 0:NPARAM], io["params"]).then_inc(s["consts_in"], 16)
                w = io["w_in"].rearrange("(k p) n -> p k n", p=P)
                for n, q in enumerate(order):
                    sp.dma_start(win[q][:, :, :], w[:, :, q * T:(q + 1) * T]).then_inc(win_in[q], 16)
                    if n == 1:
                        sp.dma_start(lora1[:, :, :], io["lora1"].rearrange("(k p) n -> p k n", p=P)).then_inc(s["lora_in"], 16)
                        sp.dma_start(lora2[:, :], io["lora2"]).then_inc(s["lora2_in"], 16)
                sp.dma_start(wglu[:, :, :], io["w_glu"].rearrange("(k p) n -> p k n", p=P)).then_inc(s["glu_in"], 16)
                sp.wait_ge(s["proj_done"], 8)
                wo = io["w_out"].rearrange("(c k p) n -> c p k n", p=P, k=2)
                for c in (2, 3):
                    sp.dma_start(wout[c][:, :, :], wo[c]).then_inc(wout_in, 16)
                sp.dma_start(ring[3][:, :, :], chunk_src(3, 0)).then_inc(chunk_in[3], 16)
                sp.wait_ge(s["scaled"], 3)
                sp.dma_start(ring[0][:, :, :], chunk_src(0, 0)).then_inc(chunk_in[0], 16)
                sp.wait_ge(s["rk_summed"], 1)
                sp.dma_start(ring[1][:, :, :], chunk_src(1, 0)).then_inc(chunk_in[1], 16)
                sp.wait_ge(s["phase_on"], 4)
                sp.wait_ge(s["s5_out_done"], 4)
                for c in (0, 1):
                    sp.dma_start(wout[c][:, :, :], wo[c]).then_inc(wout_in, 16)
                for c in range(8, NC):
                    sp.dma_start(ring[c][:, :, :], chunk_src(c, 0)).then_inc(chunk_in[c], 16)
                sp.wait_ge(s["turned"], 1)
                sp.dma_start(un(41, 2).rearrange("p (k n) -> p k n", n=D), io["ple_w_proj"].rearrange("(k p) n -> p k n", p=P)).then_inc(p_in, 16)
                sp.wait_ge(s["glu_done"], 2)
                sp.dma_start(un(30)[:, 0:TT * T].rearrange("p (k t) -> p k t", k=2), io["pT"].rearrange("(k p) t -> p k t", p=P)).then_inc(p_in, 16)
                sp.wait_ge(s["u0_done"], NCH)
                sp.wait_ge(s["y_done"], NCH)
                sp.wait_ge(s["state_done"], NCH - 1)
                sp.dma_start(x_tok[:, :, :], io["x"].rearrange("(t p) d -> p t d", p=P)).then_inc(s["x_in"], 16)
                sp.dma_start(ring[2][:, :, :], chunk_src(2, 0)).then_inc(chunk_in[2], 16)

            @block.gpsimd
            def _(pool):
                link = chain(pool, "pool_chain")
                pool.dma_start(bb[:, 0, :], io["s5_b_re"]).then_inc(s["s5_in"], 16)
                pool.dma_start(bb[:, 1, :], io["s5_b_im"]).then_inc(s["s5_in"], 16)
                pool.dma_start(cc[:, 0, :], io["s5_c_re"]).then_inc(s["s5_in"], 16)
                pool.dma_start(cc[:, 1, :], io["s5_c_im"]).then_inc(s["s5_in"], 16)
                tt = nc.gpsimd.tensor_tensor

                def phase_off(g):
                    c, sn, a, b, t1, t2 = (x[g % 2] for x in (S5C, S5S, sA, sB, sT1, sT2))
                    pool.wait_ge(s["bu_copied"], 4 * (g + 1))
                    pool.wait_ge(s["table_ready"], g + 1)
                    if g >= 2:
                        pool.wait_ge(s["s5_out_done"], g - 1)
                    tt(t1, a, c, ALU.mult)
                    link(tt(t2, b, sn, ALU.mult))
                    link(tt(t1, t1, t2, ALU.add))
                    link(tt(t2, a, sn, ALU.mult))
                    link(tt(a, b, c, ALU.mult))
                    tt(t2, a, t2, ALU.subtract).then_inc(s["phase_off"], 1)

                def phase_on(g):
                    c, sn, a, b, t1, t2 = (x[g % 2] for x in (S5C, S5S, sA, sB, sT1, sT2))
                    pool.wait_ge(s["scanned"], g + 1)
                    tt(t1, a, c, ALU.mult)
                    link(tt(t2, b, sn, ALU.mult))
                    link(tt(t1, t1, t2, ALU.subtract))
                    link(tt(t2, a, sn, ALU.mult))
                    link(tt(a, b, c, ALU.mult))
                    tt(t2, a, t2, ALU.add).then_inc(s["phase_on"], 1)

                for g in (0, 2):
                    phase_off(g)
                    phase_off(g + 1)
                    phase_on(g)
                    phase_on(g + 1)

            @block.scalar
            def _(act):
                link = chain(act, "act_chain")
                A = nc.scalar.activation
                act.wait_ge(s["xT_in"], 16)
                A(sq[:, :, :], xT[:, :, :], ACT.Square).then_inc(s["sq_ready"], 1)
                act.wait_ge(s["consts_in"], 32)
                A(s5p[:, 0, :], prm("log_dt"), ACT.Exp).then_inc(s["s5_dt"], 1)
                act.wait_ge(s["s5_arg"], 1)
                A(s5p[:, 4, :], s5p[:, 2, :], ACT.Exp).then_inc(s["s5_mag"], 1)
                act.wait_ge(s["s5_theta"], 1)
                A(s5p[:, 7, :], s5p[:, 5, :], ACT.Sin)
                A(s5p[:, 8, :], s5p[:, 5, :], ACT.Sin, scale=0.5).then_inc(s["s5_sin"], 1)
                act.wait_ge(s["rms_summed"], 1)
                act.wait_ge(s["eps_ready"], 1)
                A(un(43)[:, 0:T], banks[7][:, 0:T], ACT.Sqrt, bias=par[:, NPARAM:NPARAM + 1], scale=1.0 / D).then_inc(s["rms_root"], 1)
                act.wait_ge(s["s5_in"], 64)
                A(cc[:, 1, :], cc[:, 1, :], ACT.Copy, scale=-1.0).then_inc(s["bb_copied"], 1)

                def copy_proj(n):
                    q = order[n]
                    act.wait_ge(s["proj_done"], n + 1)
                    if q < 2:
                        dst = uT[:, 2 * q:2 * q + 2, :]
                    else:
                        dst = raw["rkv"[(q - 2) // 2]][:, 2 * (q % 2):2 * (q % 2) + 2, :]
                    A(dst, banks[n % 2][:, :].rearrange("p (f t) -> p f t", t=T), ACT.Copy).then_inc(s["proj_copied"], 1)

                def table_angle(g):
                    if g >= 2:
                        act.wait_ge(s["phase_on"], g - 1)
                    for j in range(4):
                        last = A(S5S[g % 2][:, j, :], con[:, C_TIME:C_TIME + T], ACT.Copy, scale=s5p[:, 5, 4 * g + j:4 * g + j + 1])
                    last.then_inc(s["table_angle"], 1)

                def table_sin(g):
                    act.wait_ge(s["table_arg"], g + 1)
                    A(S5C[g % 2][:, :, :], S5S[g % 2][:, :, :], ACT.Sin, scale=0.5)
                    A(S5S[g % 2][:, :, :], S5S[g % 2][:, :, :], ACT.Sin).then_inc(s["table_sin"], 1)

                def bu_copy(g):
                    for j in range(4):
                        act.wait_ge(s["bu_done"], 4 * g + j + 1)
                        if g >= 2 and j == 0:
                            act.wait_ge(s["phase_on"], g - 1)
                        A(sA[g % 2][:, j, :], banks[2 + j % 2][:, 0:T], ACT.Copy)
                        A(sB[g % 2][:, j, :], banks[2 + j % 2][:, T:2 * T], ACT.Copy).then_inc(s["bu_copied"], 1)

                table_angle(0)
                table_angle(1)
                for n in range(2):
                    copy_proj(n)
                act.wait_ge(s["lora1_done"], 2)
                A(lora_hidden[0:CH, 0:T], banks[4][0:CH, 0:T], ACT.Tanh)
                A(lora_hidden[CH:P, 0:T], banks[4][CH:P, 0:T], ACT.Copy).then_inc(s["lora_hidden_ready"], 1)
                act.wait_ge(s["lora1_done"], 3)
                A(lora_hidden[:, T:2 * T], banks[3][:, 0:T], ACT.Sigmoid).then_inc(s["lora_hidden_ready"], 1)
                table_sin(0)
                act.wait_ge(s["bb_turned"], 1)
                A(bb[:, 0, :], banks[5][:, :], ACT.Copy)
                A(bb[:, 1, :], banks[6][:, :], ACT.Copy).then_inc(s["bb_copied"], 1)
                bu_copy(0)
                table_sin(1)
                for m, (dst, bias) in enumerate(((lw, "w0"), (la, "a0"), (lg, None))):
                    if m == 0:
                        act.wait_ge(s["h_ready"], 1)
                    if m == 2:
                        act.wait_ge(s["mixed"], 3)
                    for i in range(FT):
                        if i % 2 == 0:
                            act.wait_ge(s["lora2_done"], 2 * m + i // 2 + 1)
                        src = banks[5 + i // 2][:, (i % 2) * T:(i % 2 + 1) * T]
                        if bias:
                            last = A(dst[:, i, :], src, ACT.Sigmoid, bias=prm(bias)[:, i:i + 1])
                        else:
                            last = A(dst[:, i, :], src, ACT.Copy)
                        if i % 2:
                            last.then_inc(s["lora2_copied"], 1)
                act.wait_ge(s["lora1_done"], 3)
                copy_proj(2)
                act.wait_ge(s["decay_ready"], 1)
                A(EL[:, :, :], Lc[:, :, :], ACT.Exp)
                link(A(chunk_decay[:, :, :], Lc[:, :, CH - 1::CH], ACT.Exp))
                A(Lc[:, :, :], Lc[:, :, :], ACT.Exp, scale=-1.0)
                A(lw[:, :, :], lw[:, :, :], ACT.Exp).then_inc(s["exp_ready"], 1)
                copy_proj(3)
                bu_copy(1)
                act.wait_ge(s["kk_ready"], 1)
                A(kksq[:, :, :], kkn[:, :, :], ACT.Square).then_inc(s["kk_squared"], 1)
                copy_proj(4)
                act.wait_ge(s["kk_summed"], 1)
                for b in range(2):
                    m = A(kb[:, 2 * b:2 * b + 2, :], banks[4 + b].rearrange("p (f t) -> p f t", t=T), ACT.Sqrt)
                m.then_inc(s["kk_root"], 1)
                copy_proj(5)
                table_angle(2)
                copy_proj(6)
                copy_proj(7)
                bu_copy(2)
                table_sin(2)
                table_angle(3)
                table_sin(3)
                bu_copy(3)
                for lev in range(LEVELS):
                    for b in range(2):
                        act.wait_ge(s["w_done"], 2 * lev + b + 1)
                        A(Wk[:, 8 * b:8 * b + 8, :], banks[4 + b].rearrange("p (u t) -> p u t", t=CH), ACT.Copy).then_inc(s["w_copied"], 1)
                act.wait_ge(s["s5_y"], 4)
                A(ys5[:, :, :], ys5[:, :, :], ACT.Gelu_apprx_tanh).then_inc(s["s5_gelu"], 1)
                for c in range(NCH):
                    act.wait_ge(s["u0_done"], c + 1)
                    A(u0[:, :], banks[0][:, 0:FT * CH], ACT.Copy).then_inc(s["u0_ready"], 1)
                    if c == 3:
                        act.wait_ge(s["centred"], 1)
                        A(ysq[:, :, 0:P], yc[:, :, 0:P], ACT.Square).then_inc(s["y_squared"], 1)
                    act.wait_ge(s["u_done"], c + 1)
                    A(uu[:, :], banks[1][:, 0:FT * CH], ACT.Copy).then_inc(s["u_ready"], 1)
                    act.wait_ge(s["y_done"], c + 1)
                    if c == 0:
                        act.wait_ge(s["w_done"], 2 * LEVELS)
                    A(yT[:, :, c * CH:(c + 1) * CH], banks[5][:, 0:FT * CH].rearrange("p (f t) -> p f t", t=CH), ACT.Copy).then_inc(s["y_copied"], 1)
                    if c % 2:
                        b = c // 2
                        act.wait_ge(s["glu_done"], b + 1)
                        act.wait_ge(s["s5_y"], 4)
                        A(mix_s5[:, 2 * b:2 * b + 2, :], banks[2 + b].rearrange("p (f t) -> p f t", t=T), ACT.Sigmoid).then_inc(s["glu_sig"], 1)
                for t in range(TT):
                    o = slice(t * P, (t + 1) * P)
                    if t:
                        act.wait_ge(s["centred"], 2)
                        A(ysq[:, :, o], yc[:, :, o], ACT.Square).then_inc(s["y_squared"], 1)
                    act.wait_ge(s["var_done"], t + 1)
                    A(yrs[:, :, o], banks[7].rearrange("p (f t) -> p f t", t=P), ACT.Sqrt,
                      bias=par[:, NPARAM + 1:NPARAM + 2], scale=1.0 / CH).then_inc(s["var_root"], 1)
                for t in range(TT):
                    act.wait_ge(s["x2_ready"], 2 * t + 2)
                    A(un(33 + t), x2[:, t, :], ACT.Square, accum_out=ssq[:, t:t + 1])

            @block.vector
            def _(dve):
                link = chain(dve, "dve_chain")
                V = nc.vector
                tt, ts, stt = V.tensor_tensor, V.tensor_scalar, V.scalar_tensor_tensor

                def reduce_angle(dst, turns, arg):
                    link(ts(turns, arg, INV_2PI, ROUND, ALU.mult, ALU.add))
                    link(ts(turns, turns, -ROUND, None, ALU.add))
                    link(stt(dst, turns, -PI_A, arg, ALU.mult, ALU.add))
                    link(stt(dst, turns, -PI_B, dst, ALU.mult, ALU.add))

                V.memset(par[:, NPARAM:NPARAM + 1], 1e-6)
                V.memset(par[:, NPARAM + 1:NPARAM + 2], 64e-5).then_inc(s["eps_ready"], 1)
                lre, lim = s5p[:, 1, :], prm("lam_im")
                dve.wait_ge(s["consts_in"], 32)
                link(ts(lre, prm("lam_re"), -1e-4, None, ALU.min))
                dve.wait_ge(s["s5_dt"], 1)
                tt(s5p[:, 2, :], lre, s5p[:, 0, :], ALU.mult).then_inc(s["s5_arg"], 1)
                link(tt(s5p[:, 3, :], lim, s5p[:, 0, :], ALU.mult))
                reduce_angle(s5p[:, 5, :], s5p[:, 6, :], s5p[:, 3, :])
                ts(s5p[:, 5, :], s5p[:, 5, :], PI, -PI, ALU.min, ALU.max).then_inc(s["s5_theta"], 1)
                dve.wait_ge(s["s5_sin"], 1)
                dve.wait_ge(s["s5_mag"], 1)
                sh2, cs, lbr, lbi, zre = (s5p[:, i, :] for i in range(9, 14))
                den, ca, cb, cr, ci = (s5p[:, i, :] for i in range(14, 19))
                link(tt(sh2, s5p[:, 8, :], s5p[:, 8, :], ALU.mult))
                link(ts(cs, sh2, -2.0, 1.0, ALU.mult, ALU.add))
                link(tt(lbr, s5p[:, 4, :], cs, ALU.mult))
                link(tt(lbi, s5p[:, 4, :], s5p[:, 7, :], ALU.mult))
                link(ts(zre, lbr, -1.0, None, ALU.add))
                link(tt(ca, lre, lre, ALU.mult))
                link(tt(cb, lim, lim, ALU.mult))
                link(tt(den, ca, cb, ALU.add))
                link(V.reciprocal(den, den))
                link(tt(ca, zre, lre, ALU.mult))
                link(tt(cb, lbi, lim, ALU.mult))
                link(tt(ca, ca, cb, ALU.add))
                link(tt(cr, ca, den, ALU.mult))
                link(tt(ca, lbi, lre, ALU.mult))
                link(tt(cb, zre, lim, ALU.mult))
                link(tt(ca, ca, cb, ALU.subtract))
                link(tt(ci, ca, den, ALU.mult))
                dve.wait_ge(s["rms_root"], 1)
                link(V.reciprocal(un(43)[:, 0:T], un(43)[:, 0:T]))
                for k in range(KD):
                    h = stt(hT[:, k, :], xT[:, k, :], prm("g_mix")[:, k:k + 1], un(43)[:, 0:T], ALU.mult, ALU.mult)
                h.then_inc(s["h_ready"], 1)
                dve.wait_ge(s["h_ready"], 1)
                tt(dh[:, :, 1:T], hT[:, :, 0:T - 1], hT[:, :, 1:T], ALU.subtract)
                link(ts(dh[:, :, 0:1], hT[:, :, 0:1], -1.0, None, ALU.mult))
                for dst, mu in ((xw, "mu_w"), (xa, "mu_a"), (xg, "mu_g")):
                    for k in range(KD):
                        m = stt(dst[:, k, :], dh[:, k, :], prm(mu)[:, k:k + 1], hT[:, k, :], ALU.mult, ALU.add)
                    m.then_inc(s["mixed"], 1)
                dve.wait_ge(s["s5_in"], 64)
                bre = bb[:, 0, :].rearrange("p (j c) -> p j c", j=NJ)
                bim = bb[:, 1, :].rearrange("p (j c) -> p j c", j=NJ)
                crb = cr[:, :, None].to_broadcast([P, NJ, 32])
                cib = ci[:, :, None].to_broadcast([P, NJ, 32])
                q1, q2, q3 = (un(44, 2)[:, i * 512:(i + 1) * 512].rearrange("p (j c) -> p j c", j=NJ) for i in range(3))
                link(tt(q1, bre, crb, ALU.mult))
                link(tt(q2, bim, cib, ALU.mult))
                link(tt(q1, q1, q2, ALU.subtract))
                link(tt(q2, bim, crb, ALU.mult))
                link(tt(q3, bre, cib, ALU.mult))
                link(V.tensor_copy(bre, q1))
                tt(bim, q2, q3, ALU.add).then_inc(s["bb_ready"], 1)
                def table_arg(g):
                    c, sn = S5C[g % 2], S5S[g % 2]
                    dve.wait_ge(s["table_angle"], g + 1)
                    if g >= 2:
                        dve.wait_ge(s["phase_on"], g - 1)
                    reduce_angle(sn, c, sn)
                    ts(sn, sn, PI, -PI, ALU.min, ALU.max).then_inc(s["table_arg"], 1)

                def table_cos(g):
                    c = S5C[g % 2]
                    dve.wait_ge(s["table_sin"], g + 1)
                    link(tt(c, c, c, ALU.mult))
                    ts(c, c, -2.0, 1.0, ALU.mult, ALU.add).then_inc(s["table_ready"], 1)

                def scan(g):
                    dve.wait_ge(s["phase_off"], g + 1)
                    for j in range(4):
                        mag = s5p[:, 4, 4 * g + j:4 * g + j + 1].to_broadcast([P, T])
                        V.tensor_tensor_scan(sA[g % 2][:, j, :], mag, sT1[g % 2][:, j, :], 0.0, ALU.mult, ALU.add)
                        z = V.tensor_tensor_scan(sB[g % 2][:, j, :], mag, sT2[g % 2][:, j, :], 0.0, ALU.mult, ALU.add)
                    z.then_inc(s["scanned"], 1)

                def s5_y(g):
                    dve.wait_ge(s["s5_out_done"], g + 1)
                    stt(ys5[:, g, :], uT[:, g, :], prm("s5_d")[:, g:g + 1], banks[2 + g % 2][:, 0:T], ALU.mult, ALU.add).then_inc(s["s5_y"], 1)

                def token_shift(name, dst):
                    src = raw[name]
                    tt(tmp[:, :, 1:T], src[:, :, 0:T - 1], src[:, :, 1:T], ALU.subtract)
                    link(ts(tmp[:, :, 0:1], src[:, :, 0:1], -1.0, None, ALU.mult))
                    for i in range(FT):
                        m = stt(dst[:, i, :], tmp[:, i, :], prm("mu_" + name)[:, i:i + 1], src[:, i, :], ALU.mult, ALU.add)
                    return m

                table_arg(0)
                table_arg(1)
                table_cos(0)
                dve.wait_ge(s["proj_done"], 1)
                link(V.memset(EL, 1.0))
                link(V.memset(EL[:, :, 0::CH], 0.0))
                dve.wait_ge(s["lora2_copied"], 2)
                link(ts(lw, lw, -DECAY, None, ALU.mult))
                link(V.tensor_tensor_scan(un(0), un(1), un(31), 0.0, ALU.mult, ALU.add))
                tt(lw, Lc, lw, ALU.subtract).then_inc(s["decay_ready"], 1)
                table_cos(1)
                dve.wait_ge(s["proj_copied"], 4)
                dve.wait_ge(s["lora1_done"], 3)
                link(token_shift("k", kx))
                for i in range(FT):
                    m = ts(kkn[:, i, :], kx[:, i, :], prm("k_k")[:, i:i + 1], None, ALU.mult)
                m.then_inc(s["kk_ready"], 1)
                dve.wait_ge(s["kk_ready"], 1)
                dve.wait_ge(s["lora2_copied"], 4)
                link(ts(k2, la, -1.0, None, ALU.add))
                for i in range(FT):
                    m = ts(k2[:, i, :], k2[:, i, :], prm("k_a")[:, i:i + 1], 1.0, ALU.mult, ALU.add)
                link(m)
                link(tt(k2, k2, kx, ALU.mult))
                scan(0)
                dve.wait_ge(s["kk_root"], 1)
                link(ts(kb, kb, 1e-12, None, ALU.max))
                link(V.reciprocal(kb, kb))
                link(tt(kkn, kkn, kb, ALU.mult))
                link(tt(kb, kkn, la, ALU.mult))
                dve.wait_ge(s["exp_ready"], 1)
                stt(un(31), un(31), -1.0, un(40), ALU.mult, ALU.mult)
                tt(bh, kb, Lc, ALU.mult).then_inc(s["scaled"], 1)
                dve.wait_ge(s["proj_done"], 5)
                tt(kh, k2, Lc, ALU.mult).then_inc(s["scaled"], 1)
                scan(1)
                table_arg(2)
                dve.wait_ge(s["proj_copied"], 6)
                link(token_shift("r", rr))
                s5_y(0)
                link(tt(rk, rr, k2, ALU.mult))
                for i in range(FT):
                    m = ts(rk[:, i, :], rk[:, i, :], prm("r_k")[:, i:i + 1], None, ALU.mult)
                m.then_inc(s["rk_ready"], 1)
                tt(rt, rr, EL, ALU.mult).then_inc(s["scaled"], 1)
                V.memset(state[:, :], 0.0).then_inc(s["state_zero"], 1)
                def col(c):
                    return con[:, c:c + CH][:, None, :].to_broadcast([P, 8, CH])
                eye = col(C_ID2)

                def level_mask(lev, b):
                    lm = con[:, C_LEV + lev * CH:C_LEV + (lev + 1) * CH][:, None, :].to_broadcast([P, 8, CH])
                    tt(MO[:, 8 * b:8 * b + 8, :], Mx[:, 8 * b:8 * b + 8, :], lm, ALU.mult).then_inc(s["mo_ready"], 1)

                def turn_x(b):
                    return V.transpose(Y[:, 8 * b:8 * b + 8, :], X[:, 8 * b:8 * b + 8, :])

                def turn(dst, src):
                    for h in range(2):
                        for i in range(2):
                            for j in range(2):
                                a, o = h * CH + 32 * i, h * CH + 32 * j
                                m = V.transpose(dst[o:o + 32].rearrange("p (c f) (i k) -> p f c i k", c=NCH, i=2)[:, :, :, i, :],
                                                src[a:a + 32].rearrange("p f (c j k) -> p f c j k", c=NCH, j=2)[:, :, :, j, :])
                    m.then_inc(s["turned"], 1)

                for m, (dst, mask) in enumerate(((X, C_SU1), (Mx, None), (KA, C_SU), (RB, C_UI), (RK, C_UI))):
                    for b in range(2):
                        dve.wait_ge(s["scores_done"], 2 * m + b + 1)
                        src = banks[SCORE_BANK[m] + b].rearrange("p (u t) -> p u t", t=CH)
                        d = dst[:, 8 * b:8 * b + 8, :]
                        if m == 1:
                            V.tensor_copy(d, src).then_inc(s["scores_copied"], 1)
                        elif m == 0:
                            link(tt(d, src, col(mask), ALU.mult))
                            link(tt(d, d, eye, ALU.add))
                            turn_x(b).then_inc(s["scores_copied"], 1)
                        else:
                            tt(d, src, col(mask), ALU.mult).then_inc(s["scores_copied"], 1)
                    if m == 0:
                        table_cos(2)
                    if m == 2:
                        s5_y(1)
                        table_arg(3)
                dve.wait_ge(s["proj_copied"], 8)
                token_shift("v", vv).then_inc(s["scaled"], 1)
                dve.wait_ge(s["scaled"], 4)
                dve.wait_ge(s["scores_copied"], 4)
                for b in range(2):
                    level_mask(0, b)
                table_cos(3)
                dve.wait_ge(s["rk_summed"], 1)
                for b in range(2):
                    m = tt(bonus[:, 2 * b:2 * b + 2, :], banks[b].rearrange("p (f t) -> p f t", t=T), vv[:, 2 * b:2 * b + 2, :], ALU.mult)
                m.then_inc(s["bonus_ready"], 1)
                scan(2)
                for lev in range(LEVELS):
                    for b in range(2):
                        if lev < LEVELS - 1:
                            dve.wait_ge(s["w_done"], 2 * lev + b + 1)
                            level_mask(lev + 1, b)
                    for b in range(2):
                        dve.wait_ge(s["xy_done"], 2 * lev + b + 1)
                        d = X[:, 8 * b:8 * b + 8, :]
                        tt(d, d, banks[6 + b].rearrange("p (u t) -> p u t", t=CH), ALU.add).then_inc(s["xy_ready"], 1)
                        if lev < LEVELS - 1:
                            dve.wait_ge(s["xy_ready"], 2 * lev + b + 1)
                            turn_x(b).then_inc(s["y_turned"], 1)
                    if lev == 0:
                        scan(3)
                    if lev in (1, 2, 3):
                        turn(*((Bs, bh), (Ks, kh), (Vs, vv))[lev - 1])
                    if lev in (2, 3):
                        s5_y(lev)

                def glu_gate(b):
                    dve.wait_ge(s["glu_sig"], b + 1)
                    tt(mix_s5[:, 2 * b:2 * b + 2, :], mix_s5[:, 2 * b:2 * b + 2, :], ys5[:, 2 * b:2 * b + 2, :], ALU.mult).then_inc(s["mix_s5_ready"], 1)

                def centre(t):
                    o = slice(t * P, (t + 1) * P)
                    dve.wait_ge(s["mean_done"], t + 1)
                    stt(yc[:, :, o], banks[6].rearrange("p (f t) -> p f t", t=P), -1.0 / CH, yT[:, :, o], ALU.mult, ALU.add).then_inc(s["centred"], 1)

                def normalise(t):
                    o = slice(t * P, (t + 1) * P)
                    dve.wait_ge(s["centred"], t + 1)
                    dve.wait_ge(s["var_root"], t + 1)
                    link(V.reciprocal(yrs[:, :, o], yrs[:, :, o]))
                    link(tt(yc[:, :, o], yc[:, :, o], yrs[:, :, o], ALU.mult))
                    for i in range(FT):
                        m = ts(yc[:, i, o], yc[:, i, o], prm("ln_w")[:, i:i + 1], prm("ln_b")[:, i:i + 1], ALU.mult, ALU.add)
                    link(m)
                    link(tt(yc[:, :, o], yc[:, :, o], bonus[:, :, o], ALU.add))
                    tt(mix_rw[:, :, o], yc[:, :, o], lg[:, :, o], ALU.mult).then_inc(s["mix_rw_ready"], 1)

                for c in range(NCH - 1):
                    dve.wait_ge(s["state_done"], c + 1)
                    dve.wait_ge(s["y_done"], c + 1)
                    link(tt(state[:, :], banks[4][:, 0:FT * CH], state[:, :], ALU.add))
                    tt(state[:, :].rearrange("p (f v) -> p f v", v=CH), state[:, :].rearrange("p (f v) -> p f v", v=CH),
                       chunk_decay[:, :, c:c + 1].to_broadcast([P, FT, CH]), ALU.mult).then_inc(s["state_ready"], 1)
                    if c == 1:
                        glu_gate(0)
                centre(0)
                glu_gate(1)
                centre(1)
                normalise(0)
                normalise(1)
                dve.wait_ge(s["x_in"], 16)
                for t in range(TT):
                    for hf in range(2):
                        n = 2 * t + hf
                        dve.wait_ge(s["out_done"], n + 1)
                        tt(x2[:, t, hf * 512:(hf + 1) * 512], x_tok[:, t, hf * 512:(hf + 1) * 512], banks[n][:, :], ALU.add).then_inc(s["x2_ready"], 1)

            @block.tensor
            def _(pe):
                pe.wait_ge(s["consts_in"], 32)
                pe.wait_ge(s["sq_ready"], 1)
                for k in range(KD):
                    last = mm(banks[7][:, 0:T], ones, sq[:, k, :], k == 0, k == KD - 1)
                last.then_inc(s["rms_summed"], 1)
                def project(n):
                    q = order[n]
                    pe.wait_ge(win_in[q], 16 if q < 2 else 32)
                    if n >= 2:
                        pe.wait_ge(s["proj_copied"], n - 1)
                    for f in range(2):
                        for k in range(KD):
                            last = mm(banks[n % 2][:, f * T:(f + 1) * T], win[q][:, k, f * P:(f + 1) * P], hT[:, k, :], k == 0, k == KD - 1)
                    last.then_inc(s["proj_done"], 1)

                def bu(g):
                    pe.wait_ge(s["bb_copied"], 2)
                    pe.wait_ge(s["proj_copied"], 2)
                    pe.wait_ge(s["lora_hidden_ready"], 2)
                    if g >= 2:
                        pe.wait_ge(s["s5_y"], g - 1)
                    for j in range(4):
                        if 4 * g + j >= 2:
                            pe.wait_ge(s["bu_copied"], 4 * g + j - 1)
                        a = slice(32 * j, 32 * j + 32)
                        for m in range(2):
                            last = mm(banks[2 + j % 2][:, m * T:(m + 1) * T], bb[a, m, g * P:(g + 1) * P], uT[a, g, :], True, True)
                        last.then_inc(s["bu_done"], 1)

                def s5_out(g):
                    pe.wait_ge(s["phase_on"], g + 1)
                    pe.wait_ge(s["bu_copied"], min(4 * g + 8, 16))
                    for j in range(4):
                        a = slice(32 * j, 32 * j + 32)
                        for m, src in enumerate((sT1[g % 2], sT2[g % 2])):
                            last = mm(banks[2 + g % 2][a, 0:T], cc[:, m, (4 * g + j) * 32:(4 * g + j + 1) * 32], src[:, j, :], m == 0, m == 1)
                    last.then_inc(s["s5_out_done"], 1)

                pe.wait_ge(s["h_ready"], 1)
                project(0)
                project(1)
                pe.wait_ge(s["lora_in"], 16)
                for m, (src, a, b, out) in enumerate(((xw, 0, 64, banks[4][0:CH, 0:T]), (xa, 64, 128, banks[4][CH:P, 0:T]),
                                                      (xg, 128, 256, banks[3][:, 0:T]))):
                    pe.wait_ge(s["mixed"], m + 1)
                    for k in range(KD):
                        last = mm(out, lora1[:, k, a:b], src[:, k, :], k == 0, k == KD - 1)
                    last.then_inc(s["lora1_done"], 1)
                pe.wait_ge(s["bb_ready"], 1)
                for m in range(2):
                    for J in range(4):
                        last = nc.tensor.transpose(banks[5 + m][:, J * P:(J + 1) * P], bb[:, m, J * P:(J + 1) * P], ident)
                last.then_inc(s["bb_turned"], 1)
                bu(0)
                pe.wait_ge(s["lora2_in"], 16)
                for m in range(3):
                    pe.wait_ge(s["lora_hidden_ready"], 1 if m < 2 else 2)
                    for i in range(FT):
                        if m and i % 2 == 0:
                            pe.wait_ge(s["lora2_copied"], 2 * m - 2 + i // 2 + 1)
                        out = banks[5 + i // 2][:, (i % 2) * T:(i % 2 + 1) * T]
                        if m == 0:
                            last = mm(out, lora2[0:CH, i * P:(i + 1) * P], lora_hidden[0:CH, 0:T], True, True)
                        elif m == 1:
                            last = mm(out, lora2[CH:P, i * P:(i + 1) * P], lora_hidden[CH:P, 0:T], True, True)
                        else:
                            last = mm(out, lora2[:, W + i * P:W + (i + 1) * P], lora_hidden[:, T:2 * T], True, True)
                        if i % 2:
                            last.then_inc(s["lora2_done"], 1)
                project(2)
                project(3)
                bu(1)
                project(4)
                pe.wait_ge(s["kk_squared"], 1)
                pe.wait_ge(s["lora2_copied"], 6)
                for b in range(2):
                    last = mm(banks[4 + b][:, :], head_ones, kksq[:, 2 * b:2 * b + 2, :], True, True)
                last.then_inc(s["kk_summed"], 1)
                for n in range(5, 8):
                    project(n)
                s5_out(0)

                def fm(arr, u):
                    return arr[:, u % FT, (u // FT) * CH:(u // FT + 1) * CH]

                for m, (l, r, needs) in enumerate(((bh, at, 1), (at, bh, 1), (kh, at, 2), (bh, rt, 3), (kh, rt, 3))):
                    pe.wait_ge(s["scaled"], needs)
                    for b in range(2):
                        if m == 2:
                            pe.wait_ge(s["proj_copied"], 8)
                        if m >= 3:
                            pe.wait_ge(s["scores_copied"], 2 * m - 6 + b + 1)
                        bank = banks[SCORE_BANK[m] + b]
                        for u in range(8 * b, 8 * b + 8):
                            last = pair(bank[:, (u % 8) * CH:(u % 8 + 1) * CH], fm(l, u), fm(r, u))
                        last.then_inc(s["scores_done"], 1)
                    if m == 1:
                        bu(2)
                    if m == 2:
                        s5_out(1)
                    if m == 3:
                        bu(3)
                pe.wait_ge(s["rk_ready"], 1)
                pe.wait_ge(s["scores_copied"], 6)
                for b in range(2):
                    last = mm(banks[b][:, :], head_ones, rk[:, 2 * b:2 * b + 2, :], True, True)
                last.then_inc(s["rk_summed"], 1)
                for lev in range(LEVELS):
                    for b in range(2):
                        if lev == 0:
                            pe.wait_ge(s["scores_copied"], 10)
                        else:
                            pe.wait_ge(s["xy_ready"], 2 * lev - 2 + b + 1)
                        pe.wait_ge(s["mo_ready"], 2 * lev + b + 1)
                        for u in range(8 * b, 8 * b + 8):
                            last = pair(banks[4 + b][:, (u % 8) * CH:(u % 8 + 1) * CH], MO[:, u, :], X[:, u, :])
                        last.then_inc(s["w_done"], 1)
                    for b in range(2):
                        pe.wait_ge(s["w_copied"], 2 * lev + b + 1)
                        if lev:
                            pe.wait_ge(s["y_turned"], 2 * lev - 2 + b + 1)
                        for u in range(8 * b, 8 * b + 8):
                            last = pair(banks[6 + b][:, (u % 8) * CH:(u % 8 + 1) * CH], Y[:, u, :], Wk[:, u, :])
                        last.then_inc(s["xy_done"], 1)
                    if lev in (2, 3):
                        s5_out(lev)
                pe.wait_ge(s["xy_ready"], 2 * LEVELS)
                pe.wait_ge(s["turned"], 3)
                pe.wait_ge(s["bonus_ready"], 1)
                pe.wait_ge(s["state_zero"], 1)
                pe.wait_ge(s["s5_gelu"], 1)
                pe.wait_ge(s["glu_in"], 16)

                def glu(f):
                    for k in range(FT):
                        last = mm(banks[2 + f // 2][:, (f % 2) * T:(f % 2 + 1) * T], wglu[:, k, f * P:(f + 1) * P], ys5[:, k, :], k == 0, k == FT - 1)
                    if f % 2:
                        last.then_inc(s["glu_done"], 1)

                def mean(t):
                    pe.wait_ge(s["y_copied"], 2 * t + 2)
                    if t:
                        pe.wait_ge(s["centred"], 1)
                    mm(banks[6][:, :], head_ones, yT[:, :, t * P:(t + 1) * P], True, True).then_inc(s["mean_done"], 1)

                def variance(t):
                    pe.wait_ge(s["y_squared"], t + 1)
                    if t:
                        pe.wait_ge(s["var_root"], 1)
                    mm(banks[7][:, :], head_ones, ysq[:, :, t * P:(t + 1) * P], True, True).then_inc(s["var_done"], 1)

                tiles = [slice(i * CH, (i + 1) * CH) for i in range(FT)]
                for c in range(NCH):
                    if c:
                        pe.wait_ge(s["u0_ready"], c)
                    for i, o in enumerate(tiles):
                        pair(banks[0][:, o], KA[:, c * FT + i, :], Vs[:, c * FT + i, :], i == 0, False)
                    if c:
                        pe.wait_ge(s["y_copied"], c)
                    for i, o in enumerate(tiles):
                        pair(banks[5][:, o], Vs[:, c * FT + i, :], RK[:, c * FT + i, :], i == 0, False)
                    if c:
                        pe.wait_ge(s["state_ready"], c)
                    for i, o in enumerate(tiles):
                        last = pair(banks[0][:, o], fm(at, c * FT + i), state[:, o], False, True)
                    last.then_inc(s["u0_done"], 1)
                    for i, o in enumerate(tiles):
                        pair(banks[5][:, o], state[:, o], fm(rt, c * FT + i), False, False)
                    pe.wait_ge(s["u0_ready"], c + 1)
                    for i, o in enumerate(tiles):
                        last = pair(banks[1][:, o], X[:, c * FT + i, :], u0[:, o])
                    last.then_inc(s["u_done"], 1)
                    if c < NCH - 1:
                        for i, o in enumerate(tiles):
                            pair(banks[4][:, o], Ks[:, c * FT + i, :], Vs[:, c * FT + i, :], i == 0, False)
                    glu(c)
                    if c == NCH - 1:
                        variance(0)
                    pe.wait_ge(s["u_ready"], c + 1)
                    if c < NCH - 1:
                        for i, o in enumerate(tiles):
                            last = pair(banks[4][:, o], Bs[:, c * FT + i, :], uu[:, o], False, True)
                        last.then_inc(s["state_done"], 1)
                    for i, o in enumerate(tiles):
                        last = pair(banks[5][:, o], uu[:, o], RB[:, c * FT + i, :], False, True)
                    last.then_inc(s["y_done"], 1)
                    if c == NCH - 2:
                        mean(0)
                mean(1)
                pe.wait_ge(wout_in, 64)
                pe.wait_ge(s["mix_s5_ready"], 2)

                def project_out(t, ks, first, last_part):
                    for hf in range(2):
                        for n, k in enumerate(ks):
                            src = mix_s5[:, k, t * P:(t + 1) * P] if k < FT else mix_rw[:, k - FT, t * P:(t + 1) * P]
                            last = mm(banks[2 * t + hf][:, :], src, wout[k // 2][:, k % 2, hf * 512:(hf + 1) * 512],
                                      first and n == 0, last_part and n == len(ks) - 1)
                        if last_part:
                            last.then_inc(s["out_done"], 1)

                project_out(0, range(FT), True, False)
                variance(1)
                pe.wait_ge(s["glu_sig"], 2)
                project_out(1, range(FT), True, False)
                for t in range(TT):
                    pe.wait_ge(s["mix_rw_ready"], t + 1)
                    project_out(t, range(FT, KD), False, True)

        experts(nc, io, ctx, arena, con, par, banks, ring, chunk_in, chunk_src, p_in, ssq, x2)


def experts(nc, io, ctx, arena, con, par, banks, ring, chunk_in, chunk_src, p_in, ssq, x2):
    def sb(name, shape, dt=F32):
        return ctx.enter_context(nc.sbuf_tensor(name, shape, dt))

    def un(i, n=1):
        return arena[:, i * UNIT:(i + n) * UNIT]

    def prm(name):
        a, n = PARAMS[name]
        return par[:, a:a + n]

    ident = con[:, C_ID:C_ID + P]
    ones = con[:, C_ONES:C_ONES + P]
    tri = con[:, C_TRI:C_TRI + P]
    HF = D // 2

    xn = un(33, 2).rearrange("p (t d) -> p t d", d=D)
    xres = un(35, 2).rearrange("p (t d) -> p t d", d=D)
    parts = un(24, 3).bitcast(BF16).rearrange("p (t q d) -> p t q d", t=TT, q=3)
    hT = un(27, 2).rearrange("p (k t) -> p k t", k=KD)
    bias = un(37, 3).rearrange("p (m d) -> p m d", m=3)
    y = un(40)[:, 0:HF]
    xg = un(40)[:, HF:2 * HF].rearrange("p (k s) -> p k s", k=KD)
    gt = un(41)[:, 0:HF]
    up = un(41)[:, HF:2 * HF]
    sg = un(42)[:, 0:HF]
    actT = un(42)[:, HF:2 * HF].rearrange("p (h k s) -> p k h s", h=2, k=4)
    gT = un(43)[:, 0:TT * P].rearrange("p (t m) -> p t m", t=TT)
    pg = un(43)[:, 256:512].rearrange("p (t m) -> p t m", t=TT)
    onehot = un(43)[:, 512:576].bitcast(BF16).rearrange("p (t m) -> p t m", t=TT)
    pick = un(43)[:, 576:640]
    router = un(43)[:, 640:640 + KD * E].rearrange("p (k e) -> p k e", k=KD)
    rbias = un(43)[:, 896:896 + E]
    lg = un(44)[:, 0:64].rearrange("p (t e) -> p t e", t=TT)
    gates = un(44)[:, 64:128].rearrange("p (t e) -> p t e", t=TT)
    mask = un(44)[:, 128:192].rearrange("p (t e) -> p t e", t=TT)
    rank = un(44)[:, 192:256].rearrange("p (t e) -> p t e", t=TT)
    top = un(44)[:, 256:272].rearrange("p (t e) -> p t e", t=TT)
    topi = un(44)[:, 272:288].bitcast(U32).rearrange("p (t e) -> p t e", t=TT)
    topf = un(44)[:, 288:304].rearrange("p (t e) -> p t e", t=TT)
    ex = un(44)[:, 304:320].rearrange("p (t e) -> p t e", t=TT)
    st = un(44)[:, 320:352]
    hot = un(44)[:, 512:512 + TT * TOPK * E].rearrange("p (t j e) -> p t j e", t=TT, j=TOPK)
    hotg = un(44)[:, 768:768 + TT * TOPK * E].rearrange("p (t j e) -> p t j e", t=TT, j=TOPK)
    cnt = un(44)[:, 384:416]
    cflag = un(44)[:, 416:424]
    nexp = un(44)[:, 424:425].bitcast(I32)

    def sem(name):
        return ctx.enter_context(nc.semaphore(name))

    s = {n: sem("m_" + n) for n in (
        "router_in", "bias_in", "root", "ple_done", "ple_copied", "parted", "scaled", "pool", "turned", "h_ready", "logits_done", "top_ready", "exp_ready",
        "mask_ready", "rank_done", "count_ready", "dve", "swish_ready", "tail", "up_read",
        "ranks_moved", "hot_ready", "gathered", "xg_ready", "gate_done", "up_done", "down_done", "chunks_used",
        "gt_ready", "sig_ready", "act_ready", "pg_ready", "gT_done", "gT_ready", "actT_done", "actT_ready",
        "y_ready", "scattered", "picked")}

    def mm(out, lhsT, rhs, start, stop):
        return nc.tensor.matmul(out, lhsT, rhs, start=start, stop=stop, skip_group_check=True)

    def chain(eng, name):
        n = [0]

        def link(ins):
            n[0] += 1
            ins.then_inc(s[name], 1)
            eng.wait_ge(s[name], n[0])
        return link

    pT = un(30)[:, 0:TT * T].rearrange("p (k t) -> p k t", k=2)
    wproj = un(41, 2).rearrange("p (k n) -> p k n", n=D)
    ple = un(27, 2).rearrange("p (n d) -> p n d", d=HF)

    with nc.Block() as block:
        @block.sync
        def _(sp):
            sp.dma_start(router[:, :, :], io["router_w"].rearrange("(k p) e -> p k e", p=P)).then_inc(s["router_in"], 16)
            sp.dma_start(rbias[:, :], io["router_b"].to_broadcast([P, E])).then_inc(s["router_in"], 16)
            for m, b in enumerate(("exp_b_gate", "exp_b_up", "exp_b_down")):
                sp.dma_start(bias[0:E, m, :], io[b]).then_inc(s["bias_in"], 16)
            for c in range(4, 8):
                sp.dma_start(ring[c][:, :, :], chunk_src(c, 0)).then_inc(chunk_in[c], 16)

        @block.scalar
        def _(act):
            nc.scalar.activation(st[:, 0:2], ssq[:, 0:2], ACT.Sqrt, bias=par[:, NPARAM:NPARAM + 1], scale=1.0 / D).then_inc(s["root"], 1)
            for k in range(KD):
                act.wait_ge(s["turned"], k + 1)
                nc.scalar.activation(hT[:, k, :], banks[4 + k % 4][:, 0:T], ACT.Copy, scale=prm("g_moe")[:, k:k + 1]).then_inc(s["h_ready"], 1)
            act.wait_ge(s["top_ready"], 1)
            for t in range(TT):
                last = nc.scalar.activation(ex[:, t, 0:4], top[:, t, 0:4], ACT.Exp, bias=st[:, 2 + t:3 + t], accum_out=st[:, 4 + t:5 + t])
            last.then_inc(s["exp_ready"], 1)
            for n in range(4):
                act.wait_ge(s["ple_done"], n + 1)
                nc.scalar.activation(ple[:, n, :], banks[n][:, :], ACT.Copy).then_inc(s["ple_copied"], 1)

        @block.vector
        def _(dve):
            link = chain(dve, "dve")
            V = nc.vector
            tt, ts, stt = V.tensor_tensor, V.tensor_scalar, V.scalar_tensor_tensor
            dve.wait_ge(s["root"], 1)
            link(V.reciprocal(st[:, 0:2], st[:, 0:2]))
            ts(xn[:, 1, :], x2[:, 1, :], st[:, 1:2], None, ALU.mult).then_inc(s["scaled"], 1)

            def part(t):
                link(ts(xn[:, t, :], x2[:, t, :], st[:, t:t + 1], None, ALU.mult))
                link(V.tensor_copy(parts[:, t, 0, :], xn[:, t, :]))
                link(tt(xres[:, t, :], xn[:, t, :], parts[:, t, 0, :], ALU.subtract))
                link(V.tensor_copy(parts[:, t, 1, :], xres[:, t, :]))
                link(tt(xres[:, t, :], xres[:, t, :], parts[:, t, 1, :], ALU.subtract))
                link(V.tensor_copy(parts[:, t, 2, :], xres[:, t, :]))

            part(0)
            V.memset(gT[:, :, :], 0.0).then_inc(s["gT_ready"], 1)
            V.memset(y, 0.0).then_inc(s["y_ready"], 1)
            for i, name in enumerate(("actT_ready", "gT_done")):
                V.memset(st[:, 8 + i:9 + i], 0.0).then_inc(s[name], 1)
            dve.wait_ge(s["router_in"], 32)
            for t in range(TT):
                dve.wait_ge(s["logits_done"], t + 1)
                m = stt(lg[:, t, :], banks[6 + t][:, 0:E], st[:, t:t + 1], rbias[:, :], ALU.mult, ALU.add)
            link(m)
            for t in range(TT):
                m = V.max(top[:, t, :], lg[:, t, :])
            link(m)
            ts(st[:, 2:4], top[:, :, 0], -1.0, None, ALU.mult).then_inc(s["top_ready"], 1)
            for t in range(TT):
                m = V.max_index(topi[:, t, :], top[:, t, :], lg[:, t, :])
            link(m)
            link(V.tensor_copy(topf[:, :, :], topi[:, :, :]))
            every = [P, TT, TOPK, E]
            link(tt(hot[:, :, :, :], con[:, C_E32:C_E32 + E][:, None, None, :].to_broadcast(every),
                    topf[:, :, 0:TOPK][:, :, :, None].to_broadcast(every), ALU.is_equal))
            V.tensor_reduce(mask[:, :, :], hot.rearrange("p t j e -> p t e j"), AX.X, ALU.add).then_inc(s["mask_ready"], 1)
            dve.wait_ge(s["exp_ready"], 1)
            link(V.reciprocal(st[:, 6:8], st[:, 4:6]))
            for t in range(TT):
                m = ts(ex[:, t, 0:TOPK], ex[:, t, 0:TOPK], st[:, 6 + t:7 + t], None, ALU.mult)
            link(m)
            link(tt(hotg[:, :, :, :], hot[:, :, :, :], ex[:, :, 0:TOPK][:, :, :, None].to_broadcast(every), ALU.mult))
            link(V.tensor_reduce(gates[:, :, :], hotg.rearrange("p t j e -> p t e j"), AX.X, ALU.add))
            dve.wait_ge(s["mask_ready"], 1)
            link(ts(rank[:, :, :], mask[:, :, :], -1000.0, 1000.0, ALU.mult, ALU.add))
            dve.wait_ge(s["rank_done"], 1)
            tt(rank[:, :, :], rank[:, :, :], banks[4][:, 0:TT * E].rearrange("p (t e) -> p t e", t=TT), ALU.add)
            link(V.tensor_reduce(cnt[:, 0:1], banks[4][:, TT * E:TT * E + E], AX.X, ALU.max))
            link(tt(cflag[:, 1:MAX_PASS], cnt[:, 0:1].to_broadcast([P, MAX_PASS - 1]),
                    con[:, C_TIME + SLOTS:C_TIME + T:SLOTS], ALU.is_gt))
            link(V.tensor_reduce(cnt[:, 1:2], cflag[:, 1:MAX_PASS], AX.X, ALU.add))
            ts(nexp[:, 0:1], cnt[:, 1:2], float(E), float(E), ALU.mult, ALU.add).then_inc(s["count_ready"], 1)

        @block.gpsimd
        def _(pool):
            link = chain(pool, "pool")
            tt, copy = nc.gpsimd.tensor_tensor, nc.gpsimd.tensor_copy
            pool.wait_ge(s["scaled"], 1)
            link(copy(parts[:, 1, 0, :], xn[:, 1, :]))
            link(tt(xres[:, 1, :], xn[:, 1, :], parts[:, 1, 0, :], ALU.subtract))
            link(copy(parts[:, 1, 1, :], xres[:, 1, :]))
            link(tt(xres[:, 1, :], xres[:, 1, :], parts[:, 1, 1, :], ALU.subtract))
            copy(parts[:, 1, 2, :], xres[:, 1, :]).then_inc(s["parted"], 1)

        @block.tensor
        def _(pe):
            def ple_proj(n):
                t, hf = n // 2, n % 2
                for k in range(2):
                    last = mm(banks[n][:, :], pT[:, k, t * P:(t + 1) * P], wproj[:, k, hf * HF:(hf + 1) * HF], k == 0, k == 1)
                last.then_inc(s["ple_done"], 1)

            pe.wait_ge(p_in, 32)
            for k in range(KD):
                if k >= 4:
                    pe.wait_ge(s["h_ready"], k - 3)
                for t in range(TT):
                    last = nc.tensor.transpose(banks[4 + k % 4][:, t * P:(t + 1) * P], x2[:, t, k * P:(k + 1) * P], ident)
                last.then_inc(s["turned"], 1)
            ple_proj(0)
            ple_proj(1)
            pe.wait_ge(s["router_in"], 32)
            pe.wait_ge(s["h_ready"], KD)
            for t in range(TT):
                for k in range(KD):
                    last = mm(banks[6 + t][:, 0:E], hT[:, k, t * P:(t + 1) * P], router[:, k, :], k == 0, k == KD - 1)
                last.then_inc(s["logits_done"], 1)
            ple_proj(2)
            pe.wait_ge(s["mask_ready"], 1)
            mm(banks[4][:, 0:32], tri, mask[:, 0, :], True, True)
            mm(banks[4][:, 32:64], ones, mask[:, 0, :], True, False)
            mm(banks[4][:, 32:64], tri, mask[:, 1, :], False, True)
            mm(banks[4][:, 64:96], ones, mask[:, 0, :], True, False)
            mm(banks[4][:, 64:96], ones, mask[:, 1, :], False, True).then_inc(s["rank_done"], 1)
            ple_proj(3)
            pe.wait_ge(s["y_ready"], 1)
            pe.wait_ge(s["gT_ready"], 1)
            for n in range(4):
                pe.wait_ge(s["ple_copied"], n + 1)
                mm(banks[n][:, :], gT[:, 0, 0:P // 2].bitcast(BF16), y[:, 0:HF // 2].bitcast(BF16), True, False)

    def scatter():
        for t in range(TT):
            for hf in range(2):
                a = slice(hf * 64, hf * 64 + 64)
                last = mm(banks[2 * t + hf][:, :], gT[a, t, :], y[a, :], False, True)
        return last

    GATE, UP, GAT, YB = banks[4], banks[5], banks[6], banks[7]

    def count(eng):
        return eng.value_load(nexp[0:1, 0:1], min_val=E, max_val=MAX_PASS * E)

    fin = un(33, 2).rearrange("p (t d) -> p t d", d=D)
    t2 = {n: sem("t_" + n) for n in (
        "gate_w_in", "fg_in", "scattered", "x3_ready", "squared", "root", "inverse", "turned", "h_ready",
        "gate_done", "sig_ready", "x4_ready", "squared2", "root2", "out_ready", "out")}
    fg = un(45)

    with nc.Block() as block:
        @block.sync
        def _(sp):
            n_all = count(sp)
            sp.dma_start(fg[:, :], io["final_g"].to_broadcast([P, D])).then_inc(t2["fg_in"], 16)
            with sp.Fori(1, n_all) as n:
                e = sp.snap(n % E)
                for c in range(NC):
                    sp.wait_ge(s["chunks_used"], (n - 1) * NC + c + 1)
                    sp.dma_start(ring[c][:, :, :], chunk_src(c, e)).then_inc(chunk_in[c], 16)
            wg = io["ple_w_gate"].rearrange("(c k p) n -> c p k n", p=P, k=2)
            sp.wait_ge(s["gate_done"], n_all)
            for c in range(4):
                sp.dma_start(ring[c][:, :, :], wg[c]).then_inc(t2["gate_w_in"], 16)

        @block.scalar
        def _(act):
            n_all = count(act)
            with act.Fori(0, n_all) as n:
                act.wait_ge(s["gt_ready"], n + 1)
                nc.scalar.activation(sg, gt, ACT.Sigmoid, scale=1.702).then_inc(s["sig_ready"], 1)
                act.wait_ge(s["gT_done"], n + 2)
                act.wait_ge(s["scattered"], n + 1)
                nc.scalar.activation(gT[:, :, :], YB[:, 0:TT * P].rearrange("p (t m) -> p t m", t=TT), ACT.Copy).then_inc(s["gT_ready"], 1)
                act.wait_ge(s["actT_done"], n + 1)
                nc.scalar.activation(actT[:, :, :, :], GATE[:, :].rearrange("p (k h s) -> p k h s", h=2, k=4), ACT.Copy).then_inc(s["actT_ready"], 1)

        @block.vector
        def _(dve):
            V = nc.vector
            tt, ts, stt = V.tensor_tensor, V.tensor_scalar, V.scalar_tensor_tensor
            n_all = count(dve)
            iota = con[:, C_IOTA:C_IOTA + P]

            def one_hot(e):
                for t in range(TT):
                    ts(onehot[:, t, :], iota[:, 0:SLOTS], rank[:, t, bass.ds(e, 1)], None, ALU.is_equal).then_inc(s["hot_ready"], 1)

            def gathered_times_gain():
                tt(xg[:, :, :], GAT[:, :].rearrange("p (k s) -> p k s", k=KD),
                   prm("g_moe")[:, :, None].to_broadcast([P, KD, SLOTS]), ALU.mult).then_inc(s["xg_ready"], 1)

            one_hot(0)
            dve.wait_ge(s["gathered"], 1)
            gathered_times_gain()
            with dve.Fori(0, n_all) as n:
                e = dve.snap(n % E)
                e_next = dve.snap((n + 1) % E)
                dve.wait_ge(s["gT_done"], n + 1)
                for t in range(TT):
                    ts(pg[:, t, :], iota, rank[:, t, bass.ds(e, 1)], gates[:, t, bass.ds(e, 1)], ALU.is_equal, ALU.mult).then_inc(s["pg_ready"], 1)
                V.tensor_copy(pick[0:E, :], ident[0:E, bass.ds(e, 1)].to_broadcast([E, SLOTS])).then_inc(s["picked"], 1)
                dve.wait_ge(s["pg_ready"], 2 * n + 2)
                for t in range(TT):
                    ts(rank[:, t, bass.ds(e, 1)], rank[:, t, bass.ds(e, 1)], -float(SLOTS), None, ALU.add).then_inc(s["ranks_moved"], 1)
                dve.wait_ge(s["ranks_moved"], 2 * n + 2)
                one_hot(e_next)
                dve.wait_ge(s["gate_done"], n + 1)
                ts(gt, GATE[:, :], 7.0, None, ALU.min).then_inc(s["gt_ready"], 1)
                dve.wait_ge(s["gt_ready"], n + 1)
                dve.wait_ge(s["sig_ready"], n + 1)
                tt(sg, sg, gt, ALU.mult).then_inc(s["swish_ready"], 1)
                dve.wait_ge(s["up_done"], n + 1)
                ts(up, UP[:, :], 7.0, -7.0, ALU.min, ALU.max).then_inc(s["up_read"], 1)
                dve.wait_ge(s["up_read"], n + 1)
                dve.wait_ge(s["swish_ready"], n + 1)
                stt(up, up, 1.0, sg, ALU.add, ALU.mult).then_inc(s["act_ready"], 1)
                dve.wait_ge(s["gathered"], n + 2)
                gathered_times_gain()
                dve.wait_ge(s["down_done"], n + 1)
                dve.wait_ge(s["scattered"], n + 1)
                V.tensor_copy(y, YB[:, :]).then_inc(s["y_ready"], 1)

        @block.tensor
        def _(pe):
            n_all = count(pe)

            def gather():
                for k in range(KD):
                    for i in range(3 * TT):
                        last = mm(GAT[:, k * SLOTS:(k + 1) * SLOTS], parts[:, i // 3, i % 3, k * P:(k + 1) * P], onehot[:, i // 3, :], i == 0, i == 3 * TT - 1)
                last.then_inc(s["gathered"], 1)

            pe.wait_ge(s["bias_in"], 48)
            pe.wait_ge(s["hot_ready"], 2)
            gather()
            with pe.Fori(0, n_all) as n:
                pe.wait_ge(s["xg_ready"], n + 1)
                pe.wait_ge(s["actT_ready"], n + 1)
                for m, (bank, done) in enumerate(((GATE, "gate_done"), (UP, "up_done"))):
                    for k in range(KD):
                        c = 4 * m + k // 2
                        if k % 2 == 0:
                            pe.wait_ge(chunk_in[c], 16 * n + 16)
                        for hf in range(2):
                            last = mm(bank[hf * 64:hf * 64 + 64, :], xg[:, k, :], ring[c][:, k % 2, hf * HF:(hf + 1) * HF], k == 0, False)
                        if k % 2:
                            last.then_inc(s["chunks_used"], 1)
                    pe.wait_ge(s["picked"], n + 1)
                    for hf in range(2):
                        last = mm(bank[hf * 64:hf * 64 + 64, :], pick[0:E, :], bias[0:E, m, hf * HF:(hf + 1) * HF], False, True)
                    last.then_inc(s[done], 1)
                pe.wait_ge(s["gT_ready"], n + 1)
                pe.wait_ge(s["y_ready"], n + 1)
                scatter().then_inc(s["scattered"], 1)
                pe.wait_ge(s["pg_ready"], 2 * n + 2)
                for t in range(TT):
                    last = nc.tensor.transpose(YB[:, t * P:(t + 1) * P], pg[:, t, :], ident)
                last.then_inc(s["gT_done"], 1)
                pe.wait_ge(s["act_ready"], n + 1)
                for k in range(4):
                    last = nc.tensor.transpose(GATE[:, k * P:(k + 1) * P], up[:, k * P:(k + 1) * P], ident)
                last.then_inc(s["actT_done"], 1)
                pe.wait_ge(s["hot_ready"], 2 * n + 4)
                gather()
                pe.wait_ge(s["actT_ready"], n + 2)
                pe.wait_ge(s["gT_ready"], n + 2)
                for k in range(KD):
                    c = 8 + k // 2
                    if k % 2 == 0:
                        pe.wait_ge(chunk_in[c], 16 * n + 16)
                    for hf in range(2):
                        last = mm(YB[hf * 64:hf * 64 + 64, :], actT[:, k % 4, k // 4, :], ring[c][:, k % 2, hf * HF:(hf + 1) * HF], k == 0, False)
                    if k % 2:
                        last.then_inc(s["chunks_used"], 1)
                for hf in range(2):
                    last = mm(YB[hf * 64:hf * 64 + 64, :], pick[0:E, :], bias[0:E, 2, hf * HF:(hf + 1) * HF], False, True)
                last.then_inc(s["down_done"], 1)
    hT2 = un(24, 2).rearrange("p (t k c) -> p t k c", t=TT, k=KD)
    sig = un(35, 2).rearrange("p (t d) -> p t d", d=D)
    scr, scr2 = (un(a, 2).rearrange("p (t d) -> p t d", d=D) for a in (41, 31))
    st2 = un(44)[:, 0:32]
    sums, roots, inv = st2[:, 0:2], st2[:, 4:6], st2[:, 6:8]
    sums2, roots2, inv2 = st2[:, 8:12], st2[:, 12:14], st2[:, 14:16]
    with nc.Block() as block:
        @block.vector
        def _(dve):
            link = chain(dve, "tail")

            def finish(t):
                dve.wait_ge(t2["root2"], t + 1)
                V.reciprocal(inv2[:, t:t + 1], roots2[:, t:t + 1]).then_inc(t2["inverse"], 1)
                dve.wait_ge(t2["inverse"], t + 2)
                dve.wait_ge(t2["fg_in"], 16)
                for hf in range(2):
                    o = slice(hf * HF, (hf + 1) * HF)
                    stt(fin[:, t, o], fin[:, t, o], inv2[:, t:t + 1], fg[:, o], ALU.mult, ALU.mult).then_inc(t2["out_ready"], 1)

            V = nc.vector
            tt, ts, stt = V.tensor_tensor, V.tensor_scalar, V.scalar_tensor_tensor
            for t in range(TT):
                for hf in range(2):
                    dve.wait_ge(t2["scattered"], 2 * t + hf + 1)
                    o = slice(hf * HF, (hf + 1) * HF)
                    tt(fin[:, t, o], x2[:, t, o], banks[2 * t + hf][:, :], ALU.add).then_inc(t2["x3_ready"], 1)
            for n in range(4):
                t, kh = n // 2, n % 2
                dve.wait_ge(t2["turned"], n + 1)
                tt(hT2[:, t, 4 * kh:4 * kh + 4, :], banks[n].rearrange("p (k c) -> p k c", c=P),
                   prm("g_ple")[:, 4 * kh:4 * kh + 4][:, :, None].to_broadcast([P, 4, P]), ALU.mult).then_inc(t2["h_ready"], 1)
            dve.wait_ge(t2["root"], 1)
            V.reciprocal(inv, roots).then_inc(t2["inverse"], 1)
            for n in range(4):
                t, hf = n // 2, n % 2
                o = slice(hf * HF, (hf + 1) * HF)
                dve.wait_ge(t2["sig_ready"], n + 1)
                link(tt(sig[:, t, o], sig[:, t, o], ple[:, n, :], ALU.mult))
                tt(fin[:, t, o], fin[:, t, o], sig[:, t, o], ALU.add).then_inc(t2["x4_ready"], 1)
                if n == 2:
                    finish(0)
            finish(1)

        @block.scalar
        def _(act):
            A = nc.scalar.activation
            eps = par[:, NPARAM:NPARAM + 1]
            for t in range(TT):
                act.wait_ge(t2["x3_ready"], 2 * t + 2)
                A(scr[:, t, :], fin[:, t, :], ACT.Square, accum_out=sums[:, t:t + 1]).then_inc(t2["squared"], 1)
            act.wait_ge(t2["squared"], 2)
            A(roots, sums, ACT.Sqrt, bias=eps, scale=1.0 / D).then_inc(t2["root"], 1)
            for n in range(4):
                t, hf = n // 2, n % 2
                o = slice(hf * HF, (hf + 1) * HF)
                act.wait_ge(t2["gate_done"], n + 1)
                act.wait_ge(t2["inverse"], 1)
                A(sig[:, t, o], banks[n][:, :], ACT.Sigmoid, scale=inv[:, t:t + 1]).then_inc(t2["sig_ready"], 1)
                if hf:
                    A(st2[:, 16 + t:17 + t], par[:, NPARAM:NPARAM + 1], ACT.Sqrt)
                    for m in (n - 1, n):
                        act.wait_ge(t2["x4_ready"], m + 1)
                        A(scr2[:, t, (m % 2) * HF:(m % 2 + 1) * HF], fin[:, t, (m % 2) * HF:(m % 2 + 1) * HF], ACT.Square, accum_out=sums2[:, m:m + 1]).then_inc(t2["squared2"], 1)
                    act.wait_ge(t2["squared2"], 3 * t + 2)
                    A(sums2[:, 2 * t:2 * t + 1], sums2[:, 2 * t:2 * t + 1], ACT.Identity, bias=sums2[:, 2 * t + 1:2 * t + 2]).then_inc(t2["squared2"], 1)
                    act.wait_ge(t2["squared2"], 3 * t + 3)
                    A(roots2[:, t:t + 1], sums2[:, 2 * t:2 * t + 1], ACT.Sqrt, bias=eps, scale=1.0 / D).then_inc(t2["root2"], 1)

        @block.tensor
        def _(pe):
            for t in range(TT):
                for hf in range(2):
                    a = slice(hf * 64, hf * 64 + 64)
                    mm(banks[2 * t + hf][:, :], gT[a, t, :], y[a, :], False, True).then_inc(t2["scattered"], 1)
            for n in range(4):
                t, kh = n // 2, n % 2
                pe.wait_ge(t2["x3_ready"], 2 * t + 2)
                for k in range(4 * kh, 4 * kh + 4):
                    last = nc.tensor.transpose(banks[n][:, (k % 4) * P:(k % 4 + 1) * P], fin[:, t, k * P:(k + 1) * P], ident)
                last.then_inc(t2["turned"], 1)
            pe.wait_ge(t2["gate_w_in"], 64)
            for n in range(4):
                t, hf = n // 2, n % 2
                pe.wait_ge(t2["h_ready"], 2 * t + 2)
                for k in range(KD):
                    last = mm(banks[n][:, :], hT2[:, t, k, :], ring[k // 2][:, k % 2, hf * HF:(hf + 1) * HF], k == 0, k == KD - 1)
                last.then_inc(t2["gate_done"], 1)

        @block.sync
        def _(sp):
            o = io["out"].rearrange("(t p) d -> p t d", p=P)
            for n in range(4):
                t, hf = n // 2, n % 2
                sp.wait_ge(t2["out_ready"], n + 1)
                sp.dma_start(o[:, t, hf * HF:(hf + 1) * HF], fin[:, t, hf * HF:(hf + 1) * HF]).then_inc(t2["out"], 16)
            sp.wait_ge(t2["out"], 16 * 4)


def columns(v):
    return np.ascontiguousarray(np.asarray(v).reshape(-1, P).T)


def lay_out(a):
    f = {k: np.asarray(v) for k, v in a.items()}
    o = {}
    x = f["x"].reshape(T, D)
    o["x"] = x
    o["xT"] = np.ascontiguousarray(x.T)
    o["pT"] = np.ascontiguousarray(f["p"].reshape(T, -1).T)
    o["consts"] = constants()
    dt = np.repeat(f["s5_log_dt"].reshape(NJ, 2), CH, axis=1)
    mw, mr = f["rwkv_mu_wag"][0], f["rwkv_mu_rkv"][0]
    cols = dict(g_mix=f["norm_mix_g"], mu_w=mw[0], mu_a=mw[1], mu_g=mw[2], mu_r=mr[0], mu_k=mr[1], mu_v=mr[2],
                w0=f["rwkv_w0"], a0=f["rwkv_a0"], k_k=f["rwkv_k_k"], k_a=f["rwkv_k_a"], r_k=f["rwkv_r_k"],
                ln_w=f["rwkv_ln_w"], ln_b=f["rwkv_ln_b"], s5_d=f["s5_d"], g_moe=f["norm_moe_g"],
                g_ple=f["norm_ple_g"], lam_re=f["s5_lam_re"], lam_im=f["s5_lam_im"], log_dt=dt)
    o["params"] = np.concatenate([columns(cols[n]) for n in PARAMS], axis=1)
    for n in ("re", "im"):
        b = f["s5_b_" + n].reshape(NJ, 2, CH, 16)
        bd = np.zeros((2, CH, NJ, 2, 16), np.float32)
        c = f["s5_c_" + n].reshape(NJ, 2, 16, CH)
        cd = np.zeros((2, CH, NJ, 2, 16), np.float32)
        for g in range(2):
            bd[g, :, :, g, :] = b[:, g].transpose(1, 0, 2)
            cd[g, :, :, g, :] = c[:, g].transpose(2, 0, 1)
        o["s5_b_" + n] = bd.reshape(P, NJ * 32)
        o["s5_c_" + n] = cd.reshape(P, NJ * 32)
    o["w_in"] = f["w_in"][0]
    o["lora1"] = np.concatenate([f["rwkv_w1"][0], f["rwkv_a1"][0], f["rwkv_g1"][0]], axis=1)
    o["lora2"] = np.concatenate([np.concatenate([f["rwkv_w2"][0], f["rwkv_a2"][0]], axis=0), f["rwkv_g2"][0]], axis=1)
    o["w_glu"] = f["s5_w_glu"][0]
    o["w_out"] = f["w_out"][0]
    o["router_w"] = f["router_w"][0]
    o["router_b"] = f["router_b"].reshape(1, E)
    for n in ("exp_w_gate", "exp_w_up", "exp_w_down", "exp_b_gate", "exp_b_up", "exp_b_down", "ple_w_proj", "ple_w_gate"):
        o[n] = f[n][0]
    o["final_g"] = f["final_norm_g"].reshape(1, D)
    return o


def kernel(**inputs):
    import concourse.bacc as bacc
    from concourse.bass_utils import run_bass_kernel_spmd

    nc = bacc.Bacc("TRN2", target_bir_lowering=False, num_devices=1)
    arrays, io = {}, {}
    for name, a in lay_out(inputs).items():
        a = np.ascontiguousarray(a)
        arrays["in_" + name] = a
        io[name] = nc.dram_tensor("in_" + name, a.shape, mybir.dt.from_np(a.dtype), kind="ExternalInput").ap()
    io["out"] = nc.dram_tensor("out_0", (T, D), F32, kind="ExternalOutput").ap()
    layer(nc, io)
    got = run_bass_kernel_spmd(nc, [arrays], core_ids=[0])
    return got.results[0]["out_0"].reshape(1, T, D)
```

```python
from contextlib import ExitStack

import numpy as np
import concourse.bass as bass
from concourse import mybir

P = 128
T = 256
D = 1024
KD = D // P
W = 512
FT = W // P
TT = T // P
CH = 64
NCH = T // CH
UNITS = NCH * FT
NJ = 16
E = 32
TOPK = 4
SLOTS = 64
MAX_PASS = T // SLOTS
NC = 12
UNIT = 1024
ARENA = 46

F32 = mybir.dt.float32
BF16 = mybir.dt.bfloat16
I32 = mybir.dt.int32
U32 = mybir.dt.uint32
ALU = mybir.AluOpType
ACT = mybir.ActivationFunctionType
AX = mybir.AxisListType

INV_2PI = float(1.0 / (2.0 * np.pi))
ROUND = float(1.5 * 2 ** 23)
PI_A, PI_B = 6.28125, float(2 * np.pi - 6.28125)
PI = 3.1415925
DECAY = float(np.exp(-0.5))

C_ID, C_ONES, C_TRI, C_HEAD, C_IOTA = 0, 128, 256, 384, 512
C_ID2, C_SU, C_UI, C_SU1 = 640, 704, 768, 832
C_LEV = 896
LEVELS = 5
C_TIME = C_LEV + 64 * LEVELS
C_E32 = C_TIME + T
NCONST = C_E32 + E
PARAMS = {}
for _n, _c in (("g_mix", KD), ("mu_w", KD), ("mu_a", KD), ("mu_g", KD), ("mu_r", FT), ("mu_k", FT),
               ("mu_v", FT), ("w0", FT), ("a0", FT), ("k_k", FT), ("k_a", FT), ("r_k", FT),
               ("ln_w", FT), ("ln_b", FT), ("s5_d", FT), ("g_moe", KD), ("g_ple", KD),
               ("lam_re", NJ), ("lam_im", NJ), ("log_dt", NJ)):
    PARAMS[_n] = (sum(c for _, c in PARAMS.values()), _c)
NPARAM = sum(c for _, c in PARAMS.values())


def constants():
    p = np.arange(P)
    c = np.zeros((P, NCONST), np.float32)
    c[:, C_ID:C_ID + P] = np.eye(P)
    c[:, C_ONES:C_ONES + P] = 1.0
    c[:, C_TRI:C_TRI + P] = p[:, None] < p[None, :]
    c[:, C_HEAD:C_HEAD + P] = p[:, None] // CH == p[None, :] // CH
    c[:, C_IOTA:C_IOTA + P] = np.arange(P) % SLOTS
    s, t = p[:, None] % CH, np.arange(CH)[None, :]
    c[:, C_ID2:C_ID2 + CH] = s == t
    c[:, C_SU:C_SU + CH] = s < t
    c[:, C_UI:C_UI + CH] = s <= t
    c[:, C_SU1:C_SU1 + CH] = (s < t) & (s // 2 == t // 2)
    for n in range(LEVELS):
        b = 2 << n
        c[:, C_LEV + n * CH:C_LEV + (n + 1) * CH] = (s // (2 * b) == t // (2 * b)) & (s // b > t // b)
    c[:, C_TIME:C_TIME + T] = np.arange(T)
    c[:, C_E32:C_E32 + E] = np.arange(E)
    return c


def layer(nc, io):
    with ExitStack() as ctx:
        def sb(name, shape, dt=F32):
            return ctx.enter_context(nc.sbuf_tensor(name, shape, dt))

        def sem(name):
            return ctx.enter_context(nc.semaphore(name))

        arena = sb("arena", [P, ARENA * UNIT])
        con = sb("con", [P, NCONST])
        par = sb("par", [P, NPARAM + 2])
        lora_hidden = sb("lora_hidden", [P, 2 * T])
        bb = sb("bb", [P, 2, NJ * 32])
        cc = sb("cc", [P, 2, NJ * 32])
        s5p = sb("s5p", [P, 20, NJ])
        small = sb("small", [P, TT])
        chunk_decay = sb("chunk_decay", [P, FT, NCH])
        u0 = sb("u0", [P, FT * CH])
        uu = sb("uu", [P, FT * CH])
        state = sb("state", [P, FT * CH])
        banks = [ctx.enter_context(nc.psum_tensor(f"bank{i}", [P, 512], F32)) for i in range(8)]

        def un(i, n=1):
            return arena[:, i * UNIT:(i + n) * UNIT]

        def feat(i, n=1):
            return un(i, n).rearrange("p (f t) -> p f t", t=T)

        def units(i):
            return un(i).rearrange("p (u t) -> p u t", t=CH)

        def prm(name):
            a, n = PARAMS[name]
            return par[:, a:a + n]

        ident = con[:, C_ID:C_ID + P]
        ones = con[:, C_ONES:C_ONES + P]
        head_ones = con[:, C_HEAD:C_HEAD + P]

        xT, sq, hT, dh = feat(31, 2), feat(33, 2), feat(35, 2), feat(33, 2)
        xw, xa, xg = feat(37, 2), feat(39, 2), feat(41, 2)
        lora1 = un(26, 2).rearrange("p (k f) -> p k f", k=KD)
        lora2 = un(28)
        wglu = un(29, 2).rearrange("p (k f) -> p k f", k=FT)
        uT = feat(24)
        raw = {"k": feat(43), "r": feat(44), "v": feat(45)}
        S5C, S5S = [feat(16), feat(18)], [feat(17), feat(19)]
        sA, sB, sT1, sT2 = ([feat(a), feat(b)] for a, b in ((20, 2), (21, 3), (22, 26), (23, 27)))
        lw, la, lg = feat(31), feat(32), feat(33)
        tmp = feat(34)
        rr, kx, vv = feat(37), feat(38), feat(39)
        kkn, k2, kb, bonus = feat(40), feat(41), feat(42), feat(43)
        Lc, EL = feat(0), feat(1)
        kksq, rk = feat(8), feat(9)
        at, bh, kh, rt = feat(31), feat(42), feat(5), feat(37)
        Vs, Bs, Ks = units(32), units(4), units(35)
        X, Y, Wk, Mx, MO = units(36), units(38), units(40), units(44), units(45)
        KA, RB, RK = units(6), units(7), units(28)
        yT = feat(45)
        yc, ysq, yrs = feat(44), feat(38), feat(40)
        ys5 = feat(25)
        mix_s5, mix_rw = feat(24), feat(35)
        x_tok = un(31, 2).rearrange("p (t d) -> p t d", d=D)
        x2 = x_tok
        wout = [un(8 + 2 * c, 2).rearrange("p (k n) -> p k n", n=D) for c in range(4)]
        ring = [un(2 * c, 2).rearrange("p (k n) -> p k n", n=D) for c in range(NC)]
        win = [un(2 * c, 2).rearrange("p (k n) -> p k n", n=T) for c in range(8)]

        pT = lora_hidden.rearrange("p (k t) -> p k t", k=2)
        wproj = un(29, 2).rearrange("p (k n) -> p k n", n=D)
        router = un(41)[:, 0:KD * E].rearrange("p (k e) -> p k e", k=KD)
        x2T = un(27, 2).rearrange("p (k t) -> p k t", k=KD)
        logits = [banks[6][:, 0:E], banks[7][:, 0:E]]
        ssq = small[:, 0:TT]

        s = {n: sem(n) for n in (
            "consts_in", "s5_in", "xT_in", "lora_in", "glu_in", "x_in",
            "eps_ready", "sq_ready", "rms_summed", "rms_root", "kk_root", "var_root", "h_ready", "mixed", "mixed_g", "dh_ready", "proj_done", "proj_copied",
            "lora1_done", "lora_hidden_ready", "lora2_done", "lora2_copied",
            "s5_dt", "s5_arg", "s5_mag", "s5_theta", "s5_sin", "bb_ready", "bb_turned", "bb_copied",
            "table_arg", "table_angle", "table_sin", "table_ready", "bu_done", "bu_copied", "phase_off",
            "scanned", "phase_on", "s5_out_done", "s5_y", "s5_gelu", "glu_done", "glu_sig", "mix_s5_ready",
            "kk_ready", "kk_squared", "kk_summed", "decay_ready", "exp_ready", "scaled", "rk_ready",
            "rk_summed", "bonus_ready", "scores_done", "scores_copied", "turned", "y_turned",
            "w_done", "w_copied", "xy_done", "xy_ready", "mo_ready",
            "u0_done", "u0_ready", "u_done", "u_ready", "state_done", "state_ready", "y_done", "y_copied",
            "mean_done", "centred", "y_squared", "var_done", "mix_rw_ready",
            "out_done", "x2_turned", "x2T_ready", "x2_ready",
            "dve_chain", "act_chain", "pool_chain")}
        win_in = [sem("win_in_u0"), sem("win_in_u1")] + [x for n in "rkv" for x in [sem("win_in_" + n)] * 2]
        wout_in = sem("wout_in")
        p_in = sem("p_in")
        chunk_in = [sem(f"chunk_in{c}") for c in range(NC)]

        def chain(eng, name):
            n = [0]

            def link(ins):
                n[0] += 1
                ins.then_inc(s[name], 1)
                eng.wait_ge(s[name], n[0])
            return link

        def mm(out, lhsT, rhs, start, stop):
            return nc.tensor.matmul(out, lhsT, rhs, start=start, stop=stop, skip_group_check=True)

        def pair(out, lhsT, rhs, start=True, stop=True):
            for h in range(2):
                a = slice(h * CH, (h + 1) * CH)
                last = mm(out[a], lhsT[a], rhs[a], start, stop)
            return last

        OUT_BANK = (2, 3, 0, 1)
        SCORE_BANK = (4, 6, 0, 4, 6)

        def turn_x2(t, half):
            for k in range(4 * half, 4 * half + 4):
                last = nc.tensor.transpose(banks[4 + half][:, (k % 4) * P:(k % 4 + 1) * P], x2[:, t, k * P:(k + 1) * P], ident)
            return last

        order = [0, 1, 4, 5, 2, 3, 6, 7]
        expert_weights = [io["exp_w_gate"], io["exp_w_up"], io["exp_w_down"]]

        def chunk_src(c, e):
            w = expert_weights[c // 4]
            k = 2 * (c % 4)
            return w[bass.ds(e, 1), k * P:(k + 2) * P, :].rearrange("o (k p) n -> p (o k) n", p=P)

        with nc.Block() as block:
            @block.sync
            def _(sp):
                sp.dma_start(xT[:, :, :], io["xT"].rearrange("(k p) t -> p k t", p=P)).then_inc(s["xT_in"], 16)
                sp.dma_start(con[:, :], io["consts"]).then_inc(s["consts_in"], 16)
                sp.dma_start(par[:, 0:NPARAM], io["params"]).then_inc(s["consts_in"], 16)
                w = io["w_in"].rearrange("(k p) n -> p k n", p=P)
                for n, q in enumerate(order):
                    sp.dma_start(win[q][:, :, :], w[:, :, q * T:(q + 1) * T]).then_inc(win_in[q], 16)
                    if n == 1:
                        sp.dma_start(lora1[:, :, :], io["lora1"].rearrange("(k p) n -> p k n", p=P)).then_inc(s["lora_in"], 16)
                        sp.dma_start(lora2[:, :], io["lora2"]).then_inc(s["lora_in"], 16)
                sp.dma_start(wglu[:, :, :], io["w_glu"].rearrange("(k p) n -> p k n", p=P)).then_inc(s["glu_in"], 16)
                sp.wait_ge(s["proj_done"], 8)
                wo = io["w_out"].rearrange("(c k p) n -> c p k n", p=P, k=2)
                for c in (1, 2, 3):
                    sp.dma_start(wout[c][:, :, :], wo[c]).then_inc(wout_in, 16)
                sp.wait_ge(s["scaled"], 3)
                sp.dma_start(ring[0][:, :, :], chunk_src(0, 0)).then_inc(chunk_in[0], 16)
                sp.wait_ge(s["rk_summed"], 1)
                sp.dma_start(router[:, :, :], io["router_w"].rearrange("(k p) e -> p k e", p=P)).then_inc(s["glu_in"], 16)
                sp.dma_start(wout[0][:, :, :], wo[0]).then_inc(wout_in, 16)
                sp.wait_ge(s["phase_on"], 4)
                sp.wait_ge(s["s5_out_done"], 4)
                for c in (1, *range(8, NC)):
                    sp.dma_start(ring[c][:, :, :], chunk_src(c, 0)).then_inc(chunk_in[c], 16)
                sp.wait_ge(s["lora2_done"], 6)
                sp.dma_start(pT[:, :, :], io["pT"].rearrange("(k p) t -> p k t", p=P)).then_inc(p_in, 16)
                sp.wait_ge(s["glu_done"], 2)
                sp.dma_start(wproj[:, :, :], io["ple_w_proj"].rearrange("(k p) n -> p k n", p=P)).then_inc(p_in, 16)
                sp.wait_ge(s["u0_done"], NCH)
                sp.wait_ge(s["y_done"], NCH)
                sp.wait_ge(s["state_done"], NCH - 1)
                sp.dma_start(x_tok[:, :, :], io["x"].rearrange("(t p) d -> p t d", p=P)).then_inc(s["x_in"], 16)
                for c in (2, 3):
                    sp.dma_start(ring[c][:, :, :], chunk_src(c, 0)).then_inc(chunk_in[c], 16)

            @block.gpsimd
            def _(pool):
                link = chain(pool, "pool_chain")
                pool.dma_start(bb[:, 0, :], io["s5_b_re"]).then_inc(s["s5_in"], 16)
                pool.dma_start(bb[:, 1, :], io["s5_b_im"]).then_inc(s["s5_in"], 16)
                pool.dma_start(cc[:, 0, :], io["s5_c_re"]).then_inc(s["s5_in"], 16)
                pool.dma_start(cc[:, 1, :], io["s5_c_im"]).then_inc(s["s5_in"], 16)
                tt = nc.gpsimd.tensor_tensor
                pool.wait_ge(s["dh_ready"], 1)
                pool.wait_ge(s["h_ready"], KD)
                link(tt(xg, dh, prm("mu_g")[:, :, None].to_broadcast([P, KD, T]), ALU.mult))
                tt(xg, xg, hT, ALU.add).then_inc(s["mixed_g"], 1)

                def phase_off(g):
                    c, sn, a, b, t1, t2 = (x[g % 2] for x in (S5C, S5S, sA, sB, sT1, sT2))
                    pool.wait_ge(s["bu_copied"], 4 * (g + 1))
                    pool.wait_ge(s["table_ready"], g + 1)
                    if g == 1:
                        pool.wait_ge(s["lora1_done"], 3)
                    if g >= 2:
                        pool.wait_ge(s["s5_out_done"], g - 1)
                    tt(t1, a, c, ALU.mult)
                    link(tt(t2, b, sn, ALU.mult))
                    link(tt(t1, t1, t2, ALU.add))
                    link(tt(t2, a, sn, ALU.mult))
                    link(tt(a, b, c, ALU.mult))
                    tt(t2, a, t2, ALU.subtract).then_inc(s["phase_off"], 1)

                def phase_on(g):
                    c, sn, a, b, t1, t2 = (x[g % 2] for x in (S5C, S5S, sA, sB, sT1, sT2))
                    pool.wait_ge(s["scanned"], g + 1)
                    tt(t1, a, c, ALU.mult)
                    link(tt(t2, b, sn, ALU.mult))
                    link(tt(t1, t1, t2, ALU.subtract))
                    link(tt(t2, a, sn, ALU.mult))
                    link(tt(a, b, c, ALU.mult))
                    tt(t2, a, t2, ALU.add).then_inc(s["phase_on"], 1)

                for g in (0, 2):
                    phase_off(g)
                    phase_off(g + 1)
                    phase_on(g)
                    phase_on(g + 1)

            @block.scalar
            def _(act):
                link = chain(act, "act_chain")
                A = nc.scalar.activation
                act.wait_ge(s["xT_in"], 16)
                for b in range(2):
                    A(sq[:, 4 * b:4 * b + 4, :], xT[:, 4 * b:4 * b + 4, :], ACT.Square).then_inc(s["sq_ready"], 1)
                act.wait_ge(s["consts_in"], 32)
                A(s5p[:, 0, :], prm("log_dt"), ACT.Exp).then_inc(s["s5_dt"], 1)
                act.wait_ge(s["s5_arg"], 1)
                A(s5p[:, 4, :], s5p[:, 2, :], ACT.Exp).then_inc(s["s5_mag"], 1)
                act.wait_ge(s["s5_theta"], 1)
                A(s5p[:, 7, :], s5p[:, 5, :], ACT.Sin)
                A(s5p[:, 8, :], s5p[:, 5, :], ACT.Sin, scale=0.5).then_inc(s["s5_sin"], 1)
                act.wait_ge(s["rms_summed"], 1)
                act.wait_ge(s["eps_ready"], 1)
                A(un(43)[:, 0:T], banks[7][:, 0:T], ACT.Sqrt, bias=par[:, NPARAM:NPARAM + 1], scale=1.0 / D).then_inc(s["rms_root"], 1)
                act.wait_ge(s["s5_in"], 64)
                A(cc[:, 1, :], cc[:, 1, :], ACT.Copy, scale=-1.0).then_inc(s["bb_copied"], 1)

                def copy_proj(n):
                    q = order[n]
                    act.wait_ge(s["proj_done"], n + 1)
                    if q < 2:
                        dst = uT[:, 2 * q:2 * q + 2, :]
                    else:
                        dst = raw["rkv"[(q - 2) // 2]][:, 2 * (q % 2):2 * (q % 2) + 2, :]
                    A(dst, banks[n % 2][:, :].rearrange("p (f t) -> p f t", t=T), ACT.Copy).then_inc(s["proj_copied"], 1)

                def table_angle(g):
                    if g >= 2:
                        act.wait_ge(s["phase_on"], g - 1)
                    for j in range(4):
                        last = A(S5S[g % 2][:, j, :], con[:, C_TIME:C_TIME + T], ACT.Copy, scale=s5p[:, 5, 4 * g + j:4 * g + j + 1])
                    last.then_inc(s["table_angle"], 1)

                def table_sin(g):
                    act.wait_ge(s["table_arg"], g + 1)
                    A(S5C[g % 2][:, :, :], S5S[g % 2][:, :, :], ACT.Sin, scale=0.5)
                    A(S5S[g % 2][:, :, :], S5S[g % 2][:, :, :], ACT.Sin).then_inc(s["table_sin"], 1)

                def bu_copy(g):
                    for j in range(4):
                        act.wait_ge(s["bu_done"], 4 * g + j + 1)
                        if g >= 2 and j == 0:
                            act.wait_ge(s["phase_on"], g - 1)
                        A(sA[g % 2][:, j, :], banks[2 + j % 2][:, 0:T], ACT.Copy)
                        A(sB[g % 2][:, j, :], banks[2 + j % 2][:, T:2 * T], ACT.Copy).then_inc(s["bu_copied"], 1)

                table_angle(0)
                table_angle(1)
                for n in range(2):
                    copy_proj(n)
                act.wait_ge(s["lora1_done"], 2)
                A(lora_hidden[0:CH, 0:T], banks[4][0:CH, 0:T], ACT.Tanh)
                A(lora_hidden[CH:P, 0:T], banks[4][CH:P, 0:T], ACT.Copy).then_inc(s["lora_hidden_ready"], 1)
                table_sin(0)
                bu_copy(0)
                act.wait_ge(s["lora1_done"], 3)
                A(lora_hidden[:, T:2 * T], banks[7][:, 0:T], ACT.Sigmoid).then_inc(s["lora_hidden_ready"], 1)
                for m, (dst, bias) in enumerate(((lw, "w0"), (la, "a0"), (lg, None))):
                    if m == 0:
                        act.wait_ge(s["h_ready"], KD)
                    if m == 2:
                        act.wait_ge(s["mixed"], 2)
                        act.wait_ge(s["mixed_g"], 1)
                    for i in range(FT):
                        if i % 2 == 0:
                            act.wait_ge(s["lora2_done"], 2 * m + i // 2 + 1)
                        src = banks[5 + i // 2][:, (i % 2) * T:(i % 2 + 1) * T]
                        if bias:
                            last = A(dst[:, i, :], src, ACT.Sigmoid, bias=prm(bias)[:, i:i + 1])
                        else:
                            last = A(dst[:, i, :], src, ACT.Copy)
                        if i % 2:
                            last.then_inc(s["lora2_copied"], 1)
                table_sin(1)
                bu_copy(1)
                act.wait_ge(s["lora1_done"], 3)
                copy_proj(2)
                act.wait_ge(s["decay_ready"], 1)
                A(EL[:, :, :], Lc[:, :, :], ACT.Exp)
                link(A(chunk_decay[:, :, :], Lc[:, :, CH - 1::CH], ACT.Exp))
                A(Lc[:, :, :], Lc[:, :, :], ACT.Exp, scale=-1.0)
                A(lw[:, :, :], lw[:, :, :], ACT.Exp).then_inc(s["exp_ready"], 1)
                copy_proj(3)
                act.wait_ge(s["kk_ready"], 1)
                A(kksq[:, :, :], kkn[:, :, :], ACT.Square).then_inc(s["kk_squared"], 1)
                copy_proj(4)
                act.wait_ge(s["kk_summed"], 1)
                for b in range(2):
                    m = A(kb[:, 2 * b:2 * b + 2, :], banks[4 + b].rearrange("p (f t) -> p f t", t=T), ACT.Sqrt)
                m.then_inc(s["kk_root"], 1)
                copy_proj(5)
                table_angle(2)
                copy_proj(6)
                bu_copy(2)
                copy_proj(7)
                table_sin(2)
                table_angle(3)
                table_sin(3)
                bu_copy(3)
                for lev in range(LEVELS):
                    for b in range(2):
                        act.wait_ge(s["w_done"], 2 * lev + b + 1)
                        A(Wk[:, 8 * b:8 * b + 8, :], banks[4 + b].rearrange("p (u t) -> p u t", t=CH), ACT.Copy).then_inc(s["w_copied"], 1)
                act.wait_ge(s["s5_y"], 4)
                A(ys5[:, :, :], ys5[:, :, :], ACT.Gelu_apprx_tanh).then_inc(s["s5_gelu"], 1)
                for c in range(NCH):
                    act.wait_ge(s["u0_done"], c + 1)
                    A(u0[:, :], banks[0][:, 0:FT * CH], ACT.Copy).then_inc(s["u0_ready"], 1)
                    if c == 3:
                        act.wait_ge(s["centred"], 1)
                        A(ysq[:, :, 0:P], yc[:, :, 0:P], ACT.Square).then_inc(s["y_squared"], 1)
                    act.wait_ge(s["u_done"], c + 1)
                    A(uu[:, :], banks[1][:, 0:FT * CH], ACT.Copy).then_inc(s["u_ready"], 1)
                    act.wait_ge(s["y_done"], c + 1)
                    if c == 0:
                        act.wait_ge(s["w_done"], 2 * LEVELS)
                    A(yT[:, :, c * CH:(c + 1) * CH], banks[5][:, 0:FT * CH].rearrange("p (f t) -> p f t", t=CH), ACT.Copy).then_inc(s["y_copied"], 1)
                    if c < 2:
                        b = c
                        act.wait_ge(s["glu_done"], b + 1)
                        act.wait_ge(s["s5_y"], 4)
                        A(mix_s5[:, 2 * b:2 * b + 2, :], banks[2 + b].rearrange("p (f t) -> p f t", t=T), ACT.Sigmoid).then_inc(s["glu_sig"], 1)
                for t in range(TT):
                    o = slice(t * P, (t + 1) * P)
                    if t:
                        act.wait_ge(s["centred"], 2)
                        A(ysq[:, :, o], yc[:, :, o], ACT.Square).then_inc(s["y_squared"], 1)
                    act.wait_ge(s["var_done"], t + 1)
                    A(yrs[:, :, o], banks[7].rearrange("p (f t) -> p f t", t=P), ACT.Sqrt,
                      bias=par[:, NPARAM + 1:NPARAM + 2], scale=1.0 / CH).then_inc(s["var_root"], 1)
                for t in range(TT):
                    act.wait_ge(s["x2_ready"], 2 * t + 2)
                    A(un(33 + t), x2[:, t, :], ACT.Square, accum_out=ssq[:, t:t + 1])
                    if t == 0:
                        for k in range(KD):
                            act.wait_ge(s["x2_turned"], k // 4 + 1)
                            last = A(x2T[:, k, 0:P], banks[4 + k // 4][:, (k % 4) * P:(k % 4 + 1) * P], ACT.Copy, scale=prm("g_moe")[:, k:k + 1])
                        last.then_inc(s["x2T_ready"], 1)

            @block.vector
            def _(dve):
                link = chain(dve, "dve_chain")
                V = nc.vector
                tt, ts, stt = V.tensor_tensor, V.tensor_scalar, V.scalar_tensor_tensor

                def reduce_angle(dst, turns, arg):
                    link(ts(turns, arg, INV_2PI, ROUND, ALU.mult, ALU.add))
                    link(ts(turns, turns, -ROUND, None, ALU.add))
                    link(stt(dst, turns, -PI_A, arg, ALU.mult, ALU.add))
                    link(stt(dst, turns, -PI_B, dst, ALU.mult, ALU.add))

                V.memset(par[:, NPARAM:NPARAM + 1], 1e-6)
                V.memset(par[:, NPARAM + 1:NPARAM + 2], 64e-5).then_inc(s["eps_ready"], 1)
                lre, lim = s5p[:, 1, :], prm("lam_im")
                dve.wait_ge(s["consts_in"], 32)
                link(ts(lre, prm("lam_re"), -1e-4, None, ALU.min))
                dve.wait_ge(s["s5_dt"], 1)
                tt(s5p[:, 2, :], lre, s5p[:, 0, :], ALU.mult).then_inc(s["s5_arg"], 1)
                link(tt(s5p[:, 3, :], lim, s5p[:, 0, :], ALU.mult))
                reduce_angle(s5p[:, 5, :], s5p[:, 6, :], s5p[:, 3, :])
                ts(s5p[:, 5, :], s5p[:, 5, :], PI, -PI, ALU.min, ALU.max).then_inc(s["s5_theta"], 1)
                dve.wait_ge(s["s5_sin"], 1)
                dve.wait_ge(s["s5_mag"], 1)
                sh2, cs, lbr, lbi, zre = (s5p[:, i, :] for i in range(9, 14))
                den, ca, cb, cr, ci = (s5p[:, i, :] for i in range(14, 19))
                link(tt(sh2, s5p[:, 8, :], s5p[:, 8, :], ALU.mult))
                link(ts(cs, sh2, -2.0, 1.0, ALU.mult, ALU.add))
                link(tt(lbr, s5p[:, 4, :], cs, ALU.mult))
                link(tt(lbi, s5p[:, 4, :], s5p[:, 7, :], ALU.mult))
                link(ts(zre, lbr, -1.0, None, ALU.add))
                link(tt(ca, lre, lre, ALU.mult))
                link(tt(cb, lim, lim, ALU.mult))
                link(tt(den, ca, cb, ALU.add))
                link(V.reciprocal(den, den))
                link(tt(ca, zre, lre, ALU.mult))
                link(tt(cb, lbi, lim, ALU.mult))
                link(tt(ca, ca, cb, ALU.add))
                link(tt(cr, ca, den, ALU.mult))
                link(tt(ca, lbi, lre, ALU.mult))
                link(tt(cb, zre, lim, ALU.mult))
                link(tt(ca, ca, cb, ALU.subtract))
                link(tt(ci, ca, den, ALU.mult))
                dve.wait_ge(s["rms_root"], 1)
                link(V.reciprocal(un(43)[:, 0:T], un(43)[:, 0:T]))
                for k in range(KD):
                    stt(hT[:, k, :], xT[:, k, :], prm("g_mix")[:, k:k + 1], un(43)[:, 0:T], ALU.mult, ALU.mult).then_inc(s["h_ready"], 1)
                dve.wait_ge(s["h_ready"], KD)
                tt(dh[:, :, 1:T], hT[:, :, 0:T - 1], hT[:, :, 1:T], ALU.subtract)
                ts(dh[:, :, 0:1], hT[:, :, 0:1], -1.0, None, ALU.mult).then_inc(s["dh_ready"], 1)
                dve.wait_ge(s["dh_ready"], 1)
                for dst, mu in ((xw, "mu_w"), (xa, "mu_a")):
                    for k in range(KD):
                        m = stt(dst[:, k, :], dh[:, k, :], prm(mu)[:, k:k + 1], hT[:, k, :], ALU.mult, ALU.add)
                    m.then_inc(s["mixed"], 1)
                dve.wait_ge(s["s5_in"], 64)
                bre = bb[:, 0, :].rearrange("p (j c) -> p j c", j=NJ)
                bim = bb[:, 1, :].rearrange("p (j c) -> p j c", j=NJ)
                crb = cr[:, :, None].to_broadcast([P, NJ, 32])
                cib = ci[:, :, None].to_broadcast([P, NJ, 32])
                q1, q2, q3 = (un(44, 2)[:, i * 512:(i + 1) * 512].rearrange("p (j c) -> p j c", j=NJ) for i in range(3))
                link(tt(q1, bre, crb, ALU.mult))
                link(tt(q2, bim, cib, ALU.mult))
                link(tt(q1, q1, q2, ALU.subtract))
                link(tt(q2, bim, crb, ALU.mult))
                link(tt(q3, bre, cib, ALU.mult))
                link(V.tensor_copy(bre, q1))
                tt(bim, q2, q3, ALU.add).then_inc(s["bb_ready"], 1)
                def table_arg(g):
                    c, sn = S5C[g % 2], S5S[g % 2]
                    dve.wait_ge(s["table_angle"], g + 1)
                    if g >= 2:
                        dve.wait_ge(s["phase_on"], g - 1)
                    reduce_angle(sn, c, sn)
                    ts(sn, sn, PI, -PI, ALU.min, ALU.max).then_inc(s["table_arg"], 1)

                def table_cos(g):
                    c = S5C[g % 2]
                    dve.wait_ge(s["table_sin"], g + 1)
                    link(tt(c, c, c, ALU.mult))
                    ts(c, c, -2.0, 1.0, ALU.mult, ALU.add).then_inc(s["table_ready"], 1)

                def scan(g):
                    dve.wait_ge(s["phase_off"], g + 1)
                    for j in range(4):
                        mag = s5p[:, 4, 4 * g + j:4 * g + j + 1].to_broadcast([P, T])
                        V.tensor_tensor_scan(sA[g % 2][:, j, :], mag, sT1[g % 2][:, j, :], 0.0, ALU.mult, ALU.add)
                        z = V.tensor_tensor_scan(sB[g % 2][:, j, :], mag, sT2[g % 2][:, j, :], 0.0, ALU.mult, ALU.add)
                    z.then_inc(s["scanned"], 1)

                def s5_y(g):
                    dve.wait_ge(s["s5_out_done"], g + 1)
                    stt(ys5[:, g, :], uT[:, g, :], prm("s5_d")[:, g:g + 1], banks[2 + g % 2][:, 0:T], ALU.mult, ALU.add).then_inc(s["s5_y"], 1)

                def token_shift(name, dst):
                    src = raw[name]
                    tt(tmp[:, :, 1:T], src[:, :, 0:T - 1], src[:, :, 1:T], ALU.subtract)
                    link(ts(tmp[:, :, 0:1], src[:, :, 0:1], -1.0, None, ALU.mult))
                    for i in range(FT):
                        m = stt(dst[:, i, :], tmp[:, i, :], prm("mu_" + name)[:, i:i + 1], src[:, i, :], ALU.mult, ALU.add)
                    return m

                table_arg(0)
                dve.wait_ge(s["bb_turned"], 1)
                V.tensor_copy(bb[:, 0, :], banks[5][:, :])
                V.tensor_copy(bb[:, 1, :], banks[6][:, :]).then_inc(s["bb_copied"], 1)
                table_arg(1)
                table_cos(0)
                dve.wait_ge(s["proj_done"], 1)
                link(V.memset(EL, 1.0))
                link(V.memset(EL[:, :, 0::CH], 0.0))
                dve.wait_ge(s["lora2_copied"], 2)
                link(ts(lw, lw, -DECAY, None, ALU.mult))
                link(V.tensor_tensor_scan(un(0), un(1), un(31), 0.0, ALU.mult, ALU.add))
                tt(lw, Lc, lw, ALU.subtract).then_inc(s["decay_ready"], 1)
                table_cos(1)
                scan(0)
                dve.wait_ge(s["proj_copied"], 4)
                dve.wait_ge(s["lora1_done"], 3)
                link(token_shift("k", kx))
                for i in range(FT):
                    m = ts(kkn[:, i, :], kx[:, i, :], prm("k_k")[:, i:i + 1], None, ALU.mult)
                m.then_inc(s["kk_ready"], 1)
                dve.wait_ge(s["kk_ready"], 1)
                dve.wait_ge(s["lora2_copied"], 4)
                link(ts(k2, la, -1.0, None, ALU.add))
                for i in range(FT):
                    m = ts(k2[:, i, :], k2[:, i, :], prm("k_a")[:, i:i + 1], 1.0, ALU.mult, ALU.add)
                link(m)
                link(tt(k2, k2, kx, ALU.mult))
                scan(1)
                dve.wait_ge(s["kk_root"], 1)
                link(ts(kb, kb, 1e-12, None, ALU.max))
                link(V.reciprocal(kb, kb))
                link(tt(kkn, kkn, kb, ALU.mult))
                link(tt(kb, kkn, la, ALU.mult))
                s5_y(0)
                dve.wait_ge(s["exp_ready"], 1)
                stt(un(31), un(31), -1.0, un(40), ALU.mult, ALU.mult)
                tt(bh, kb, Lc, ALU.mult).then_inc(s["scaled"], 1)
                dve.wait_ge(s["proj_done"], 5)
                tt(kh, k2, Lc, ALU.mult).then_inc(s["scaled"], 1)
                table_arg(2)
                dve.wait_ge(s["proj_copied"], 6)
                link(token_shift("r", rr))
                link(tt(rk, rr, k2, ALU.mult))
                tt(rt, rr, EL, ALU.mult).then_inc(s["scaled"], 1)
                V.memset(state[:, :], 0.0)
                table_cos(2)
                def col(c):
                    return con[:, c:c + CH][:, None, :].to_broadcast([P, 8, CH])
                eye = col(C_ID2)

                def level_mask(lev, b):
                    lm = con[:, C_LEV + lev * CH:C_LEV + (lev + 1) * CH][:, None, :].to_broadcast([P, 8, CH])
                    tt(MO[:, 8 * b:8 * b + 8, :], Mx[:, 8 * b:8 * b + 8, :], lm, ALU.mult).then_inc(s["mo_ready"], 1)

                def turn_x(b):
                    return V.transpose(Y[:, 8 * b:8 * b + 8, :], X[:, 8 * b:8 * b + 8, :])

                def turn(dst, src):
                    for h in range(2):
                        for i in range(2):
                            for j in range(2):
                                a, o = h * CH + 32 * i, h * CH + 32 * j
                                m = V.transpose(dst[o:o + 32].rearrange("p (c f) (i k) -> p f c i k", c=NCH, i=2)[:, :, :, i, :],
                                                src[a:a + 32].rearrange("p f (c j k) -> p f c j k", c=NCH, j=2)[:, :, :, j, :])
                    m.then_inc(s["turned"], 1)

                for m, (dst, mask) in enumerate(((X, C_SU1), (Mx, None), (KA, C_SU), (RB, C_UI), (RK, C_UI))):
                    for b in range(2):
                        dve.wait_ge(s["scores_done"], 2 * m + b + 1)
                        src = banks[SCORE_BANK[m] + b].rearrange("p (u t) -> p u t", t=CH)
                        d = dst[:, 8 * b:8 * b + 8, :]
                        if m == 1:
                            V.tensor_copy(d, src).then_inc(s["scores_copied"], 1)
                        elif m == 0:
                            link(tt(d, src, col(mask), ALU.mult))
                            link(tt(d, d, eye, ALU.add))
                            turn_x(b).then_inc(s["scores_copied"], 1)
                        else:
                            tt(d, src, col(mask), ALU.mult).then_inc(s["scores_copied"], 1)
                    if m == 0:
                        for i in range(FT):
                            last = ts(rk[:, i, :], rk[:, i, :], prm("r_k")[:, i:i + 1], None, ALU.mult)
                        last.then_inc(s["rk_ready"], 1)
                        table_arg(3)
                    if m == 1:
                        s5_y(1)
                dve.wait_ge(s["proj_copied"], 8)
                token_shift("v", vv).then_inc(s["scaled"], 1)
                dve.wait_ge(s["scaled"], 4)
                dve.wait_ge(s["scores_copied"], 4)
                for b in range(2):
                    level_mask(0, b)
                table_cos(3)
                dve.wait_ge(s["rk_summed"], 1)
                for b in range(2):
                    m = tt(bonus[:, 2 * b:2 * b + 2, :], banks[b].rearrange("p (f t) -> p f t", t=T), vv[:, 2 * b:2 * b + 2, :], ALU.mult)
                m.then_inc(s["bonus_ready"], 1)
                scan(2)
                for lev in range(LEVELS):
                    for b in range(2):
                        if lev < LEVELS - 1:
                            dve.wait_ge(s["w_done"], 2 * lev + b + 1)
                            level_mask(lev + 1, b)
                    for b in range(2):
                        dve.wait_ge(s["xy_done"], 2 * lev + b + 1)
                        d = X[:, 8 * b:8 * b + 8, :]
                        tt(d, d, banks[6 + b].rearrange("p (u t) -> p u t", t=CH), ALU.add).then_inc(s["xy_ready"], 1)
                        if lev < LEVELS - 1:
                            dve.wait_ge(s["xy_ready"], 2 * lev + b + 1)
                            turn_x(b).then_inc(s["y_turned"], 1)
                    if lev == 0:
                        scan(3)
                    if lev in (1, 2, 3):
                        turn(*((Bs, bh), (Ks, kh), (Vs, vv))[lev - 1])
                    if lev in (2, 3):
                        s5_y(lev)

                def glu_gate(b):
                    dve.wait_ge(s["glu_sig"], b + 1)
                    tt(mix_s5[:, 2 * b:2 * b + 2, :], mix_s5[:, 2 * b:2 * b + 2, :], ys5[:, 2 * b:2 * b + 2, :], ALU.mult).then_inc(s["mix_s5_ready"], 1)

                def centre(t):
                    o = slice(t * P, (t + 1) * P)
                    dve.wait_ge(s["mean_done"], t + 1)
                    stt(yc[:, :, o], banks[6].rearrange("p (f t) -> p f t", t=P), -1.0 / CH, yT[:, :, o], ALU.mult, ALU.add).then_inc(s["centred"], 1)

                def normalise(t):
                    o = slice(t * P, (t + 1) * P)
                    dve.wait_ge(s["centred"], t + 1)
                    dve.wait_ge(s["var_root"], t + 1)
                    link(V.reciprocal(yrs[:, :, o], yrs[:, :, o]))
                    link(tt(yc[:, :, o], yc[:, :, o], yrs[:, :, o], ALU.mult))
                    for i in range(FT):
                        m = ts(yc[:, i, o], yc[:, i, o], prm("ln_w")[:, i:i + 1], prm("ln_b")[:, i:i + 1], ALU.mult, ALU.add)
                    link(m)
                    link(tt(yc[:, :, o], yc[:, :, o], bonus[:, :, o], ALU.add))
                    tt(mix_rw[:, :, o], yc[:, :, o], lg[:, :, o], ALU.mult).then_inc(s["mix_rw_ready"], 1)

                for c in range(NCH - 1):
                    dve.wait_ge(s["state_done"], c + 1)
                    dve.wait_ge(s["y_done"], c + 1)
                    link(tt(state[:, :], banks[4][:, 0:FT * CH], state[:, :], ALU.add))
                    tt(state[:, :].rearrange("p (f v) -> p f v", v=CH), state[:, :].rearrange("p (f v) -> p f v", v=CH),
                       chunk_decay[:, :, c:c + 1].to_broadcast([P, FT, CH]), ALU.mult).then_inc(s["state_ready"], 1)
                    if c < 2:
                        glu_gate(c)
                centre(0)
                centre(1)
                normalise(0)
                normalise(1)
                dve.wait_ge(s["x_in"], 16)
                for t in range(TT):
                    for hf in range(2):
                        n = 2 * t + hf
                        dve.wait_ge(s["out_done"], n + 1)
                        tt(x2[:, t, hf * 512:(hf + 1) * 512], x_tok[:, t, hf * 512:(hf + 1) * 512], banks[OUT_BANK[n]][:, :], ALU.add).then_inc(s["x2_ready"], 1)

            @block.tensor
            def _(pe):
                pe.wait_ge(s["consts_in"], 32)
                for k in range(KD):
                    pe.wait_ge(s["sq_ready"], k // 4 + 1)
                    last = mm(banks[7][:, 0:T], ones, sq[:, k, :], k == 0, k == KD - 1)
                last.then_inc(s["rms_summed"], 1)
                def bu_tile(g, j):
                    if g == 0 and j == 0:
                        pe.wait_ge(s["bb_copied"], 2)
                        pe.wait_ge(s["proj_copied"], 2)
                    if g >= 2 and j == 0:
                        pe.wait_ge(s["s5_y"], g - 1)
                    if 4 * g + j >= 2:
                        pe.wait_ge(s["bu_copied"], 4 * g + j - 1)
                    a = slice(32 * j, 32 * j + 32)
                    for m in range(2):
                        last = mm(banks[2 + j % 2][:, m * T:(m + 1) * T], bb[a, m, g * P:(g + 1) * P], uT[a, g, :], True, True)
                    last.then_inc(s["bu_done"], 1)

                def project(n, group=None):
                    q = order[n]
                    pe.wait_ge(win_in[q], 16 if q < 2 else 32)
                    if n >= 2:
                        pe.wait_ge(s["proj_copied"], n - 1)
                    for f in range(2):
                        for k in range(KD):
                            if n == 0 and f == 0:
                                pe.wait_ge(s["h_ready"], k + 1)
                            last = mm(banks[n % 2][:, f * T:(f + 1) * T], win[q][:, k, f * P:(f + 1) * P], hT[:, k, :], k == 0, k == KD - 1)
                            if group is not None and k % 4 == 1:
                                bu_tile(group, 2 * f + k // 4)
                    last.then_inc(s["proj_done"], 1)

                def s5_out(g):
                    pe.wait_ge(s["phase_on"], g + 1)
                    pe.wait_ge(s["bu_copied"], min(4 * g + 8, 16))
                    for j in range(4):
                        a = slice(32 * j, 32 * j + 32)
                        for m, src in enumerate((sT1[g % 2], sT2[g % 2])):
                            last = mm(banks[2 + g % 2][a, 0:T], cc[:, m, (4 * g + j) * 32:(4 * g + j + 1) * 32], src[:, j, :], m == 0, m == 1)
                    last.then_inc(s["s5_out_done"], 1)

                project(0)
                project(1)
                pe.wait_ge(s["lora_in"], 32)
                for m, (src, a, b, out) in enumerate(((xw, 0, 64, banks[4][0:CH, 0:T]), (xa, 64, 128, banks[4][CH:P, 0:T]),
                                                      (xg, 128, 256, banks[7][:, 0:T]))):
                    pe.wait_ge(s["mixed"], m + 1) if m < 2 else pe.wait_ge(s["mixed_g"], 1)
                    for k in range(KD):
                        last = mm(out, lora1[:, k, a:b], src[:, k, :], k == 0, k == KD - 1)
                        if m == 2 and k % 2:
                            bu_tile(0, k // 2)
                    last.then_inc(s["lora1_done"], 1)
                    if m == 1:
                        pe.wait_ge(s["bb_ready"], 1)
                        for m in range(2):
                            for J in range(4):
                                last = nc.tensor.transpose(banks[5 + m][:, J * P:(J + 1) * P], bb[:, m, J * P:(J + 1) * P], ident)
                        last.then_inc(s["bb_turned"], 1)
                for m in range(3):
                    pe.wait_ge(s["lora_hidden_ready"], 1 if m < 2 else 2)
                    for i in range(FT):
                        if m and i % 2 == 0:
                            pe.wait_ge(s["lora2_copied"], 2 * m - 2 + i // 2 + 1)
                        out = banks[5 + i // 2][:, (i % 2) * T:(i % 2 + 1) * T]
                        if m == 0:
                            last = mm(out, lora2[0:CH, i * P:(i + 1) * P], lora_hidden[0:CH, 0:T], True, True)
                        elif m == 1:
                            last = mm(out, lora2[CH:P, i * P:(i + 1) * P], lora_hidden[CH:P, 0:T], True, True)
                        else:
                            last = mm(out, lora2[:, W + i * P:W + (i + 1) * P], lora_hidden[:, T:2 * T], True, True)
                        if i % 2:
                            last.then_inc(s["lora2_done"], 1)
                project(2, 1)
                project(3)
                project(4)
                pe.wait_ge(s["kk_squared"], 1)
                pe.wait_ge(s["lora2_copied"], 6)
                for b in range(2):
                    last = mm(banks[4 + b][:, :], head_ones, kksq[:, 2 * b:2 * b + 2, :], True, True)
                last.then_inc(s["kk_summed"], 1)
                project(5)
                project(6)
                s5_out(0)
                project(7, 2)

                def fm(arr, u):
                    return arr[:, u % FT, (u // FT) * CH:(u // FT + 1) * CH]

                for m, (l, r, needs) in enumerate(((bh, at, 1), (at, bh, 1), (kh, at, 2), (bh, rt, 3), (kh, rt, 3))):
                    pe.wait_ge(s["scaled"], needs)
                    for b in range(2):
                        if m == 2:
                            pe.wait_ge(s["proj_copied"], 8)
                        if m >= 3:
                            pe.wait_ge(s["scores_copied"], 2 * m - 6 + b + 1)
                        bank = banks[SCORE_BANK[m] + b]
                        for u in range(8 * b, 8 * b + 8):
                            last = pair(bank[:, (u % 8) * CH:(u % 8 + 1) * CH], fm(l, u), fm(r, u))
                        last.then_inc(s["scores_done"], 1)
                    if m == 1:
                        s5_out(1)
                    if m == 2:
                        for j in range(4):
                            bu_tile(3, j)
                pe.wait_ge(s["rk_ready"], 1)
                pe.wait_ge(s["scores_copied"], 6)
                for b in range(2):
                    last = mm(banks[b][:, :], head_ones, rk[:, 2 * b:2 * b + 2, :], True, True)
                last.then_inc(s["rk_summed"], 1)
                for lev in range(LEVELS):
                    for b in range(2):
                        if lev == 0:
                            pe.wait_ge(s["scores_copied"], 10)
                        else:
                            pe.wait_ge(s["xy_ready"], 2 * lev - 2 + b + 1)
                        pe.wait_ge(s["mo_ready"], 2 * lev + b + 1)
                        for u in range(8 * b, 8 * b + 8):
                            last = pair(banks[4 + b][:, (u % 8) * CH:(u % 8 + 1) * CH], MO[:, u, :], X[:, u, :])
                        last.then_inc(s["w_done"], 1)
                    for b in range(2):
                        pe.wait_ge(s["w_copied"], 2 * lev + b + 1)
                        if lev:
                            pe.wait_ge(s["y_turned"], 2 * lev - 2 + b + 1)
                        for u in range(8 * b, 8 * b + 8):
                            last = pair(banks[6 + b][:, (u % 8) * CH:(u % 8 + 1) * CH], Y[:, u, :], Wk[:, u, :])
                        last.then_inc(s["xy_done"], 1)
                    if lev in (2, 3):
                        s5_out(lev)
                pe.wait_ge(s["xy_ready"], 2 * LEVELS)
                pe.wait_ge(s["turned"], 3)
                pe.wait_ge(s["bonus_ready"], 1)
                pe.wait_ge(s["s5_gelu"], 1)
                pe.wait_ge(s["glu_in"], 32)

                def glu(f):
                    for k in range(FT):
                        last = mm(banks[2 + f // 2][:, (f % 2) * T:(f % 2 + 1) * T], wglu[:, k, f * P:(f + 1) * P], ys5[:, k, :], k == 0, k == FT - 1)
                    if f % 2:
                        last.then_inc(s["glu_done"], 1)

                def mean(t):
                    pe.wait_ge(s["y_copied"], 2 * t + 2)
                    if t:
                        pe.wait_ge(s["centred"], 1)
                    mm(banks[6][:, :], head_ones, yT[:, :, t * P:(t + 1) * P], True, True).then_inc(s["mean_done"], 1)

                def variance(t):
                    pe.wait_ge(s["y_squared"], t + 1)
                    if t:
                        pe.wait_ge(s["var_root"], 1)
                    mm(banks[7][:, :], head_ones, ysq[:, :, t * P:(t + 1) * P], True, True).then_inc(s["var_done"], 1)

                def project_out(t, halves, ks, first, last_part):
                    for hf in halves:
                        for n, k in enumerate(ks):
                            src = mix_s5[:, k, t * P:(t + 1) * P] if k < FT else mix_rw[:, k - FT, t * P:(t + 1) * P]
                            last = mm(banks[OUT_BANK[2 * t + hf]][:, :], src, wout[k // 2][:, k % 2, hf * 512:(hf + 1) * 512],
                                      first and n == 0, last_part and n == len(ks) - 1)
                        if last_part:
                            last.then_inc(s["out_done"], 1)

                tiles = [slice(i * CH, (i + 1) * CH) for i in range(FT)]
                for c in range(NCH):
                    if c:
                        pe.wait_ge(s["u0_ready"], c)
                    for i, o in enumerate(tiles):
                        pair(banks[0][:, o], KA[:, c * FT + i, :], Vs[:, c * FT + i, :], i == 0, False)
                    if c:
                        pe.wait_ge(s["y_copied"], c)
                    for i, o in enumerate(tiles):
                        pair(banks[5][:, o], Vs[:, c * FT + i, :], RK[:, c * FT + i, :], i == 0, False)
                    if c:
                        pe.wait_ge(s["state_ready"], c)
                    for i, o in enumerate(tiles):
                        last = pair(banks[0][:, o], fm(at, c * FT + i), state[:, o], False, True)
                    last.then_inc(s["u0_done"], 1)
                    if c < 2:
                        glu(2 * c)
                    for i, o in enumerate(tiles):
                        pair(banks[5][:, o], state[:, o], fm(rt, c * FT + i), False, False)
                    pe.wait_ge(s["u0_ready"], c + 1)
                    for i, o in enumerate(tiles):
                        last = pair(banks[1][:, o], X[:, c * FT + i, :], u0[:, o])
                    last.then_inc(s["u_done"], 1)
                    if c < NCH - 1:
                        for i, o in enumerate(tiles):
                            pair(banks[4][:, o], Ks[:, c * FT + i, :], Vs[:, c * FT + i, :], i == 0, False)
                    if c < 2:
                        glu(2 * c + 1)
                    else:
                        if c == 2:
                            pe.wait_ge(wout_in, 64)
                            pe.wait_ge(s["glu_sig"], 2)
                            pe.wait_ge(s["mix_s5_ready"], 2)
                        project_out(0, (c - 2,), range(FT), True, False)
                    if c == NCH - 1:
                        variance(0)
                    pe.wait_ge(s["u_ready"], c + 1)
                    if c < NCH - 1:
                        for i, o in enumerate(tiles):
                            last = pair(banks[4][:, o], Bs[:, c * FT + i, :], uu[:, o], False, True)
                        last.then_inc(s["state_done"], 1)
                    for i, o in enumerate(tiles):
                        last = pair(banks[5][:, o], uu[:, o], RB[:, c * FT + i, :], False, True)
                    last.then_inc(s["y_done"], 1)
                    if c == NCH - 2:
                        mean(0)
                mean(1)
                variance(1)
                project_out(1, (0, 1), range(FT), True, False)
                for t in range(TT):
                    pe.wait_ge(s["mix_rw_ready"], t + 1)
                    project_out(t, (0,), range(FT, KD), False, True)
                    if t:
                        pe.wait_ge(s["x2_ready"], 2)
                        for half in range(2):
                            turn_x2(0, half).then_inc(s["x2_turned"], 1)
                    project_out(t, (1,), range(FT, KD), False, True)
                pe.wait_ge(s["x2T_ready"], 1)
                for k in range(KD):
                    mm(logits[0], x2T[:, k, 0:P], router[:, k, :], k == 0, k == KD - 1)

        experts(nc, io, ctx, arena, con, par, banks, ring, chunk_in, chunk_src, p_in, pT, wproj, router, x2T, logits, turn_x2, ssq, x2)


def experts(nc, io, ctx, arena, con, par, banks, ring, chunk_in, chunk_src, p_in, pT, wproj, router, x2T, logits, turn_x2, ssq, x2):
    def sb(name, shape, dt=F32):
        return ctx.enter_context(nc.sbuf_tensor(name, shape, dt))

    def un(i, n=1):
        return arena[:, i * UNIT:(i + n) * UNIT]

    def prm(name):
        a, n = PARAMS[name]
        return par[:, a:a + n]

    ident = con[:, C_ID:C_ID + P]
    ones = con[:, C_ONES:C_ONES + P]
    tri = con[:, C_TRI:C_TRI + P]
    HF = D // 2

    xn = un(33, 2).rearrange("p (t d) -> p t d", d=D)
    xres = un(35, 2).rearrange("p (t d) -> p t d", d=D)
    parts = un(24, 3).bitcast(BF16).rearrange("p (t q d) -> p t q d", t=TT, q=3)
    bias = un(37, 3).rearrange("p (m d) -> p m d", m=3)
    y = un(40)[:, 0:HF]
    xg = un(40)[:, HF:2 * HF].rearrange("p (k s) -> p k s", k=KD)
    gt = un(41)[:, 0:HF]
    up = un(41)[:, HF:2 * HF]
    sg = un(42)[:, 0:HF]
    actT = un(42)[:, HF:2 * HF].rearrange("p (h k s) -> p k h s", h=2, k=4)
    gT = un(43)[:, 0:TT * P].rearrange("p (t m) -> p t m", t=TT)
    pg = un(43)[:, 256:512].rearrange("p (t m) -> p t m", t=TT)
    onehot = un(43)[:, 512:576].bitcast(BF16).rearrange("p (t m) -> p t m", t=TT)
    pick = un(43)[:, 576:640]
    rbias = un(43)[:, 896:896 + E]
    lg = un(44)[:, 0:64].rearrange("p (t e) -> p t e", t=TT)
    gates = un(44)[:, 64:128].rearrange("p (t e) -> p t e", t=TT)
    mask = un(44)[:, 128:192].rearrange("p (t e) -> p t e", t=TT)
    rank = un(44)[:, 192:256].rearrange("p (t e) -> p t e", t=TT)
    top = un(44)[:, 256:272].rearrange("p (t e) -> p t e", t=TT)
    topi = un(44)[:, 272:288].bitcast(U32).rearrange("p (t e) -> p t e", t=TT)
    topf = un(44)[:, 288:304].rearrange("p (t e) -> p t e", t=TT)
    ex = un(44)[:, 304:320].rearrange("p (t e) -> p t e", t=TT)
    st = un(44)[:, 320:352]
    hot = un(44)[:, 512:512 + TT * TOPK * E].rearrange("p (t j e) -> p t j e", t=TT, j=TOPK)
    hotg = un(44)[:, 768:768 + TT * TOPK * E].rearrange("p (t j e) -> p t j e", t=TT, j=TOPK)
    cnt = un(44)[:, 384:416]
    cflag = un(44)[:, 416:424]
    nexp = un(44)[:, 424:425].bitcast(I32)

    def sem(name):
        return ctx.enter_context(nc.semaphore(name))

    s = {n: sem("m_" + n) for n in (
        "router_in", "bias_in", "root", "parted", "rest_ready", "scaled", "ple_done", "ple_copied", "turned", "h_ready", "logits_done", "top_ready", "exp_ready",
        "mask_ready", "rank_done", "count_ready", "dve", "swish_ready", "tail", "up_read",
        "ranks_moved", "hot_ready", "gathered", "xg_ready", "gate_done", "up_done", "down_done", "chunks_used",
        "gt_ready", "sig_ready", "act_ready", "pg_ready", "gT_done", "gT_ready", "actT_done", "actT_ready",
        "y_ready", "scattered", "picked")}

    def mm(out, lhsT, rhs, start, stop):
        return nc.tensor.matmul(out, lhsT, rhs, start=start, stop=stop, skip_group_check=True)

    def chain(eng, name):
        n = [0]

        def link(ins):
            n[0] += 1
            ins.then_inc(s[name], 1)
            eng.wait_ge(s[name], n[0])
        return link

    ple = un(27, 2).rearrange("p (n d) -> p n d", d=HF)
    EARLY = 3

    def ple_proj(n, bank):
        t, hf = n // 2, n % 2
        for k in range(2):
            last = mm(bank[:, :], pT[:, k, t * P:(t + 1) * P], wproj[:, k, hf * HF:(hf + 1) * HF], k == 0, k == 1)
        return last

    with nc.Block() as block:
        @block.sync
        def _(sp):
            sp.dma_start(rbias[:, :], io["router_b"].to_broadcast([P, E])).then_inc(s["router_in"], 16)
            for m, b in enumerate(("exp_b_gate", "exp_b_up", "exp_b_down")):
                sp.dma_start(bias[0:E, m, :], io[b]).then_inc(s["bias_in"], 16)
            for c in range(4, 8):
                sp.dma_start(ring[c][:, :, :], chunk_src(c, 0)).then_inc(chunk_in[c], 16)

        @block.scalar
        def _(act):
            nc.scalar.activation(st[:, 0:2], ssq[:, 0:2], ACT.Sqrt, bias=par[:, NPARAM:NPARAM + 1], scale=1.0 / D).then_inc(s["root"], 1)
            for k in range(KD):
                act.wait_ge(s["turned"], k // 4 + 1)
                last = nc.scalar.activation(x2T[:, k, P:T], banks[4 + k // 4][:, (k % 4) * P:(k % 4 + 1) * P], ACT.Copy, scale=prm("g_moe")[:, k:k + 1])
            last.then_inc(s["h_ready"], 1)
            act.wait_ge(s["scaled"], 1)
            nc.scalar.activation(parts[:, 1, 0, :], xn[:, 1, :], ACT.Copy).then_inc(s["parted"], 1)
            act.wait_ge(s["rest_ready"], 1)
            nc.scalar.activation(parts[:, 1, 1, :], xres[:, 1, :], ACT.Copy).then_inc(s["parted"], 1)
            act.wait_ge(s["top_ready"], 1)
            for t in range(TT):
                last = nc.scalar.activation(ex[:, t, 0:4], top[:, t, 0:4], ACT.Exp, bias=st[:, 2 + t:3 + t], accum_out=st[:, 4 + t:5 + t])
            last.then_inc(s["exp_ready"], 1)
            act.wait_ge(s["rest_ready"], 2)
            nc.scalar.activation(parts[:, 1, 2, :], xres[:, 1, :], ACT.Copy)
            for n in range(EARLY):
                act.wait_ge(s["ple_done"], n + 1)
                nc.scalar.activation(ple[:, n, :], banks[(5, 7)[n % 2]][:, :], ACT.Copy).then_inc(s["ple_copied"], 1)
        @block.vector
        def _(dve):
            link = chain(dve, "dve")
            V = nc.vector
            tt, ts, stt = V.tensor_tensor, V.tensor_scalar, V.scalar_tensor_tensor
            V.memset(gT[:, :, :], 0.0).then_inc(s["gT_ready"], 1)
            V.memset(y, 0.0).then_inc(s["y_ready"], 1)
            for i, name in enumerate(("actT_ready", "gT_done")):
                V.memset(st[:, 8 + i:9 + i], 0.0).then_inc(s[name], 1)
            dve.wait_ge(s["root"], 1)
            link(V.reciprocal(st[:, 0:2], st[:, 0:2]))
            ts(xn[:, 1, :], x2[:, 1, :], st[:, 1:2], None, ALU.mult).then_inc(s["scaled"], 1)

            def part(t):
                link(ts(xn[:, t, :], x2[:, t, :], st[:, t:t + 1], None, ALU.mult))
                link(V.tensor_copy(parts[:, t, 0, :], xn[:, t, :]))
                link(tt(xres[:, t, :], xn[:, t, :], parts[:, t, 0, :], ALU.subtract))
                link(V.tensor_copy(parts[:, t, 1, :], xres[:, t, :]))
                link(tt(xres[:, t, :], xres[:, t, :], parts[:, t, 1, :], ALU.subtract))
                link(V.tensor_copy(parts[:, t, 2, :], xres[:, t, :]))

            part(0)
            dve.wait_ge(s["router_in"], 16)
            dve.wait_ge(s["logits_done"], 1)
            for t in range(TT):
                m = stt(lg[:, t, :], logits[t], st[:, t:t + 1], rbias[:, :], ALU.mult, ALU.add)
            link(m)
            for t in range(TT):
                m = V.max(top[:, t, :], lg[:, t, :])
            link(m)
            ts(st[:, 2:4], top[:, :, 0], -1.0, None, ALU.mult).then_inc(s["top_ready"], 1)
            for t in range(TT):
                m = V.max_index(topi[:, t, :], top[:, t, :], lg[:, t, :])
            link(m)
            link(V.tensor_copy(topf[:, :, :], topi[:, :, :]))
            every = [P, TT, TOPK, E]
            link(tt(hot[:, :, :, :], con[:, C_E32:C_E32 + E][:, None, None, :].to_broadcast(every),
                    topf[:, :, 0:TOPK][:, :, :, None].to_broadcast(every), ALU.is_equal))
            V.tensor_reduce(mask[:, :, :], hot.rearrange("p t j e -> p t e j"), AX.X, ALU.add).then_inc(s["mask_ready"], 1)
            dve.wait_ge(s["exp_ready"], 1)
            link(V.reciprocal(st[:, 6:8], st[:, 4:6]))
            for t in range(TT):
                m = ts(ex[:, t, 0:TOPK], ex[:, t, 0:TOPK], st[:, 6 + t:7 + t], None, ALU.mult)
            link(m)
            link(tt(hotg[:, :, :, :], hot[:, :, :, :], ex[:, :, 0:TOPK][:, :, :, None].to_broadcast(every), ALU.mult))
            link(V.tensor_reduce(gates[:, :, :], hotg.rearrange("p t j e -> p t e j"), AX.X, ALU.add))
            dve.wait_ge(s["mask_ready"], 1)
            link(ts(rank[:, :, :], mask[:, :, :], -1000.0, 1000.0, ALU.mult, ALU.add))
            dve.wait_ge(s["rank_done"], 1)
            tt(rank[:, :, :], rank[:, :, :], banks[4][:, 0:TT * E].rearrange("p (t e) -> p t e", t=TT), ALU.add)
            link(V.tensor_reduce(cnt[:, 0:1], banks[4][:, TT * E:TT * E + E], AX.X, ALU.max))
            link(tt(cflag[:, 1:MAX_PASS], cnt[:, 0:1].to_broadcast([P, MAX_PASS - 1]),
                    con[:, C_TIME + SLOTS:C_TIME + T:SLOTS], ALU.is_gt))
            link(V.tensor_reduce(cnt[:, 1:2], cflag[:, 1:MAX_PASS], AX.X, ALU.add))
            ts(nexp[:, 0:1], cnt[:, 1:2], float(E), float(E), ALU.mult, ALU.add).then_inc(s["count_ready"], 1)

        @block.gpsimd
        def _(pool):
            tt = nc.gpsimd.tensor_tensor
            pool.wait_ge(s["parted"], 1)
            tt(xres[:, 1, :], xn[:, 1, :], parts[:, 1, 0, :], ALU.subtract).then_inc(s["rest_ready"], 1)
            pool.wait_ge(s["parted"], 2)
            tt(xres[:, 1, :], xres[:, 1, :], parts[:, 1, 1, :], ALU.subtract).then_inc(s["rest_ready"], 1)

        @block.tensor
        def _(pe):
            for half in range(2):
                turn_x2(1, half).then_inc(s["turned"], 1)
            pe.wait_ge(s["y_ready"], 1)
            pe.wait_ge(s["gT_ready"], 1)
            for n in range(4):
                mm(banks[n][:, :], gT[:, 0, 0:P // 2].bitcast(BF16), y[:, 0:HF // 2].bitcast(BF16), True, False)
            pe.wait_ge(s["h_ready"], 1)
            for k in range(KD):
                last = mm(logits[1], x2T[:, k, P:T], router[:, k, :], k == 0, k == KD - 1)
            last.then_inc(s["logits_done"], 1)
            pe.wait_ge(p_in, 32)
            ple_proj(0, banks[5]).then_inc(s["ple_done"], 1)
            pe.wait_ge(s["mask_ready"], 1)
            mm(banks[4][:, 0:32], tri, mask[:, 0, :], True, True)
            mm(banks[4][:, 32:64], ones, mask[:, 0, :], True, False)
            mm(banks[4][:, 32:64], tri, mask[:, 1, :], False, True)
            mm(banks[4][:, 64:96], ones, mask[:, 0, :], True, False)
            mm(banks[4][:, 64:96], ones, mask[:, 1, :], False, True).then_inc(s["rank_done"], 1)
            ple_proj(1, banks[7]).then_inc(s["ple_done"], 1)
            pe.wait_ge(s["ple_copied"], 1)
            ple_proj(2, banks[5]).then_inc(s["ple_done"], 1)

    def scatter():
        for t in range(TT):
            for hf in range(2):
                a = slice(hf * 64, hf * 64 + 64)
                last = mm(banks[2 * t + hf][:, :], gT[a, t, :], y[a, :], False, True)
        return last

    GATE, UP, GAT, YB = banks[4], banks[5], banks[6], banks[7]

    def count(eng):
        return eng.value_load(nexp[0:1, 0:1], min_val=E, max_val=MAX_PASS * E)

    fin = un(33, 2).rearrange("p (t d) -> p t d", d=D)
    t2 = {n: sem("t_" + n) for n in (
        "fg_in", "scattered", "x3_ready", "squared", "root", "inverse", "ple_done", "turned", "h_ready",
        "gate_done", "sig_ready", "x4_ready", "squared2", "root2", "out_ready", "out")}
    fg = un(45)

    with nc.Block() as block:
        @block.sync
        def _(sp):
            n_all = count(sp)
            sp.dma_start(fg[:, :], io["final_g"].to_broadcast([P, D])).then_inc(t2["fg_in"], 16)
            with sp.Fori(1, n_all) as n:
                e = sp.snap(n % E)
                for c in range(NC):
                    sp.wait_ge(s["chunks_used"], (n - 1) * NC + c + 1)
                    sp.dma_start(ring[c][:, :, :], chunk_src(c, e)).then_inc(chunk_in[c], 16)
            wg = io["ple_w_gate"].rearrange("(c k p) n -> c p k n", p=P, k=2)
            sp.wait_ge(s["gate_done"], n_all)
            for c in range(4):
                sp.dma_start(ring[c][:, :, :], wg[c]).then_inc(chunk_in[c], 16)

        @block.scalar
        def _(act):
            n_all = count(act)
            with act.Fori(0, n_all) as n:
                act.wait_ge(s["gt_ready"], n + 1)
                nc.scalar.activation(sg, gt, ACT.Sigmoid, scale=1.702).then_inc(s["sig_ready"], 1)
                act.wait_ge(s["gT_done"], n + 2)
                act.wait_ge(s["scattered"], n + 1)
                nc.scalar.activation(gT[:, :, :], YB[:, 0:TT * P].rearrange("p (t m) -> p t m", t=TT), ACT.Copy).then_inc(s["gT_ready"], 1)
                act.wait_ge(s["actT_done"], n + 1)
                nc.scalar.activation(actT[:, :, :, :], GATE[:, :].rearrange("p (k h s) -> p k h s", h=2, k=4), ACT.Copy).then_inc(s["actT_ready"], 1)

        @block.vector
        def _(dve):
            V = nc.vector
            tt, ts, stt = V.tensor_tensor, V.tensor_scalar, V.scalar_tensor_tensor
            n_all = count(dve)
            iota = con[:, C_IOTA:C_IOTA + P]

            def one_hot(e):
                for t in range(TT):
                    ts(onehot[:, t, :], iota[:, 0:SLOTS], rank[:, t, bass.ds(e, 1)], None, ALU.is_equal).then_inc(s["hot_ready"], 1)

            def gathered_times_gain():
                tt(xg[:, :, :], GAT[:, :].rearrange("p (k s) -> p k s", k=KD),
                   prm("g_moe")[:, :, None].to_broadcast([P, KD, SLOTS]), ALU.mult).then_inc(s["xg_ready"], 1)

            one_hot(0)
            dve.wait_ge(s["gathered"], 1)
            gathered_times_gain()
            with dve.Fori(0, n_all) as n:
                e = dve.snap(n % E)
                e_next = dve.snap((n + 1) % E)
                dve.wait_ge(s["gT_done"], n + 1)
                for t in range(TT):
                    ts(pg[:, t, :], iota, rank[:, t, bass.ds(e, 1)], gates[:, t, bass.ds(e, 1)], ALU.is_equal, ALU.mult).then_inc(s["pg_ready"], 1)
                V.tensor_copy(pick[0:E, :], ident[0:E, bass.ds(e, 1)].to_broadcast([E, SLOTS])).then_inc(s["picked"], 1)
                dve.wait_ge(s["pg_ready"], 2 * n + 2)
                for t in range(TT):
                    ts(rank[:, t, bass.ds(e, 1)], rank[:, t, bass.ds(e, 1)], -float(SLOTS), None, ALU.add).then_inc(s["ranks_moved"], 1)
                dve.wait_ge(s["ranks_moved"], 2 * n + 2)
                one_hot(e_next)
                dve.wait_ge(s["gate_done"], n + 1)
                ts(gt, GATE[:, :], 7.0, None, ALU.min).then_inc(s["gt_ready"], 1)
                dve.wait_ge(s["gt_ready"], n + 1)
                dve.wait_ge(s["sig_ready"], n + 1)
                tt(sg, sg, gt, ALU.mult).then_inc(s["swish_ready"], 1)
                dve.wait_ge(s["up_done"], n + 1)
                ts(up, UP[:, :], 7.0, -7.0, ALU.min, ALU.max).then_inc(s["up_read"], 1)
                dve.wait_ge(s["up_read"], n + 1)
                dve.wait_ge(s["swish_ready"], n + 1)
                stt(up, up, 1.0, sg, ALU.add, ALU.mult).then_inc(s["act_ready"], 1)
                dve.wait_ge(s["gathered"], n + 2)
                gathered_times_gain()
                dve.wait_ge(s["down_done"], n + 1)
                dve.wait_ge(s["scattered"], n + 1)
                V.tensor_copy(y, YB[:, :]).then_inc(s["y_ready"], 1)

        @block.tensor
        def _(pe):
            n_all = count(pe)

            def gather():
                for k in range(KD):
                    for i in range(3 * TT):
                        last = mm(GAT[:, k * SLOTS:(k + 1) * SLOTS], parts[:, i // 3, i % 3, k * P:(k + 1) * P], onehot[:, i // 3, :], i == 0, i == 3 * TT - 1)
                last.then_inc(s["gathered"], 1)

            pe.wait_ge(s["bias_in"], 48)
            pe.wait_ge(s["hot_ready"], 2)
            gather()
            with pe.Fori(0, n_all) as n:
                pe.wait_ge(s["xg_ready"], n + 1)
                pe.wait_ge(s["actT_ready"], n + 1)
                for m, (bank, done) in enumerate(((GATE, "gate_done"), (UP, "up_done"))):
                    for k in range(KD):
                        c = 4 * m + k // 2
                        if k % 2 == 0:
                            pe.wait_ge(chunk_in[c], 16 * n + 16)
                        for hf in range(2):
                            last = mm(bank[hf * 64:hf * 64 + 64, :], xg[:, k, :], ring[c][:, k % 2, hf * HF:(hf + 1) * HF], k == 0, False)
                        if k % 2:
                            last.then_inc(s["chunks_used"], 1)
                    pe.wait_ge(s["picked"], n + 1)
                    for hf in range(2):
                        last = mm(bank[hf * 64:hf * 64 + 64, :], pick[0:E, :], bias[0:E, m, hf * HF:(hf + 1) * HF], False, True)
                    last.then_inc(s[done], 1)
                pe.wait_ge(s["gT_ready"], n + 1)
                pe.wait_ge(s["y_ready"], n + 1)
                scatter().then_inc(s["scattered"], 1)
                pe.wait_ge(s["pg_ready"], 2 * n + 2)
                for t in range(TT):
                    last = nc.tensor.transpose(YB[:, t * P:(t + 1) * P], pg[:, t, :], ident)
                last.then_inc(s["gT_done"], 1)
                pe.wait_ge(s["act_ready"], n + 1)
                for k in range(4):
                    last = nc.tensor.transpose(GATE[:, k * P:(k + 1) * P], up[:, k * P:(k + 1) * P], ident)
                last.then_inc(s["actT_done"], 1)
                pe.wait_ge(s["hot_ready"], 2 * n + 4)
                gather()
                pe.wait_ge(s["actT_ready"], n + 2)
                pe.wait_ge(s["gT_ready"], n + 2)
                for k in range(KD):
                    c = 8 + k // 2
                    if k % 2 == 0:
                        pe.wait_ge(chunk_in[c], 16 * n + 16)
                    for hf in range(2):
                        last = mm(YB[hf * 64:hf * 64 + 64, :], actT[:, k % 4, k // 4, :], ring[c][:, k % 2, hf * HF:(hf + 1) * HF], k == 0, False)
                    if k % 2:
                        last.then_inc(s["chunks_used"], 1)
                for hf in range(2):
                    last = mm(YB[hf * 64:hf * 64 + 64, :], pick[0:E, :], bias[0:E, 2, hf * HF:(hf + 1) * HF], False, True)
                last.then_inc(s["down_done"], 1)
    hT2 = un(24, 2).rearrange("p (t k c) -> p t k c", t=TT, k=KD)
    sig = un(35, 2).rearrange("p (t d) -> p t d", d=D)
    scr, scr2 = (un(a, 2).rearrange("p (t d) -> p t d", d=D) for a in (41, 31))
    st2 = un(44)[:, 0:32]
    sums, roots, inv = st2[:, 0:2], st2[:, 4:6], st2[:, 6:8]
    sums2, roots2, inv2 = st2[:, 8:12], st2[:, 12:14], st2[:, 14:16]
    with nc.Block() as block:
        @block.vector
        def _(dve):
            link = chain(dve, "tail")

            def finish(t):
                dve.wait_ge(t2["root2"], t + 1)
                V.reciprocal(inv2[:, t:t + 1], roots2[:, t:t + 1]).then_inc(t2["inverse"], 1)
                dve.wait_ge(t2["inverse"], t + 2)
                dve.wait_ge(t2["fg_in"], 16)
                for hf in range(2):
                    o = slice(hf * HF, (hf + 1) * HF)
                    stt(fin[:, t, o], fin[:, t, o], inv2[:, t:t + 1], fg[:, o], ALU.mult, ALU.mult).then_inc(t2["out_ready"], 1)

            V = nc.vector
            tt, ts, stt = V.tensor_tensor, V.tensor_scalar, V.scalar_tensor_tensor
            for t in range(TT):
                for hf in range(2):
                    dve.wait_ge(t2["scattered"], 2 * t + hf + 1)
                    o = slice(hf * HF, (hf + 1) * HF)
                    tt(fin[:, t, o], x2[:, t, o], banks[2 * t + hf][:, :], ALU.add).then_inc(t2["x3_ready"], 1)
            for n in range(4):
                t, kh = n // 2, n % 2
                dve.wait_ge(t2["turned"], n + 1)
                tt(hT2[:, t, 4 * kh:4 * kh + 4, :], banks[n].rearrange("p (k c) -> p k c", c=P),
                   prm("g_ple")[:, 4 * kh:4 * kh + 4][:, :, None].to_broadcast([P, 4, P]), ALU.mult).then_inc(t2["h_ready"], 1)
            dve.wait_ge(t2["root"], 1)
            V.reciprocal(inv, roots).then_inc(t2["inverse"], 1)
            for n in range(4):
                t, hf = n // 2, n % 2
                o = slice(hf * HF, (hf + 1) * HF)
                dve.wait_ge(t2["sig_ready"], n + 1)
                if n >= EARLY:
                    dve.wait_ge(t2["ple_done"], 1)
                link(tt(sig[:, t, o], sig[:, t, o], ple[:, n, :] if n < EARLY else banks[7][:, :], ALU.mult))
                tt(fin[:, t, o], fin[:, t, o], sig[:, t, o], ALU.add).then_inc(t2["x4_ready"], 1)
                if n == 2:
                    finish(0)
            finish(1)

        @block.scalar
        def _(act):
            A = nc.scalar.activation
            eps = par[:, NPARAM:NPARAM + 1]
            for t in range(TT):
                act.wait_ge(t2["x3_ready"], 2 * t + 2)
                A(scr[:, t, :], fin[:, t, :], ACT.Square, accum_out=sums[:, t:t + 1]).then_inc(t2["squared"], 1)
            act.wait_ge(t2["squared"], 2)
            A(roots, sums, ACT.Sqrt, bias=eps, scale=1.0 / D).then_inc(t2["root"], 1)
            for n in range(4):
                t, hf = n // 2, n % 2
                o = slice(hf * HF, (hf + 1) * HF)
                act.wait_ge(t2["gate_done"], n + 1)
                act.wait_ge(t2["inverse"], 1)
                A(sig[:, t, o], banks[n][:, :], ACT.Sigmoid, scale=inv[:, t:t + 1]).then_inc(t2["sig_ready"], 1)
                if hf:
                    A(st2[:, 16 + t:17 + t], par[:, NPARAM:NPARAM + 1], ACT.Sqrt)
                    for m in (n - 1, n):
                        act.wait_ge(t2["x4_ready"], m + 1)
                        A(scr2[:, t, (m % 2) * HF:(m % 2 + 1) * HF], fin[:, t, (m % 2) * HF:(m % 2 + 1) * HF], ACT.Square, accum_out=sums2[:, m:m + 1]).then_inc(t2["squared2"], 1)
                    act.wait_ge(t2["squared2"], 3 * t + 2)
                    A(sums2[:, 2 * t:2 * t + 1], sums2[:, 2 * t:2 * t + 1], ACT.Identity, bias=sums2[:, 2 * t + 1:2 * t + 2]).then_inc(t2["squared2"], 1)
                    act.wait_ge(t2["squared2"], 3 * t + 3)
                    A(roots2[:, t:t + 1], sums2[:, 2 * t:2 * t + 1], ACT.Sqrt, bias=eps, scale=1.0 / D).then_inc(t2["root2"], 1)

        @block.tensor
        def _(pe):
            for t in range(TT):
                for hf in range(2):
                    a = slice(hf * 64, hf * 64 + 64)
                    mm(banks[2 * t + hf][:, :], gT[a, t, :], y[a, :], False, True).then_inc(t2["scattered"], 1)
            n_all = count(pe)

            def gate(n, chunks):
                t, hf = n // 2, n % 2
                for c in chunks:
                    pe.wait_ge(chunk_in[c], 16 * n_all + 16)
                    for k in (2 * c, 2 * c + 1):
                        last = mm(banks[n][:, :], hT2[:, t, k, :], ring[c][:, k % 2, hf * HF:(hf + 1) * HF], k == 0, k == KD - 1)
                return last

            ple_proj(3, banks[7]).then_inc(t2["ple_done"], 1)
            for n in range(4):
                t, kh = n // 2, n % 2
                pe.wait_ge(t2["x3_ready"], 2 * t + 2)
                for k in range(4 * kh, 4 * kh + 4):
                    last = nc.tensor.transpose(banks[n][:, (k % 4) * P:(k % 4 + 1) * P], fin[:, t, k * P:(k + 1) * P], ident)
                last.then_inc(t2["turned"], 1)
            for n in range(4):
                pe.wait_ge(t2["h_ready"], 4 if n > 1 else 2)
                gate(n, (0, 1))
            for n in range(4):
                gate(n, (2, 3)).then_inc(t2["gate_done"], 1)

        @block.sync
        def _(sp):
            o = io["out"].rearrange("(t p) d -> p t d", p=P)
            for n in range(4):
                t, hf = n // 2, n % 2
                sp.wait_ge(t2["out_ready"], n + 1)
                sp.dma_start(o[:, t, hf * HF:(hf + 1) * HF], fin[:, t, hf * HF:(hf + 1) * HF]).then_inc(t2["out"], 16)
            sp.wait_ge(t2["out"], 16 * 4)


def columns(v):
    return np.ascontiguousarray(np.asarray(v).reshape(-1, P).T)


def lay_out(a):
    f = {k: np.asarray(v) for k, v in a.items()}
    o = {}
    x = f["x"].reshape(T, D)
    o["x"] = x
    o["xT"] = np.ascontiguousarray(x.T)
    o["pT"] = np.ascontiguousarray(f["p"].reshape(T, -1).T)
    o["consts"] = constants()
    dt = np.repeat(f["s5_log_dt"].reshape(NJ, 2), CH, axis=1)
    mw, mr = f["rwkv_mu_wag"][0], f["rwkv_mu_rkv"][0]
    cols = dict(g_mix=f["norm_mix_g"], mu_w=mw[0], mu_a=mw[1], mu_g=mw[2], mu_r=mr[0], mu_k=mr[1], mu_v=mr[2],
                w0=f["rwkv_w0"], a0=f["rwkv_a0"], k_k=f["rwkv_k_k"], k_a=f["rwkv_k_a"], r_k=f["rwkv_r_k"],
                ln_w=f["rwkv_ln_w"], ln_b=f["rwkv_ln_b"], s5_d=f["s5_d"], g_moe=f["norm_moe_g"],
                g_ple=f["norm_ple_g"], lam_re=f["s5_lam_re"], lam_im=f["s5_lam_im"], log_dt=dt)
    o["params"] = np.concatenate([columns(cols[n]) for n in PARAMS], axis=1)
    for n in ("re", "im"):
        b = f["s5_b_" + n].reshape(NJ, 2, CH, 16)
        bd = np.zeros((2, CH, NJ, 2, 16), np.float32)
        c = f["s5_c_" + n].reshape(NJ, 2, 16, CH)
        cd = np.zeros((2, CH, NJ, 2, 16), np.float32)
        for g in range(2):
            bd[g, :, :, g, :] = b[:, g].transpose(1, 0, 2)
            cd[g, :, :, g, :] = c[:, g].transpose(2, 0, 1)
        o["s5_b_" + n] = bd.reshape(P, NJ * 32)
        o["s5_c_" + n] = cd.reshape(P, NJ * 32)
    o["w_in"] = f["w_in"][0]
    o["lora1"] = np.concatenate([f["rwkv_w1"][0], f["rwkv_a1"][0], f["rwkv_g1"][0]], axis=1)
    o["lora2"] = np.concatenate([np.concatenate([f["rwkv_w2"][0], f["rwkv_a2"][0]], axis=0), f["rwkv_g2"][0]], axis=1)
    o["w_glu"] = f["s5_w_glu"][0]
    o["w_out"] = f["w_out"][0]
    o["router_w"] = f["router_w"][0]
    o["router_b"] = f["router_b"].reshape(1, E)
    for n in ("exp_w_gate", "exp_w_up", "exp_w_down", "exp_b_gate", "exp_b_up", "exp_b_down", "ple_w_proj", "ple_w_gate"):
        o[n] = f[n][0]
    o["final_g"] = f["final_norm_g"].reshape(1, D)
    return o


def kernel(**inputs):
    import concourse.bacc as bacc
    from concourse.bass_utils import run_bass_kernel_spmd

    nc = bacc.Bacc("TRN2", target_bir_lowering=False, num_devices=1)
    arrays, io = {}, {}
    for name, a in lay_out(inputs).items():
        a = np.ascontiguousarray(a)
        arrays["in_" + name] = a
        io[name] = nc.dram_tensor("in_" + name, a.shape, mybir.dt.from_np(a.dtype), kind="ExternalInput").ap()
    io["out"] = nc.dram_tensor("out_0", (T, D), F32, kind="ExternalOutput").ap()
    layer(nc, io)
    got = run_bass_kernel_spmd(nc, [arrays], core_ids=[0])
    return got.results[0]["out_0"].reshape(1, T, D)
```
